# Optimizing a Trainium2 kernel written in Bass

```python
import math
import jax, jax.numpy as jnp
from jax import lax
import numpy as np

D_MODEL = 1024
BATCH = 1
SEQ = 512
DEPTH = 1

MIX_WIDTH = D_MODEL
GLA_HEADS = 4
GLA_DV = MIX_WIDTH // 2 // GLA_HEADS
GLA_DK = GLA_DV // 2
GLA_GATE_RANK = 16
GLA_GATE_NORM = 16.0
GLA_CHUNK = 64
SWA_HEAD_DIM = 64
SWA_Q_HEADS = MIX_WIDTH // 2 // SWA_HEAD_DIM
SWA_KV_HEADS = 2
SWA_BLOCK = 128
SWA_WINDOW = 128
REL_BUCKETS = 32
REL_MAX_DIST = 128
D_FF = 4 * D_MODEL
NORM_EPS = 1e-6

COL_SIZES = (
    GLA_HEADS * GLA_DK,
    GLA_HEADS * GLA_DK,
    GLA_HEADS * GLA_DV,
    GLA_HEADS * GLA_DV,
    2 * GLA_GATE_RANK,
    SWA_Q_HEADS * SWA_HEAD_DIM,
    SWA_KV_HEADS * SWA_HEAD_DIM,
    SWA_KV_HEADS * SWA_HEAD_DIM,
)
IN_COLS = int(sum(COL_SIZES))
SPLITS = [int(s) for s in np.cumsum(COL_SIZES)[:-1]]


def rmsnorm(x, g):
    xf = x.astype(jnp.float32)
    r = lax.rsqrt(jnp.mean(xf * xf, axis=-1, keepdims=True) + NORM_EPS)
    return (xf * r).astype(x.dtype) * g

def t5_buckets(rel):
    nb = REL_BUCKETS // 2
    ret = (rel > 0).astype(np.int32) * nb
    n = np.abs(rel)
    max_exact = nb // 2
    large = max_exact + (np.log(np.maximum(n, 1).astype(np.float32) / max_exact)
                         / math.log(REL_MAX_DIST / max_exact) * (nb - max_exact)).astype(np.int32)
    large = np.minimum(large, nb - 1)
    return ret + np.where(n < max_exact, n, large)

def gla_chunked(q, k, v, log_a):
    B, H, L, dk = q.shape
    dv = v.shape[-1]
    C = GLA_CHUNK
    N = L // C
    q = q.reshape(B, H, N, C, dk)
    k = k.reshape(B, H, N, C, dk)
    v = v.reshape(B, H, N, C, dv)
    b = jnp.cumsum(log_a.reshape(B, H, N, C, dk), axis=3)
    b_last = b[:, :, :, -1:, :]
    q_dec = q * jnp.exp(b)
    k_intra = k * jnp.exp(-b)
    k_state = k * jnp.exp(b_last - b)
    causal = jnp.asarray(np.tril(np.ones((C, C), dtype=bool)))
    A = jnp.where(causal, jnp.einsum('bhncd,bhnsd->bhncs', q_dec, k_intra), 0.0)
    o_intra = jnp.einsum('bhncs,bhnse->bhnce', A, v)
    dS = jnp.einsum('bhncd,bhnce->bhnde', k_state, v)
    decay = jnp.exp(b_last[:, :, :, 0, :])

    def step(S, inp):
        d, ds = inp
        return d[..., None] * S + ds, S

    S0 = jnp.zeros((B, H, dk, dv), jnp.float32)
    _, S_enter = lax.scan(step, S0, (jnp.moveaxis(decay, 2, 0), jnp.moveaxis(dS, 2, 0)))
    S_enter = jnp.moveaxis(S_enter, 0, 2)
    o_inter = jnp.einsum('bhncd,bhnde->bhnce', q_dec, S_enter)
    return (o_intra + o_inter).reshape(B, H, L, dv)

def banded_window_gqa(q, k, v, sink, rel_table):
    B, Hq, L, dh = q.shape
    Hkv = k.shape[1]
    G = Hq // Hkv
    W = SWA_BLOCK
    N = L // W
    qb = q.reshape(B, Hkv, G, N, W, dh)

    def band(t):
        tp = jnp.pad(t, ((0, 0), (0, 0), (W, W), (0, 0))).reshape(B, Hkv, N + 2, W, dh)
        return jnp.concatenate([tp[:, :, :N], tp[:, :, 1:N + 1], tp[:, :, 2:N + 2]], axis=3)

    kb, vb = band(k), band(v)
    c = np.arange(W)[:, None]
    s = np.arange(3 * W)[None, :]
    rel = s - W - c
    key_pos = (np.arange(N)[:, None, None] - 1) * W + s[None]
    mask = jnp.asarray((np.abs(rel)[None] <= SWA_WINDOW) & (key_pos >= 0) & (key_pos < L))
    bias = rel_table.astype(jnp.float32)[jnp.asarray(t5_buckets(rel))]
    bias = jnp.transpose(bias, (2, 0, 1)).reshape(Hkv, G, 1, W, 3 * W)

    logits = jnp.einsum('bkgncd,bknsd->bkgncs', qb, kb).astype(jnp.float32) * (dh ** -0.5) + bias
    logits = jnp.where(mask, logits, -1e30)
    sink_l = sink.astype(jnp.float32).reshape(Hkv, G, 1, 1, 1)
    m = jnp.maximum(jnp.max(logits, axis=-1, keepdims=True), sink_l)
    p = jnp.exp(logits - m)
    denom = jnp.sum(p, axis=-1, keepdims=True) + jnp.exp(sink_l - m)
    o = jnp.einsum('bkgncs,bknsd->bkgncd', (p / denom).astype(v.dtype), vb)
    return o.reshape(B, Hq, L, dh)

def hybrid_mixer(u, w_in, w_gu_f, b_g_f, w_gu_b, b_g_b, gla_norm, sink, rel_table, w_out):
    B, L, _ = u.shape
    proj = u @ w_in
    qa, ka, va, ga, za, qs, ks, vs = jnp.split(proj, SPLITS, axis=-1)

    def heads(t, h):
        return t.reshape(B, L, h, -1).transpose(0, 2, 1, 3)

    f32 = jnp.float32
    qh = heads(qa, GLA_HEADS).astype(f32) * (GLA_DK ** -0.5)
    kh = heads(ka, GLA_HEADS).astype(f32)
    vh = heads(va, GLA_HEADS).astype(f32)
    zf, zb = za[..., :GLA_GATE_RANK], za[..., GLA_GATE_RANK:]
    la_f = heads(jax.nn.log_sigmoid((zf @ w_gu_f + b_g_f).astype(f32)) / GLA_GATE_NORM, GLA_HEADS)
    la_b = heads(jax.nn.log_sigmoid((zb @ w_gu_b + b_g_b).astype(f32)) / GLA_GATE_NORM, GLA_HEADS)
    o_f = gla_chunked(qh, kh, vh, la_f)
    flip = lambda t: jnp.flip(t, axis=2)
    o_b = flip(gla_chunked(flip(qh), flip(kh), flip(vh), flip(la_b)))
    o_a = o_f + o_b
    o_a = o_a * lax.rsqrt(jnp.mean(o_a * o_a, axis=-1, keepdims=True) + NORM_EPS)
    o_a = o_a.transpose(0, 2, 1, 3) * gla_norm.astype(f32)
    o_a = (o_a.reshape(B, L, GLA_HEADS * GLA_DV) * jax.nn.silu(ga.astype(f32))).astype(u.dtype)

    o_s = banded_window_gqa(heads(qs, SWA_Q_HEADS), heads(ks, SWA_KV_HEADS), heads(vs, SWA_KV_HEADS),
                            sink, rel_table)
    o_s = o_s.transpose(0, 2, 1, 3).reshape(B, L, SWA_Q_HEADS * SWA_HEAD_DIM)

    return jnp.concatenate([o_a, o_s], axis=-1) @ w_out

def first_inputs(seed: int = 0) -> dict:
    key = jax.random.key(seed)
    ks = jax.random.split(key, 20)
    nrm = lambda k, shape, scale: jax.random.normal(k, shape, jnp.float32) * scale
    gain = lambda k, shape: 1.0 + nrm(k, shape, 0.02)
    gla_w = GLA_HEADS * GLA_DK
    return {
        "x": nrm(ks[0], (BATCH, SEQ, D_MODEL), 1.0),
        "norm_mix_pre": gain(ks[1], (DEPTH, D_MODEL)),
        "w_in": nrm(ks[2], (DEPTH, D_MODEL, IN_COLS), D_MODEL ** -0.5),
        "w_gate_up_fwd": nrm(ks[3], (DEPTH, GLA_GATE_RANK, gla_w), GLA_GATE_RANK ** -0.5),
        "b_gate_fwd": nrm(ks[4], (DEPTH, gla_w), 0.1),
        "w_gate_up_bwd": nrm(ks[5], (DEPTH, GLA_GATE_RANK, gla_w), GLA_GATE_RANK ** -0.5),
        "b_gate_bwd": nrm(ks[6], (DEPTH, gla_w), 0.1),
        "gla_norm": gain(ks[7], (DEPTH, GLA_DV)),
        "swa_sink": nrm(ks[8], (DEPTH, SWA_Q_HEADS), 0.5),
        "rel_bias": nrm(ks[9], (REL_BUCKETS, SWA_Q_HEADS), 0.5),
        "w_out": nrm(ks[10], (DEPTH, MIX_WIDTH, D_MODEL), MIX_WIDTH ** -0.5),
        "norm_mix_post": gain(ks[11], (DEPTH, D_MODEL)),
        "norm_mlp_pre": gain(ks[12], (DEPTH, D_MODEL)),
        "w_up": nrm(ks[13], (DEPTH, D_MODEL, D_FF), D_MODEL ** -0.5),
        "w_down": nrm(ks[14], (DEPTH, D_FF, D_MODEL), D_FF ** -0.5),
        "norm_mlp_post": gain(ks[15], (DEPTH, D_MODEL)),
    }

def first_block(x, norm_mix_pre, w_in, w_gate_up_fwd, b_gate_fwd, w_gate_up_bwd, b_gate_bwd,
              gla_norm, swa_sink, rel_bias, w_out, norm_mix_post, norm_mlp_pre, w_up, w_down,
              norm_mlp_post):
    h = x
    for l in range(DEPTH):
        u = rmsnorm(h, norm_mix_pre[l])
        mix = hybrid_mixer(u, w_in[l], w_gate_up_fwd[l], b_gate_fwd[l], w_gate_up_bwd[l], b_gate_bwd[l],
                           gla_norm[l], swa_sink[l], rel_bias, w_out[l])
        h = h + rmsnorm(mix, norm_mix_post[l])
        z = rmsnorm(h, norm_mlp_pre[l]) @ w_up[l]
        ff = jnp.square(jax.nn.relu(z)) @ w_down[l]
        h = h + rmsnorm(ff, norm_mlp_post[l])
    return h


DEPTH_2 = 2

HEAD_DIM = 64
Q_HEADS = 8
KV_HEADS = 2
GROUP = Q_HEADS // KV_HEADS
ATTN_WIDTH = Q_HEADS * HEAD_DIM
KV_WIDTH = KV_HEADS * HEAD_DIM
WINDOW = 128
BLOCK = 128
POOL_WIDTH = D_MODEL - ATTN_WIDTH
POOL_WINDOWS = (2, 4, 8, 16)
POOL_GROUPS = len(POOL_WINDOWS)
POOL_GC = POOL_WIDTH // POOL_GROUPS
EVEN_IN = ATTN_WIDTH + 2 * KV_WIDTH + ATTN_WIDTH + POOL_WIDTH + POOL_WIDTH
EVEN_MIX = ATTN_WIDTH + POOL_WIDTH
CONV_WIDTH = D_MODEL
CONV_K = 31
ODD_IN = 3 * CONV_WIDTH
EPS = 1e-6
NEG = -1e30
N_EVEN = (DEPTH_2 + 1) // 2
N_ODD = DEPTH_2 // 2


def rms_norm(x, g):
    xf = x.astype(jnp.float32)
    y = xf * lax.rsqrt(jnp.mean(xf * xf, axis=-1, keepdims=True) + EPS)
    return (y * g.astype(jnp.float32)).astype(x.dtype)

def alibi_slopes(n):
    return jnp.exp2(-8.0 * jnp.arange(1, n + 1, dtype=jnp.float32) / n)

def sliding_window_attention(q, k, v, sinks):
    B, S, _ = q.shape
    nb = S // BLOCK
    q = q.reshape(B, nb, BLOCK, KV_HEADS, GROUP, HEAD_DIM)
    k = k.reshape(B, nb, BLOCK, KV_HEADS, HEAD_DIM)
    v = v.reshape(B, nb, BLOCK, KV_HEADS, HEAD_DIM)
    kpad = jnp.zeros_like(k[:, :1])
    vpad = jnp.zeros_like(v[:, :1])
    kk = jnp.concatenate([jnp.concatenate([kpad, k[:, :-1]], axis=1), k], axis=2)
    vv = jnp.concatenate([jnp.concatenate([vpad, v[:, :-1]], axis=1), v], axis=2)
    scores = jnp.einsum('bnqkgd,bnskd->bnkgqs', q, kk).astype(jnp.float32) * (HEAD_DIM ** -0.5)
    qi = jnp.arange(BLOCK)[:, None] + BLOCK
    sj = jnp.arange(2 * BLOCK)[None, :]
    dist = qi - sj
    key_pos = jnp.arange(nb)[:, None, None] * BLOCK + sj[None] - BLOCK
    valid = (dist >= 0)[None] & (dist < WINDOW)[None] & (key_pos >= 0)
    slopes = alibi_slopes(Q_HEADS).reshape(KV_HEADS, GROUP)
    bias = -slopes[:, :, None, None] * dist.astype(jnp.float32)
    scores = jnp.where(valid[None, :, None, None], scores + bias, NEG)
    sink = sinks.astype(jnp.float32).reshape(KV_HEADS, GROUP)[None, None, :, :, None, None]
    mx = jnp.maximum(jnp.max(scores, axis=-1, keepdims=True), sink)
    p = jnp.exp(scores - mx)
    p = p / (jnp.sum(p, axis=-1, keepdims=True) + jnp.exp(sink - mx))
    out = jnp.einsum('bnkgqs,bnskd->bnqkgd', p.astype(vv.dtype), vv)
    return out.reshape(B, S, ATTN_WIDTH)

def multiscale_pool(u, pool_w, pool_scale):
    B, S, _ = u.shape
    uf = u.astype(jnp.float32).reshape(B, S, POOL_GROUPS, POOL_GC)
    cs = jnp.concatenate([jnp.zeros_like(uf[:, :1]), jnp.cumsum(uf, axis=1)], axis=1)
    t = jnp.arange(S)[:, None]
    win = jnp.array(POOL_WINDOWS, dtype=jnp.int32)[None, :]
    lo = jnp.maximum(t + 1 - win, 0)
    cnt = (t + 1 - lo).astype(jnp.float32)
    lower = cs[:, lo, jnp.arange(POOL_GROUPS)[None, :]]
    pooled = (cs[:, 1:] - lower) / cnt[None, :, :, None] - uf
    y = jnp.einsum('bsgc,gcd->bsgd', pooled, pool_w.astype(jnp.float32))
    y = y * pool_scale.astype(jnp.float32).reshape(POOL_GROUPS, POOL_GC)
    return y.reshape(B, S, POOL_WIDTH).astype(u.dtype)

def even_mixer(h, w_in, sinks, pool_w, pool_scale, w_out):
    proj = h @ w_in
    splits = np.cumsum([ATTN_WIDTH, KV_WIDTH, KV_WIDTH, ATTN_WIDTH, POOL_WIDTH]).tolist()
    q, k, v, ga, u, gb = jnp.split(proj, splits, axis=-1)
    ya = sliding_window_attention(q, k, v, sinks).astype(h.dtype) * jax.nn.silu(ga)
    yb = multiscale_pool(u, pool_w, pool_scale) * jax.nn.silu(gb)
    return jnp.concatenate([ya, yb], axis=-1) @ w_out

def odd_mixer(h, w_in, dw_w, dw_b, ln_g, ln_b, w_out):
    proj = h @ w_in
    a, b, gate = jnp.split(proj, [CONV_WIDTH, 2 * CONV_WIDTH], axis=-1)
    glu = a * jax.nn.sigmoid(b)
    conv = lax.conv_general_dilated(
        glu, dw_w.astype(glu.dtype), window_strides=(1,), padding=[(CONV_K - 1, 0)],
        dimension_numbers=('NWC', 'WIO', 'NWC'), feature_group_count=CONV_WIDTH)
    cf = conv.astype(jnp.float32) + dw_b.astype(jnp.float32)
    mu = jnp.mean(cf, axis=-1, keepdims=True)
    var = jnp.mean(jnp.square(cf - mu), axis=-1, keepdims=True)
    cn = (cf - mu) * lax.rsqrt(var + EPS) * ln_g.astype(jnp.float32) + ln_b.astype(jnp.float32)
    y = jax.nn.silu(cn).astype(h.dtype) * jax.nn.silu(gate)
    return y @ w_out

def second_inputs(seed: int = 0) -> dict:
    key = jax.random.key(seed)
    ks = jax.random.split(key, 16)
    f32 = jnp.float32
    nrm = lambda k, shape, s: jax.random.normal(k, shape, f32) * s
    return {
        'x': nrm(ks[0], (BATCH, SEQ, D_MODEL), 1.0),
        'pre_norm': 1.0 + nrm(ks[1], (DEPTH_2, D_MODEL), 0.05),
        'post_norm': 1.0 + nrm(ks[2], (DEPTH_2, D_MODEL), 0.05),
        'a_w_in': nrm(ks[3], (N_EVEN, D_MODEL, EVEN_IN), D_MODEL ** -0.5),
        'a_sinks': nrm(ks[4], (N_EVEN, Q_HEADS), 0.5),
        'b_pool_w': nrm(ks[5], (N_EVEN, POOL_GROUPS, POOL_GC, POOL_GC), POOL_GC ** -0.5),
        'b_pool_scale': 1.0 + nrm(ks[6], (N_EVEN, POOL_WIDTH), 0.1),
        'ab_w_out': nrm(ks[7], (N_EVEN, EVEN_MIX, D_MODEL), EVEN_MIX ** -0.5),
        'c_w_in': nrm(ks[8], (N_ODD, D_MODEL, ODD_IN), D_MODEL ** -0.5),
        'c_dw_w': nrm(ks[9], (N_ODD, CONV_K, 1, CONV_WIDTH), CONV_K ** -0.5),
        'c_dw_b': nrm(ks[10], (N_ODD, CONV_WIDTH), 0.02),
        'c_ln_g': 1.0 + nrm(ks[11], (N_ODD, CONV_WIDTH), 0.05),
        'c_ln_b': nrm(ks[12], (N_ODD, CONV_WIDTH), 0.02),
        'c_w_out': nrm(ks[13], (N_ODD, CONV_WIDTH, D_MODEL), CONV_WIDTH ** -0.5),
    }

def second_block(x, pre_norm, post_norm, a_w_in, a_sinks, b_pool_w, b_pool_scale, ab_w_out,
              c_w_in, c_dw_w, c_dw_b, c_ln_g, c_ln_b, c_w_out):
    for layer in range(DEPTH_2):
        h = rms_norm(x, pre_norm[layer])
        if layer % 2 == 0:
            i = layer // 2
            y = even_mixer(h, a_w_in[i], a_sinks[i], b_pool_w[i], b_pool_scale[i], ab_w_out[i])
        else:
            i = layer // 2
            y = odd_mixer(h, c_w_in[i], c_dw_w[i], c_dw_b[i], c_ln_g[i], c_ln_b[i], c_w_out[i])
        x = x + rms_norm(y, post_norm[layer])
    return x


def setup_inputs(seed=0):
    out = dict(first_inputs(seed))
    for name, value in second_inputs(seed + 1).items():
        if name != "x":
            out[name + "_2"] = value
    return out


def reference(
    x, norm_mix_pre, w_in, w_gate_up_fwd, b_gate_fwd, w_gate_up_bwd, b_gate_bwd, gla_norm,
    swa_sink, rel_bias, w_out, norm_mix_post, norm_mlp_pre, w_up, w_down, norm_mlp_post,
    pre_norm_2, post_norm_2, a_w_in_2, a_sinks_2, b_pool_w_2, b_pool_scale_2, ab_w_out_2,
    c_w_in_2, c_dw_w_2, c_dw_b_2, c_ln_g_2, c_ln_b_2, c_w_out_2,
):
    x = first_block(
        x, norm_mix_pre, w_in, w_gate_up_fwd, b_gate_fwd, w_gate_up_bwd, b_gate_bwd, gla_norm,
        swa_sink, rel_bias, w_out, norm_mix_post, norm_mlp_pre, w_up, w_down, norm_mlp_post,
    )
    return second_block(
        x, pre_norm_2, post_norm_2, a_w_in_2, a_sinks_2, b_pool_w_2, b_pool_scale_2, ab_w_out_2,
        c_w_in_2, c_dw_w_2, c_dw_b_2, c_ln_g_2, c_ln_b_2, c_w_out_2,
    )


_drawn_inputs = setup_inputs


def setup_inputs(seed=0):
    import zlib

    import numpy as np

    out = dict(_drawn_inputs(seed))
    spreads = {}
    factors = {'gla_norm': 2.888,
     'swa_sink': 64.0,
     'norm_mix_post': 2.937,
     'norm_mlp_pre': 10.244,
     'norm_mlp_post': 13.203,
     'a_sinks_2': 24.874,
     'c_dw_b_2': 15.511,
     'c_ln_b_2': 48.02,
     'pre_norm_2': 2.671,
     'post_norm_2': 11.351,
     'b_pool_scale_2': 3.141,
     'c_ln_g_2': 18.327}
    for name, (base, spread) in spreads.items():
        noise = np.random.default_rng([zlib.crc32(name.encode()), seed]).standard_normal(out[name].shape)
        drawn = base * np.exp(spread * noise) if base else spread * noise
        out[name] = __import__('jax').numpy.asarray(drawn.astype(out[name].dtype))
    for name, factor in factors.items():
        out[name] = (out[name] * factor).astype(out[name].dtype)
    return out
```

```python
import numpy as np
import concourse.bass as bass
from concourse import mybir
from contextlib import ExitStack

F32 = mybir.dt.float32
F32R = mybir.dt.float32r
I32 = mybir.dt.int32
ALU = mybir.AluOpType
ACT = mybir.ActivationFunctionType
AX = mybir.AxisListType

P = 128
TOK = 512
NBLK = TOK // P
D = 1024
KT = D // P
CW = 256
FF = 4096
HID = FF // P // 2
EPS = 1e-6

QA, KA, VA, GA, ZA, QS, KS, WIN_COLS = 0, 256, 512, 1024, 1536, 1568, 2080, 2336
AQ, AKV, AGA, AU, AGB, AIN_COLS = 0, 512, 768, 1280, 1792, 2304
GATE_RANK = 16
GLA_C = 64
NCH = TOK // GLA_C
GATE_NORM = 16.0
QSCALE = 0.125
BAND1 = 3 * P
BAND2 = 2 * P
LGW = BAND1 + 1
POOLW = (2, 4, 8, 16)
UPAD = 16
TAPS = 31
CPAD = TAPS - 1
DVE_TAPS = 19
ACT_TAPS = TAPS - DVE_TAPS

V_PRE1, V_POST1, V_PREM, V_POSTM, V_PRE2A, V_POST2A, V_PRE2B, V_POST2B = [8 * i for i in range(8)]
V_DWB, V_LNG, V_LNB = 64, 72, 80
V_PSC, V_GN, V_BF, V_BB, V_N = 88, 92, 93, 95, 97

C_WIN, C_WOUT, C_UP0, C_DN0, C_UP1, C_DN1 = 0, 10, 14, 22, 30, 38
C_AIN, C_ABOUT, C_CAB, C_CGATE, C_COUT, C_END = 46, 55, 59, 67, 71, 75
E_WOUT, E_UP0, E_DN0, E_UP1, E_DN1 = 19, 27, 43, 51, 67
E_AIN, E_ABOUT, E_CAB, E_CGATE, E_COUT = 75, 93, 101, 117, 125

SLACK = {}


def t5_bucket_onehot():
    rel = np.arange(-255, 256)
    nb, max_exact = 16, 8
    n = np.abs(rel)
    large = max_exact + (np.log(np.maximum(n, 1).astype(np.float32) / max_exact)
                         / np.log(128 / max_exact) * (nb - max_exact)).astype(np.int32)
    bucket = (rel > 0) * nb + np.where(n < max_exact, n, np.minimum(large, nb - 1))
    hot = np.zeros((33, 512), np.float32)
    seen = n <= 128
    hot[bucket[seen], np.arange(511)[seen]] = 1.0
    hot[32, :511] = ~seen
    return hot


def shape_constants():
    i = np.arange(P)
    same = (i[:, None] // GLA_C) == (i[None, :] // GLA_C)
    fwd = same & (i[:, None] <= i[None, :])
    bwd = same & (i[:, None] >= i[None, :])
    restart = np.broadcast_to((np.arange(TOK) % GLA_C != 0), (P, TOK))
    t = np.arange(16)
    cnt = np.concatenate([w / np.minimum(t + 1, w) for w in POOLW])
    return np.concatenate([np.eye(P), np.ones((P, P)), fwd, bwd, restart,
                           np.broadcast_to(cnt, (P, 64)), np.eye(P)[::-1]], axis=1).astype(np.float32)


def alibi_band():
    slopes = np.exp2(-8.0 * np.arange(1, 9, dtype=np.float32) / 8).astype(np.float32)
    dist = (np.arange(P)[:, None] + P - np.arange(BAND2)[None, :]).astype(np.float32)
    bias = -slopes[None, :, None] * dist[:, None, :]
    return np.where(((dist >= 0) & (dist < 128))[:, None, :], bias, np.float32(-1e30)).astype(np.float32)


MIX1_LOADS, MIX2_LOADS, VEC_LOADS = 5, 4, 15


class Chain:

    def __init__(self, eng, sem):
        self.eng, self.sem, self.n, self.reg, self.per = eng, sem, 0, None, 0

    def link(self, ins):
        self.n += 1
        ins.then_inc(self.sem, 1)
        self.eng.wait_ge(self.sem, self.n if self.reg is None else self.reg * self.per + self.n)

    def enter(self, reg, per):
        self.reg, self.per, self.start = reg, per, self.n

    def leave(self, trips):
        assert self.n - self.start == self.per, (self.n - self.start, self.per)
        self.n, self.reg = self.start + trips * self.per, None


def block_kernel(nc, a, out):
    ctx = ExitStack()
    with ctx:
        top = [(nc.sbuf_base + 31) // 32 * 32]

        def at(name, shape, offset, dt=F32):
            return nc.alloc_sbuf_tensor_at(name, shape, dt, offset=offset)

        def sb(name, shape, dt=F32):
            size = 4 * int(np.prod(shape[1:]))
            t = at(name, shape, top[0], dt)
            top[0] += (size + 31) // 32 * 32
            return t

        def sem(name):
            return ctx.enter_context(nc.semaphore(name))

        raw = sb("raw", [P, 2, KT, CW])
        w_hi = sb("w_hi", [P, 2, KT, CW], F32R)
        w_lo = sb("w_lo", [P, 2, KT, CW], F32R)
        resid = sb("resid", [P, KT, TOK])
        act_hi = sb("act_hi", [P, KT, TOK], F32R)
        act_lo = sb("act_lo", [P, KT, TOK], F32R)
        R = sb("R", [P, TOK])
        sq = sb("sq", [P, 2, TOK])
        sq_sum = sb("sq_sum", [P, TOK])
        ident_ones = sb("ident_ones", [P, 2 * P])
        ident, ones = ident_ones[:, 0:P], ident_ones[:, P:2 * P]
        vec = sb("vec", [P, V_N])
        eps = sb("eps", [P, 1])
        arena = top[0]

        def arena_alloc(start):
            at_ = [start]

            def take(name, shape, dt=F32):
                t = at(name, shape, at_[0], dt)
                at_[0] += (4 * int(np.prod(shape[1:])) + 31) // 32 * 32
                SLACK[name] = nc.sbuf_usable_end - at_[0]
                return t
            take.pos = at_
            return take

        m1 = arena_alloc(arena)
        o1 = m1("o1", [P, KT, TOK])
        qa = m1("qa", [P, 2, TOK])
        ka = m1("ka", [P, 2, TOK])
        va_tok = m1("va_tok", [P, NBLK, 512])
        ga = m1("ga", [P, 4, TOK])
        masks = m1("masks", [P, 2, P])
        restart = m1("restart", [P, TOK])
        zz = m1("zz", [32, TOK])
        gate_w = m1("gate_w", [32, 2, 256])
        decay = m1("decay", [P, 2, 2, NCH])
        late = m1.pos[0]
        sA = arena_alloc(late)
        bias1 = sA("bias1", [P, 8, BAND1])
        qs1 = sA("qs1", [P, 4, TOK])
        k1 = sA("k1", [P, TOK])
        k1x = sA("k1x", [P, TOK])
        v1 = sA("v1", [P, TOK])
        v1_tok = sA("v1_tok", [P, NBLK, P])
        lg1 = sA("lg1", [P, 3, 2, LGW])
        pT1 = sA("pT1", [P, 2, 3 * 2 * P])
        sm1 = sA("sm1", [P, 3, 2, 4])
        sink1 = sA("sink1", [P, 8])
        vaf = sA("vaf", [P, 2, TOK])
        gA = arena_alloc(late)
        qdec = gA("qdec", [P, 2, 2, TOK])
        kint = gA("kint", [P, 2, 2, TOK])
        kst = gA("kst", [P, 2, 2, NBLK, P])
        S = gA("S", [P, 2, NCH, P])
        Am = gA("Am", [P, 2, TOK])
        gx = gA("gx", [P, TOK])
        gl = gA("gl", [P, TOK])
        bb = gA("bb", [P, TOK])
        eb = gA("eb", [P, TOK])
        hankel = at("hankel", [P, 8, BAND1], arena + 4 * (KT + 4) * TOK)
        flip = at("flip", [P, P], arena + 4 * (KT + 4) * TOK + 4 * 8 * BAND1)
        x_tok = at("x_tok", [P, NBLK, D], arena)
        relw = at("relw", [33, 8], arena + 4 * NBLK * D)
        hot = at("hot", [33, 512], arena + 4 * NBLK * D + 32)
        relF = at("relF", [8, 512], arena + 4 * NBLK * D + 32 + 2048)
        vec_rows = at("vec_rows", [V_N, P], arena + 4 * NBLK * D + 32 + 4096)
        mA = arena_alloc(arena)
        y = mA("y", [P, KT, TOK])
        hid_hi = mA("hid_hi", [P, HID, TOK], F32R)
        hid_lo = mA("hid_lo", [P, HID, TOK], F32R)
        zt = mA("zt", [P, 2, TOK])
        ty = mA("ty", [P, 2, TOK])
        zq = sq
        eA = arena_alloc(arena + 4 * KT * TOK)
        o2 = eA("o2", [P, KT, TOK])
        q2 = eA("q2", [P, 4, TOK])
        k2 = eA("k2", [P, TOK])
        k2x = eA("k2x", [P, TOK])
        v2 = eA("v2", [P, TOK])
        v2_tok = eA("v2_tok", [P, NBLK, P])
        bias2 = eA("bias2", [P, 8, BAND2])
        lg2 = eA("lg2", [P, 3, 2, BAND2 + 1])
        pT2 = eA("pT2", [P, 2, 2 * 2 * P])
        sm2 = eA("sm2", [P, 3, 2, 4])
        sink2 = eA("sink2", [P, 8])
        ga2 = eA("ga2", [P, 4, TOK])
        gb2 = at("gb2", [P, 4, TOK], arena + 4 * 2 * KT * TOK)
        uu = eA("uu", [P, 4, UPAD + TOK])
        pw = eA("pw", [P, 4, P])
        wsum = eA("wsum", [P, 2, UPAD + TOK])
        pooled = eA("pooled", [P, 4, TOK])
        ty_e = at("ty_e", [P, 2, TOK], eA.pos[0])
        wcnt = at("wcnt", [P, 4, 16], eA.pos[0] + 4096)
        cA = arena_alloc(arena + 4 * KT * TOK)
        conv = cA("conv", [P, KT, TOK])
        gate = cA("gate", [P, KT, TOK])
        glu = cA("glu", [P, 2, CPAD + TOK])
        ab = cA("ab", [P, 2, TOK])
        taps = cA("taps", [P, KT, TAPS])
        tapw = cA("tapw", [P, 2, TAPS + 1])
        prod = cA("prod", [P, 2, TOK])
        pacc = cA("pacc", [P, TOK])
        vacc = cA("vacc", [P, TOK])
        csum = cA("csum", [P, TOK])
        mu = cA("mu", [P, TOK])
        yc = cA("yc", [P, 2, TOK])
        ty_c = cA("ty_c", [P, 2, TOK])
        tap_rows = at("tap_rows", [TAPS, D], cA.pos[0])
        o_tok = at("o_tok", [P, 2, 512], arena + 4 * KT * TOK)

        acc = ctx.enter_context(nc.psum_tensor("acc", [P, 4, 512], F32))
        psT = ctx.enter_context(nc.psum_tensor("psT", [P, 2, 512], F32))
        ps6 = ctx.enter_context(nc.psum_tensor("ps6", [P, 512], F32))
        ps7 = ctx.enter_context(nc.psum_tensor("ps7", [P, 512], F32))
        psTf = psT[:, :, :].rearrange("p a b -> p (a b)")

        relF_dram = nc.dram_tensor("relF_dram", [8, 512], F32, kind="Internal").ap()

        raw_ready = [sem("raw_ready0"), sem("raw_ready1")]
        hi_done = sem("hi_done")
        lo_done = sem("lo_done")
        tile_done = [sem("tile_done0"), sem("tile_done1")]
        evac_done = sem("evac_done")
        x_in = sem("x_in")
        vec_in = sem("vec_in")
        vec_ps = sem("vec_ps")
        vec_done = sem("vec_done")
        taps_ps = sem("taps_ps")
        taps_done = sem("taps_done")
        const_in = sem("const_in")
        rel_in = sem("rel_in")
        gatew_set = sem("gatew_set")
        relf_ps = sem("relf_ps")
        relf_sb = sem("relf_sb")
        relf_out = sem("relf_out")
        bias1_in = sem("bias1_in")
        bias1_ps = sem("bias1_ps")
        bias1_done = sem("bias1_done")
        mix1_in = sem("mix1_in")
        xT_done = sem("xT_done")
        resid_done = sem("resid_done")
        act_hi_done = sem("act_hi_done")
        act_lo_done = sem("act_lo_done")
        sq_done = sem("sq_done")
        sqsum_done = sem("sqsum_done")
        rsum_done = sem("rsum_done")
        r_done = sem("r_done")
        ty_done = sem("ty_done")
        eps_set = sem("eps_set")
        dve_step = sem("dve_step")
        act_step = sem("act_step")
        pool_step = sem("pool_step")
        kx_done = sem("kx_done")
        vT_done = sem("vT_done")
        vtok_done = sem("vtok_done")
        sink_set = sem("sink_set")
        qk_done = sem("qk_done")
        logits_done = sem("logits_done")
        negmax_done = sem("negmax_done")
        exp_done = sem("exp_done")
        rden_done = sem("rden_done")
        p_done = sem("p_done")
        pT_done = sem("pT_done")
        pTs_done = sem("pTs_done")
        pv_done = sem("pv_done")
        o_done = sem("o_done")
        vaT_done = sem("vaT_done")
        vatok_done = sem("vatok_done")
        gate_ps = sem("gate_ps")
        gx_done = sem("gx_done")
        ln_done = sem("ln_done")
        ls_done = sem("ls_done")
        bb_done = sem("bb_done")
        eb_done = sem("eb_done")
        enb_done = sem("enb_done")
        qdec_done = sem("qdec_done")
        kint_done = sem("kint_done")
        dk_done = sem("dk_done")
        ek_done = sem("ek_done")
        ks_done = sem("ks_done")
        kT_done = sem("kT_done")
        kst_done = sem("kst_done")
        decay_done = sem("decay_done")
        dS_done = sem("dS_done")
        S_done = sem("S_done")
        A_done = sem("A_done")
        Am_set = sem("Am_set")
        Am_done = sem("Am_done")
        og_done = sem("og_done")
        og_out = sem("og_out")
        ogsq_done = sem("ogsq_done")
        ogsum_done = sem("ogsum_done")
        rr_done = sem("rr_done")
        on_done = sem("on_done")
        silu_done = sem("silu_done")
        og_gated = sem("og_gated")
        zt_done = sem("zt_done")
        zq_done = sem("zq_done")
        hhi_done = sem("hhi_done")
        hlo_done = sem("hlo_done")
        mix2_in = sem("mix2_in")
        upad_set = sem("upad_set")
        pooled_done = sem("pooled_done")
        wsum_done = sem("wsum_done")
        yb_ps = sem("yb_ps")
        o2_done = sem("o2_done")
        ob_done = sem("ob_done")
        silu2_done = sem("silu2_done")
        taps_in = sem("taps_in")
        sig_done = sem("sig_done")
        glu_done = sem("glu_done")
        tapw_done = sem("tapw_done")
        prod_done = sem("prod_done")
        pacc_step = sem("pacc_step")
        pacc_done = sem("pacc_done")
        conv_step = sem("conv_step")
        musum_done = sem("musum_done")
        mu_done = sem("mu_done")
        cen_done = sem("cen_done")
        cn_done = sem("cn_done")
        csilu_done = sem("csilu_done")
        gsilu_done = sem("gsilu_done")
        yc_done = sem("yc_done")
        fT_done = sem("fT_done")
        fo_done = sem("fo_done")
        out_done = [sem("out_done0"), sem("out_done1")]

        block = ctx.enter_context(nc.Block())

        def attention_steps(k, n=16):
            found = []
            for what, lag in (("pv", 3), ("qk", 0), ("softmax", 0), ("normalise", 1), ("transpose", 2)):
                if 0 <= k - lag < n:
                    found.append((what, k - lag))
            return found

        def mixer1_steps():
            steps = []
            for c in (0, 1, 2):
                steps += [("split", c + 1), ("tile", c, 0), ("tile", c, 1)]
            steps += [("keys_values", 0), ("split", 4), ("tile", 3, 1)]
            k = 0
            for c in (4, 5, 6, 7):
                for j in (0, 1):
                    steps += attention_steps(k) + attention_steps(k + 1)
                    k += 2
                    if j == 0:
                        steps.append(("split", c + 1))
                    steps.append(("tile", c, j))
                    if c >= 6:
                        steps.append(("gla_values", 2 * (c - 6) + j))
            for k in (16, 17, 18):
                steps += attention_steps(k)
            steps.append(("gla_begin", 0))
            for i in range(4):
                if i % 2 == 0:
                    steps.append(("split", 9 + i // 2))
                steps += [("gla_gate", i), ("tile", 8 + i // 2, i % 2)]
            for t in range(2):
                steps += [("gla_dS", t)]
                for h in (2 * t, 2 * t + 1):
                    steps += [("gla_A", h), ("gla_out", h)]
            steps.append(("gla_gating", 0))
            return steps

        def mixer2_steps():
            steps = []
            for c in (46, 47, 48):
                steps += [("split", c + 1), ("tile", c, 0), ("tile", c, 1)]
            steps += [("keys_values", 1)]
            k = 0
            for c in (49, 50, 51, 52):
                for j in (0, 1):
                    if j == 0:
                        steps.append(("split", c + 1))
                    steps += attention_steps(k) + attention_steps(k + 1)
                    k += 2
                    steps.append(("tile", c, j))
                    if c >= 51:
                        steps.append(("pool_window", 2 * (c - 51) + j))
            for k in (16, 17, 18):
                steps += attention_steps(k)
            steps += [("split", 54), ("attention_gate", 0), ("tile", 53, 0), ("tile", 53, 1)]
            steps += [("split", 55), ("tile", 54, 0), ("tile", 54, 1), ("pool_out", 0)]
            return steps

        def window(layer, n):
            kbs = [b for b in (range(n - 1, n + 2) if layer == 0 else range(n - 1, n + 1)) if 0 <= b < NBLK]
            return kbs, (kbs[0] - (n - 1)) * P

        LG, PT, SM, SINK, BIAS = (lg1, lg2), (pT1, pT2), (sm1, sm2), (sink1, sink2), (bias1, bias2)
        QH, KH, KX, VT, VTOK, OO = (qs1, q2), (k1, k2), (k1x, k2x), (v1, v2), (v1_tok, v2_tok), (o1, o2)

        def o_tile(layer, hp):
            return (4 if layer == 0 else 0) + hp

        def mixer_tile(c, j):
            if c < C_WOUT:
                e = 2 * c + j if c < 3 else (6 if c == 3 else 2 * c - 1 + j)
                return e, j if c != 3 else 0
            return E_AIN + 2 * (c - C_AIN) + j, j

        @block.sync
        def _(sp):
            for b in range(NBLK):
                sp.dma_start(x_tok[:, b, :], a["x"][0, b * P:(b + 1) * P, :]).then_inc(x_in, 16)

            def wait_slot(c):
                if isinstance(c, int) and c < 2:
                    return
                sp.wait_ge(lo_done, c - 1)

            def load(slot, w, n0, rows0=0, width=CW):
                rows = w[rows0:rows0 + D, :].rearrange("(k p) n -> p k n", p=P)
                for kk in (slice(0, KT // 2), slice(KT // 2, KT)):
                    sp.dma_start(raw[:, slot, kk, 0:width], rows[:, kk, bass.ds(n0, width)])\
                      .then_inc(raw_ready[slot], 16)

            def load_plain(w, c0, n, n0=0):
                with sp.Fori(0, n // 2) as i:
                    for s in range(2):
                        wait_slot(i * 2 + (c0 + s))
                        load((c0 + s) % 2, w, i * (2 * CW) + (n0 + s * CW))

            w_in, w_out, w_up, w_down = a["w_in"][0], a["w_out"][0], a["w_up"][0], a["w_down"][0]
            for c, n0 in enumerate((QS, QS + CW, KS, ZA, QA, KA, VA, VA + CW, GA, GA + CW)):
                wait_slot(c)
                load(c % 2, w_in, n0, 0, P if n0 == ZA else CW)
            load_plain(w_out, C_WOUT, 4)
            for half in range(2):
                cu, cd = (C_UP0, C_DN0) if half == 0 else (C_UP1, C_DN1)
                load_plain(w_up, cu, 8, half * FF // 2)
                with sp.Fori(0, 4) as i:
                    for s in range(2):
                        wait_slot(i * 2 + (cd + s))
                        load(s, w_down, i * CW, half * FF // 2 + s * D)
            for i in range(9):
                wait_slot(C_AIN + i)
                load((C_AIN + i) % 2, a["a_w_in_2"][0], i * CW)
            load_plain(a["ab_w_out_2"][0], C_ABOUT, 4)
            c_w_in = a["c_w_in_2"][0]
            ab_cols = c_w_in.rearrange("(k p) n -> p k n", p=P)
            with sp.Fori(0, 4) as i:
                for s in range(2):
                    slot = (C_CAB + s) % 2
                    wait_slot(i * 2 + (C_CAB + s))
                    for g in range(2):
                        sp.dma_start(raw[:, slot, :, g * P:(g + 1) * P],
                                     ab_cols[:, :, bass.ds(i * (2 * P) + (g * D + s * P), P)])\
                          .then_inc(raw_ready[slot], 16)
            load_plain(c_w_in, C_CGATE, 4, 2 * D)
            load_plain(a["c_w_out_2"][0], C_COUT, 4)
            for f in range(2 * NBLK):
                sp.wait_ge(fo_done, f + 1)
                sp.dma_start(out[0, (f // 2) * P:(f // 2 + 1) * P, (f % 2) * 512:(f % 2 + 1) * 512],
                             o_tok[:, f % 2, :]).then_inc(out_done[f % 2], 16)
            for s in range(2):
                sp.wait_ge(out_done[s], 16 * NBLK)

        @block.tensor
        def _(pe):
            def mm3(dst, hi, lo, x_hi, x_lo, first, last):
                pe.matmul(dst, hi, x_hi, start=first, stop=False)
                pe.matmul(dst, hi, x_lo, start=False, stop=False)
                return pe.matmul(dst, lo, x_hi, start=False, stop=last)

            def w_tiles(slot, k, j):
                return w_hi[:, slot, k, j * P:(j + 1) * P], w_lo[:, slot, k, j * P:(j + 1) * P]

            def project(dst, slot, j):
                for k in range(KT):
                    last = mm3(dst, *w_tiles(slot, k, j), act_hi[:, k, :], act_lo[:, k, :], k == 0, k == KT - 1)
                last.then_inc(tile_done[j], 1)

            def project_pair(c, e, n, order=range(KT)):
                pe.wait_ge(evac_done, e)
                pe.wait_ge(lo_done, c + 2)
                for i, k in enumerate(order):
                    pe.wait_ge(act_lo_done, 8 * n + i + 1)
                    for s in range(2):
                        for j in range(2):
                            last = mm3(acc[:, 2 * s + j, :], *w_tiles((c + s) % 2, k, j),
                                       act_hi[:, k, :], act_lo[:, k, :], i == 0, i == KT - 1)
                            if i == KT - 1:
                                last.then_inc(tile_done[j], 1)

            def project_chunks(c, e, order=range(KT)):
                for s in range(2):
                    pe.wait_ge(lo_done, c + (s + 1))
                    for j in range(2):
                        pe.wait_ge(evac_done, e + (2 * s + j - 3))
                        for i, k in enumerate(order):
                            last = mm3(acc[:, 2 * s + j, :], *w_tiles((c_par + s) % 2, k, j),
                                       act_hi[:, k, :], act_lo[:, k, :], i == 0, i == KT - 1)
                        last.then_inc(tile_done[j], 1)

            pe.wait_ge(const_in, 16)
            pe.wait_ge(vec_in, 16 * VEC_LOADS)
            pe.transpose(ps7[:, 0:V_N], vec_rows[:, :], ident[0:V_N, 0:V_N]).then_inc(vec_ps, 1)
            for k in range(KT):
                if k == 0:
                    pe.wait_ge(x_in, 16 * NBLK)
                if k >= 4:
                    pe.wait_ge(resid_done, k - 3)
                for b in range(NBLK):
                    last = pe.transpose(acc[:, k % 4, b * P:(b + 1) * P], x_tok[:, b, k * P:(k + 1) * P], ident[:, :])
                last.then_inc(xT_done, 1)
            pe.wait_ge(rel_in, 2 * 16)
            pe.wait_ge(gatew_set, 1)
            pe.matmul(ps6[0:8, :], relw[:, :], hot[:, :], start=True, stop=True).then_inc(relf_ps, 1)

            def token_sums(n):
                pe.wait_ge(sqsum_done, 8 * (n + 1))
                pe.matmul(ps7[:, :], ones[:, :], sq_sum[:, :], start=True, stop=True).then_inc(rsum_done, 1)

            last_in_bank = {}

            def mixer_tile_pe(c, j):
                e, bank = mixer_tile(c, j)
                if j == 0 or c == 3:
                    pe.wait_ge(lo_done, c + 1)
                if c == C_AIN and j == 0:
                    last_in_bank.clear()
                if bank in last_in_bank:
                    pe.wait_ge(evac_done, last_in_bank[bank] + 1)
                elif c == C_AIN:
                    pe.wait_ge(evac_done, E_AIN)
                elif c == 0:
                    pe.wait_ge(resid_done, KT)
                last_in_bank[bank] = e
                n = 0 if c < C_WOUT else 3
                for k in range(KT):
                    if c in (0, C_AIN) and j == 0:
                        pe.wait_ge(act_lo_done, 8 * n + k + 1)
                    if c == 3:
                        wh, wl = w_hi[:, 1, k, 0:P], w_lo[:, 1, k, 0:P]
                    else:
                        wh, wl = w_tiles(c % 2, k, j)
                    last = mm3(acc[:, bank, :], wh, wl, act_hi[:, k, :], act_lo[:, k, :], k == 0, k == KT - 1)
                    if c == 3 and k == KT - 2:
                        last.then_inc(tile_done[0], 1)
                last.then_inc(tile_done[j], 1)
                if c == 0 and j == 0:
                    token_sums(0)
                if c == C_AIN and j == 0:
                    token_sums(4)

            def gla_keys(i):
                d, t = i % 2, i // 2
                pe.wait_ge(ks_done, i + 1)
                pe.wait_ge(kst_done, i) if i else None
                for b in range(NBLK):
                    last = pe.transpose(ps6[:, b * P:(b + 1) * P], bb[:, b * P:(b + 1) * P], ident[:, :])
                last.then_inc(kT_done, 1)

            def gla_sum(h):
                pe.wait_ge(ogsq_done, h + 1)
                if h >= 1:
                    pe.wait_ge(rr_done, h)
                pe.matmul(ps7[:, :], ones[:, :], sq[:, h % 2, :], start=True, stop=True).then_inc(ogsum_done, 1)

            def mixer_step_pe(layer, step):
                what, i = step[0], step[1]
                if what == "tile":
                    mixer_tile_pe(step[1], step[2])
                elif what == "keys_values":
                    if layer == 0:
                        pe.wait_ge(bias1_in, 2 * 16)
                        for h in range(8):
                            if h >= 2:
                                pe.wait_ge(bias1_done, h - 1)
                            pe.matmul(psT[:, h % 2, 0:BAND1], flip[:, :], hankel[:, h, :], start=True, stop=True)\
                              .then_inc(bias1_ps, 1)
                    pe.wait_ge(evac_done, 6 if layer == 0 else E_AIN + 6)
                    pe.wait_ge(r_done, 1 if layer == 0 else 5)
                    for b in range(NBLK):
                        last = pe.transpose(ps7[:, b * P:(b + 1) * P], VT[layer][:, b * P:(b + 1) * P], ident[:, :])
                    last.then_inc(vT_done, 1)
                elif what == "qk":
                    n, hp, k = i // 4, i % 4, 16 * layer + i
                    kbs, _ = window(layer, n)
                    if i == 0:
                        pe.wait_ge(kx_done, 2 * (layer + 1))
                    if k >= 1:
                        pe.wait_ge(logits_done, k)
                    for j in range(2):
                        keys = KH[layer] if hp // 2 == j else KX[layer]
                        h64 = slice(64 * j, 64 * j + 64)
                        last = pe.matmul(acc[:, 2 + j, 0:len(kbs) * P], QH[layer][h64, hp, n * P:(n + 1) * P],
                                         keys[h64, kbs[0] * P:(kbs[-1] + 1) * P], start=True, stop=True)
                    last.then_inc(qk_done, 1)
                elif what == "transpose":
                    n, k = i // 4, 16 * layer + i
                    kbs, _ = window(layer, n)
                    pe.wait_ge(p_done, 2 * (k + 1))
                    if k >= 1:
                        pe.wait_ge(pTs_done, k)
                    for b in range(len(kbs)):
                        for j in range(2):
                            last = pe.transpose(psTf[:, (2 * b + j) * P:(2 * b + j + 1) * P],
                                                LG[layer][:, i % 3, j, 1 + b * P:1 + (b + 1) * P], ident[:, :])
                    last.then_inc(pT_done, 1)
                elif what == "pv":
                    n, hp, k = i // 4, i % 4, 16 * layer + i
                    g = hp // 2
                    kbs, _ = window(layer, n)
                    pe.wait_ge(pTs_done, k + 1)
                    if i == 0:
                        pe.wait_ge(vtok_done, layer + 1)
                    if k >= 1:
                        pe.wait_ge(o_done, k)
                    if k == 0:
                        pe.wait_ge(relf_sb, 1)
                    for j in range(2):
                        for b, kb in enumerate(kbs):
                            last = pe.matmul(ps6[64 * j:64 * j + 64, 0:P], VTOK[layer][:, kb, 64 * g:64 * g + 64],
                                             PT[layer][:, i % 2, (2 * b + j) * P:(2 * b + j + 1) * P],
                                             start=b == 0, stop=b == len(kbs) - 1)
                    last.then_inc(pv_done, 1)
                elif what == "gla_values":
                    pe.wait_ge(evac_done, mixer_tile(6 + i // 2, i % 2)[0] + 1)
                    pe.wait_ge(vtok_done, 1)
                    if i >= 1:
                        pe.wait_ge(vatok_done, i)
                    for b in range(NBLK):
                        last = pe.transpose(ps7[:, b * P:(b + 1) * P], vaf[:, i % 2, b * P:(b + 1) * P], ident[:, :])
                    last.then_inc(vaT_done, 1)
                elif what == "gla_gate":
                    d, t = i % 2, i // 2
                    if i == 0:
                        pe.wait_ge(mix1_in, 16 * MIX1_LOADS)
                        pe.wait_ge(vatok_done, 4)
                        pe.wait_ge(o_done, 16)
                    else:
                        pe.wait_ge(gx_done, i)
                    pe.matmul(ps7[:, :], gate_w[:, d, t * P:(t + 1) * P], zz[:, :], start=True, stop=True)\
                      .then_inc(gate_ps, 1)
                    if i >= 1:
                        gla_keys(i - 1)
                elif what == "gla_dS":
                    if i == 0:
                        gla_keys(3)
                    pe.wait_ge(kst_done, 4)
                    if i == 1:
                        pe.wait_ge(S_done, 14)
                    for d in range(2):
                        dst = acc[:, 2:4, :] if d == 0 else psT
                        for n in range(NCH):
                            if n == (NCH - 1 if d == 0 else 0):
                                continue
                            s64 = slice(64 * (n % 2), 64 * (n % 2) + 64)
                            for hh in range(2):
                                h = 2 * i + hh
                                last = pe.matmul(dst[64 * hh:64 * hh + 64, n % 2, (n // 2) * P:(n // 2 + 1) * P],
                                                 kst[s64, d, i, n // 2, 64 * hh:64 * hh + 64],
                                                 va_tok[s64, n // 2, h * P:(h + 1) * P], start=True, stop=True)
                    last.then_inc(dS_done, 1)
                elif what == "gla_A":
                    t, h64 = i // 2, slice(64 * (i % 2), 64 * (i % 2) + 64)
                    pe.wait_ge(kint_done, 4)
                    pe.wait_ge(qdec_done, 4)
                    pe.wait_ge(evac_done, E_WOUT)
                    for d in range(2):
                        if i >= 1:
                            pe.wait_ge(Am_done, 2 * (i - 1) + d + 1)
                        dst = ps6 if d == 0 else acc[:, 1, :]
                        for m in range(NBLK):
                            mm = slice(m * P, (m + 1) * P)
                            last = pe.matmul(dst[:, mm], kint[h64, d, t, mm], qdec[h64, d, t, mm], start=True, stop=True)
                        last.then_inc(A_done, 1)
                elif what == "gla_out":
                    t, h64 = i // 2, slice(64 * (i % 2), 64 * (i % 2) + 64)
                    pe.wait_ge(Am_done, 2 * i + 2)
                    pe.wait_ge(S_done, 14 * (t + 1))
                    if i >= 1:
                        pe.wait_ge(og_out, i)
                    for m in range(NBLK):
                        mm = slice(m * P, (m + 1) * P)
                        for d in range(2):
                            pe.matmul(acc[:, 0, mm], va_tok[:, m, i * P:(i + 1) * P], Am[:, d, mm],
                                      start=m == 0 and d == 0, stop=False)
                    for n in range(NCH):
                        nn = slice(n * GLA_C, (n + 1) * GLA_C)
                        for d in range(2):
                            if n == (0 if d == 0 else NCH - 1):
                                continue
                            last = pe.matmul(acc[:, 0, nn], S[h64, d, n, :], qdec[h64, d, t, nn],
                                             start=False, stop=n == NCH - 1)
                    last.then_inc(og_done, 1)
                    if i >= 1:
                        gla_sum(i - 1)
                elif what == "gla_gating":
                    gla_sum(3)
                elif what == "pool_out":
                    pe.wait_ge(mix2_in, 16 * MIX2_LOADS)
                    pe.wait_ge(o_done, 32)
                    pe.wait_ge(vtok_done, 2)
                    for g in range(4):
                        pe.wait_ge(pooled_done, g + 1)
                        dst = (ps6[:, :], ps7[:, :], psT[:, 0, :], psT[:, 1, :])[g]
                        pe.matmul(dst, pw[:, g, :], pooled[:, g, :], start=True, stop=True).then_inc(yb_ps, 1)

            for step in mixer1_steps():
                mixer_step_pe(0, step)
            order = (4, 5, 6, 7, 0, 1, 2, 3)
            c_par = 0
            project_pair(C_WOUT, E_WOUT, 1, order)
            project_chunks(C_WOUT + 2, E_WOUT + 4, order)
            token_sums(1)
            project_pair(C_UP0, E_UP0, 2)
            for half in range(2):
                if half == 0:
                    token_sums(2)
                    with pe.Fori(0, 3) as i:
                        project_chunks(i * 2 + (C_UP0 + 2), i * 4 + (E_UP0 + 4))
                else:
                    with pe.Fori(0, 4) as i:
                        project_chunks(i * 2 + C_UP1, i * 4 + E_UP1)
                c0, e0 = (C_DN0, E_DN0) if half == 0 else (C_DN1, E_DN1)
                with pe.Fori(0, 2) as i:
                    for pair in range(2):
                        for kg in range(2):
                            pe.wait_ge(hlo_done, HID * half + 8 * (kg + 1))
                            pe.wait_ge(lo_done, i * 4 + (c0 + 2 * pair + kg + 1))
                            for j in range(2):
                                bank = 2 * pair + j
                                if kg == 0:
                                    pe.wait_ge(evac_done, i * 4 + (e0 + bank - 3))
                                for k in range(KT):
                                    last = mm3(acc[:, bank, :], *w_tiles(kg, k, j), hid_hi[:, 8 * kg + k, :],
                                               hid_lo[:, 8 * kg + k, :], kg == 0 and k == 0, kg == 1 and k == KT - 1)
                                last.then_inc(tile_done[j], 1)
            token_sums(3)
            for step in mixer2_steps():
                mixer_step_pe(1, step)
            c_par = C_ABOUT
            project_pair(C_ABOUT, E_ABOUT, 4)
            project_chunks(C_ABOUT + 2, E_ABOUT + 4)
            token_sums(5)
            c_par = C_CAB
            pe.wait_ge(taps_in, 16)
            for k in range(KT):
                last = pe.transpose(ps6[:, k * TAPS:(k + 1) * TAPS], tap_rows[:, k * P:(k + 1) * P],
                                    ident[0:TAPS, 0:TAPS])
            last.then_inc(taps_ps, 1)
            project_pair(C_CAB, E_CAB, 5)
            token_sums(6)
            with pe.Fori(0, 3) as i:
                project_chunks(i * 2 + (C_CAB + 2), i * 4 + (E_CAB + 4))
            with pe.Fori(0, 2) as i:
                project_chunks(i * 2 + C_CGATE, i * 4 + E_CGATE)
            pe.wait_ge(conv_step, 2 * KT + 1)
            pe.matmul(ps6[:, :], ones[:, :], csum[:, :], start=True, stop=True).then_inc(musum_done, 1)
            token_sums(7)
            project_pair(C_COUT, E_COUT, 6)
            project_chunks(C_COUT + 2, E_COUT + 4)
            token_sums(8)
            for f in range(2 * NBLK):
                b, half = f // 2, f % 2
                pe.wait_ge(resid_done, 5 * KT if b else 4 * KT + 4 * (half + 1))
                if f >= 2:
                    pe.wait_ge(fo_done, f - 1)
                for k in range(4):
                    last = pe.transpose(psT[:, f % 2, k * P:(k + 1) * P],
                                        resid[:, 4 * half + k, b * P:(b + 1) * P], ident[:, :])
                last.then_inc(fT_done, 1)

        @block.gpsimd
        def _(pool):
            chain = Chain(pool, pool_step)
            pool.memset(eps[:, :], EPS).then_inc(eps_set, 1)
            pool.wait_ge(eps_set, 1)
            chain.link(pool.memset(relw[32:33, :], -1e30))
            pool.memset(gate_w[:, :, :], 0.0).then_inc(gatew_set, 1)
            pool.wait_ge(gatew_set, 1)

            def sum_squares(n, src=None):
                for k in range(KT):
                    pool.wait_ge(sq_done, 8 * n + k + 1)
                    if k == 0:
                        if n >= 1:
                            pool.wait_ge(rsum_done, n)
                        pool.tensor_copy(sq_sum[:, :], sq[:, k % 2, :]).then_inc(sqsum_done, 1)
                    else:
                        pool.wait_ge(sqsum_done, 8 * n + k)
                        pool.tensor_tensor(sq_sum[:, :], sq_sum[:, :], sq[:, k % 2, :], ALU.add)\
                            .then_inc(sqsum_done, 1)

            def sink_columns(layer, i):
                k, hp = 16 * layer + i, i % 4
                if i == 0:
                    pool.wait_ge(*((mix1_in, 16 * MIX1_LOADS) if layer == 0 else (mix2_in, 16 * MIX2_LOADS)))
                if i >= 3:
                    pool.wait_ge(pT_done, k - 2)
                pool.tensor_copy(LG[layer][:, i % 3, :, 0], SINK[layer][:, 2 * hp:2 * hp + 2]).then_inc(sink_set, 1)

            def mixer_step_pool(layer, step):
                what, i = step[0], step[1]
                k = 16 * layer + i
                if what == "keys_values":
                    for m in range(3):
                        sink_columns(layer, m)
                elif what == "normalise":
                    n = i // 4
                    kbs, _ = window(layer, n)
                    pool.wait_ge(rden_done, k + 1)
                    for j in range(2):
                        row = LG[layer][:, i % 3, j, 1:1 + len(kbs) * P]
                        pool.tensor_scalar(row, row, SM[layer][:, i % 3, j, 3:4], None, ALU.mult)\
                            .then_inc(p_done, 1)
                elif what == "transpose":
                    if i + 3 < 16:
                        sink_columns(layer, i + 3)
                elif what == "gla_gate":
                    d, t = i % 2, i // 2
                    if i == 0:
                        pool.wait_ge(o_done, 16)
                        pool.wait_ge(vatok_done, 4)
                        pool.memset(Am[:, :, :], 0.0).then_inc(Am_set, 1)
                    pool.wait_ge(enb_done, i + 1)
                    pool.tensor_tensor(kint[:, d, t, :], ka[:, t, :], gx[:, :], ALU.mult).then_inc(kint_done, 1)
                    pool.wait_ge(ek_done, i + 1)
                    pool.wait_ge(eb_done, i + 1)
                    pool.tensor_tensor(bb[:, :], ka[:, t, :], gl[:, :], ALU.mult).then_inc(ks_done, 1)
                elif what == "pool_window":
                    pool.wait_ge(evac_done, E_AIN + 2 * (5 + i // 2) + i % 2 + 1)
                    if i == 0:
                        pool.wait_ge(upad_set, 1)
                        pool.wait_ge(mix2_in, 16 * MIX2_LOADS)
                    else:
                        pool.wait_ge(pooled_done, i)
                    src = uu[:, i, :]
                    for m in range(i + 1):
                        sh, lo = 1 << m, (2 << m) - 1
                        dst = wsum[:, m % 2, :]
                        chain.link(pool.tensor_tensor(dst[:, lo:], src[:, lo:], src[:, lo - sh:UPAD + TOK - sh], ALU.add))
                        src = dst
                    pool.tensor_tensor(src[:, UPAD:UPAD + 16], src[:, UPAD:UPAD + 16], wcnt[:, i, :], ALU.mult)\
                        .then_inc(wsum_done, 1)

            sum_squares(0)
            for step in mixer1_steps():
                mixer_step_pool(0, step)
            for n in (1, 2, 3, 4):
                sum_squares(n)
            pool.memset(uu[:, :, 0:UPAD], 0.0).then_inc(upad_set, 1)
            for step in mixer2_steps():
                mixer_step_pool(1, step)
            sum_squares(5)
            pool.memset(glu[:, :, 0:CPAD], 0.0).then_inc(glu_done, 1)
            sum_squares(6)
            with pool.Fori(0, 4) as i:
                for s in range(2):
                    idx = i * 2 + s
                    pool.wait_ge(sig_done, i * 2 + (s + 1))
                    pool.tensor_tensor(glu[:, s, CPAD:], ab[:, 0, :], ab[:, 1, :], ALU.mult).then_inc(glu_done, 1)
                    for m in range(1, ACT_TAPS):
                        pool.wait_ge(prod_done, i * (2 * ACT_TAPS) + (s * ACT_TAPS + m + 1))
                        if m == 1:
                            pool.wait_ge(conv_step, i * 4 + (2 * s + 1))
                            pool.tensor_tensor(pacc[:, :], prod[:, 0, :], prod[:, 1, :], ALU.add)\
                                .then_inc(pacc_step, 1)
                        else:
                            pool.wait_ge(pacc_step, i * (2 * (ACT_TAPS - 1)) + (s * (ACT_TAPS - 1) + m - 1))
                            pool.tensor_tensor(pacc[:, :], pacc[:, :], prod[:, m % 2, :], ALU.add)\
                                .then_inc(pacc_step, 1)
            sum_squares(7)
            sum_squares(8)

        @block.scalar
        def _(act):
            chain = Chain(act, act_step)

            def col(v):
                return v.rearrange("(k p) -> k p", p=P)

            act.dma_start(ident_ones[:, :], a["shapes"][:, 0:2 * P]).then_inc(const_in, 16)
            for off, name in ((V_PRE1, "norm_mix_pre"), (V_POST1, "norm_mix_post"), (V_PREM, "norm_mlp_pre"),
                              (V_POSTM, "norm_mlp_post"), (V_DWB, "c_dw_b_2"), (V_LNG, "c_ln_g_2"),
                              (V_LNB, "c_ln_b_2")):
                act.dma_start(vec_rows[off:off + KT, :], col(a[name][0])).then_inc(vec_in, 16)
            for layer, (pre, post) in enumerate(((V_PRE2A, V_POST2A), (V_PRE2B, V_POST2B))):
                act.dma_start(vec_rows[pre:pre + KT, :], col(a["pre_norm_2"][layer])).then_inc(vec_in, 16)
                act.dma_start(vec_rows[post:post + KT, :], col(a["post_norm_2"][layer])).then_inc(vec_in, 16)
            act.dma_start(vec_rows[V_PSC:V_PSC + 4, :], col(a["b_pool_scale_2"][0])).then_inc(vec_in, 16)
            act.dma_start(vec_rows[V_GN:V_GN + 1, :], col(a["gla_norm"][0])).then_inc(vec_in, 16)
            act.dma_start(vec_rows[V_BF:V_BF + 2, :], col(a["b_gate_fwd"][0])).then_inc(vec_in, 16)
            act.dma_start(vec_rows[V_BB:V_BB + 2, :], col(a["b_gate_bwd"][0])).then_inc(vec_in, 16)
            act.dma_start(relw[0:32, :], a["rel_bias"]).then_inc(rel_in, 16)
            act.dma_start(hot[:, :], a["onehot"]).then_inc(rel_in, 16)

            def split(c):
                slot = (c if isinstance(c, int) else c_par) % 2
                if isinstance(c, int):
                    act.wait_ge(raw_ready[slot], 32 * (c // 2 + 1))
                    if c >= 2:
                        act.wait_ge(tile_done[1], c - 1)
                else:
                    act.wait_ge(raw_ready[slot], c * 16 + 16 * (2 - slot))
                    act.wait_ge(tile_done[1], c - 1)
                if isinstance(c, int) and c == 3:
                    act.activation(w_hi[:, slot, :, 0:P], raw[:, slot, :, 0:P], ACT.Copy).then_inc(hi_done, 1)
                else:
                    act.activation(w_hi[:, slot, :, :], raw[:, slot, :, :], ACT.Copy).then_inc(hi_done, 1)

            def square(n, k, src):
                if 8 * n + k >= 2:
                    act.wait_ge(sqsum_done, 8 * n + k - 1)
                act.activation(sq[:, k % 2, :], src, ACT.Square).then_inc(sq_done, 1)

            def token_scale(n, src=None):
                act.wait_ge(rsum_done, n + 1)
                chain.link(act.activation(R[:, :], ps7[:, :], ACT.Ln, bias=eps[:, 0:1], scale=1.0 / D))
                act.activation(R[:, :], R[:, :], ACT.Exp, scale=-0.5).then_inc(r_done, 1)

            def boundary(n, gain):
                for k in range(KT):
                    act.wait_ge(resid_done, 8 * n + k + 1)
                    act.activation(act_hi[:, k, :], resid[:, k, :], ACT.Copy, scale=vec[:, gain + k:gain + k + 1])\
                       .then_inc(act_hi_done, 1)
                    square((0, 2, 4, 6)[n], k, resid[:, k, :])

            def halves(tensor, order, wait):
                for k in order:
                    wait(act, k)
                    act.activation(act_hi[:, k, :], tensor[:, k, :], ACT.Copy).then_inc(act_hi_done, 1)

            def mixer_step_act(layer, step):
                what, i = step[0], step[1]
                k = 16 * layer + i
                if what == "split":
                    split(i)
                elif what == "keys_values":
                    for h in range(8 if layer == 0 else 0):
                        act.wait_ge(bias1_ps, h + 1)
                        act.activation(bias1[:, h, :], psT[:, h % 2, 0:BAND1], ACT.Copy).then_inc(bias1_done, 1)
                    act.wait_ge(evac_done, 6 if layer == 0 else E_AIN + 6)
                    act.activation(KX[layer][64:128, :], KH[layer][0:64, :], ACT.Copy).then_inc(kx_done, 1)
                    act.activation(KX[layer][0:64, :], KH[layer][64:128, :], ACT.Copy).then_inc(kx_done, 1)
                    act.wait_ge(vT_done, layer + 1)
                    act.activation(VTOK[layer][:, :, :], ps7[:, :].rearrange("p (b n) -> p b n", b=NBLK), ACT.Copy)\
                       .then_inc(vtok_done, 1)
                elif what == "softmax":
                    w = len(window(layer, i // 4)[0]) * P + 1
                    act.wait_ge(negmax_done, k + 1)
                    for j in range(2):
                        row = LG[layer][:, i % 3, j, 0:w]
                        act.activation(row, row, ACT.Exp, bias=SM[layer][:, i % 3, j, 1:2],
                                       accum_out=SM[layer][:, i % 3, j, 2:3]).then_inc(exp_done, 1)
                elif what == "transpose":
                    w = len(window(layer, i // 4)[0]) * 2 * P
                    act.wait_ge(pT_done, k + 1)
                    if k >= 2:
                        act.wait_ge(pv_done, k - 1)
                    act.activation(PT[layer][:, i % 2, 0:w], psTf[:, 0:w], ACT.Copy).then_inc(pTs_done, 1)
                elif what == "pv":
                    n, hp = i // 4, i % 4
                    act.wait_ge(pv_done, k + 1)
                    act.activation(OO[layer][:, o_tile(layer, hp), n * P:(n + 1) * P], ps6[:, 0:P], ACT.Copy)\
                       .then_inc(o_done, 1)
                elif what == "gla_values":
                    act.wait_ge(vaT_done, i + 1)
                    act.activation(va_tok[:, :, i * P:(i + 1) * P], ps7[:, :].rearrange("p (b n) -> p b n", b=NBLK),
                                   ACT.Copy).then_inc(vatok_done, 1)
                elif what == "gla_gate":
                    d, t = i % 2, i // 2
                    act.wait_ge(gx_done, i + 1)
                    if i >= 1:
                        act.wait_ge(ks_done, i)
                        kst_copy(i - 1)
                    chain.link(act.activation(gl[:, :], gx[:, :], ACT.Abs))
                    chain.link(act.activation(gl[:, :], gl[:, :], ACT.Exp, scale=-1.0))
                    act.activation(gl[:, :], gl[:, :], ACT.Ln, bias=1.0).then_inc(ln_done, 1)
                    act.wait_ge(bb_done, i + 1)
                    if i >= 1:
                        act.wait_ge(qdec_done, i)
                        act.wait_ge(decay_done, i)
                    act.activation(eb[:, :], bb[:, :], ACT.Exp, scale=1.0 / GATE_NORM).then_inc(eb_done, 1)
                    act.activation(gx[:, :], bb[:, :], ACT.Exp, scale=-1.0 / GATE_NORM).then_inc(enb_done, 1)
                    act.wait_ge(dk_done, i + 1)
                    act.activation(gl[:, :], gl[:, :], ACT.Exp, scale=1.0 / GATE_NORM).then_inc(ek_done, 1)
                elif what == "gla_dS" and i == 0:
                    kst_copy(3)
                elif what == "gla_out":
                    act.wait_ge(og_done, i + 1)
                    act.activation(o1[:, i, :], acc[:, 0, :], ACT.Copy).then_inc(og_out, 1)
                    act.wait_ge(og_out, i + 1)
                    if i >= 2:
                        act.wait_ge(ogsum_done, i - 1)
                    act.activation(sq[:, i % 2, :], o1[:, i, :], ACT.Square).then_inc(ogsq_done, 1)
                    if i >= 1:
                        head_scale(i - 1)
                elif what == "gla_gating":
                    split(11)
                    halves(o1, (4, 5, 6, 7), lambda e, k: e.wait_ge(o_done, 16))
                    head_scale(3)
                    act.wait_ge(evac_done, E_WOUT)
                    for h in range(4):
                        act.activation(ga[:, h, :], ga[:, h, :], ACT.Silu).then_inc(silu_done, 1)
                    halves(o1, (0, 1, 2, 3), lambda e, k: e.wait_ge(og_gated, k + 1))
                elif what == "attention_gate":
                    act.wait_ge(evac_done, E_AIN + 10)
                    for h in range(4):
                        act.activation(ga2[:, h, :], ga2[:, h, :], ACT.Silu).then_inc(silu2_done, 1)
                elif what == "pool_out":
                    act.wait_ge(evac_done, E_ABOUT)
                    for h in range(4):
                        act.activation(gb2[:, h, :], gb2[:, h, :], ACT.Silu).then_inc(silu2_done, 1)
                    split(56)
                    halves(o2, range(KT), lambda e, k: e.wait_ge(ob_done, k + 1))

            def kst_copy(i):
                act.wait_ge(kT_done, i + 1)
                act.activation(kst[:, i % 2, i // 2, :, :], ps6[:, :].rearrange("p (b n) -> p b n", b=NBLK), ACT.Copy)\
                   .then_inc(kst_done, 1)

            def head_scale(h):
                rr = (gx, gl)[h % 2]
                act.wait_ge(ogsum_done, h + 1)
                if h >= 2:
                    act.wait_ge(on_done, h - 1)
                chain.link(act.activation(rr[:, :], ps7[:, :], ACT.Ln, bias=eps[:, 0:1], scale=1.0 / P))
                act.activation(rr[:, :], rr[:, :], ACT.Exp, scale=-0.5).then_inc(rr_done, 1)

            act.wait_ge(vec_ps, 1)
            act.activation(vec[:, :], ps7[:, 0:V_N], ACT.Copy).then_inc(vec_done, 1)
            act.wait_ge(vec_done, 1)
            boundary(0, V_PRE1)
            act.wait_ge(relf_ps, 1)
            act.activation(relF[:, :], ps6[0:8, :], ACT.Copy).then_inc(relf_sb, 1)
            act.wait_ge(relf_sb, 1)
            act.dma_start(relF_dram, relF[:, :]).then_inc(relf_out, 16)
            act.wait_ge(relf_out, 16)
            act.dma_start(hankel[:, :, :], bass.AP(relF_dram.tensor, 0, [[1, P], [512, 8], [1, BAND1]]))\
               .then_inc(bias1_in, 16)
            act.dma_start(flip[:, :], a["shapes"][:, 4 * P + TOK + 64:5 * P + TOK + 64]).then_inc(bias1_in, 16)
            act.dma_start(sink1[:, :], bass.AP(a["swa_sink"].tensor, 0, [[0, P], [1, 8]])).then_inc(mix1_in, 16)
            act.dma_start(masks[:, :, :], a["shapes"][:, 2 * P:4 * P].rearrange("p (d n) -> p d n", d=2))\
               .then_inc(mix1_in, 16)
            act.dma_start(restart[:, :], a["shapes"][:, 4 * P:4 * P + TOK]).then_inc(mix1_in, 16)
            act.wait_ge(gatew_set, 1)
            act.dma_start(gate_w[0:16, 0, :], a["w_gate_up_fwd"][0]).then_inc(mix1_in, 16)
            act.dma_start(gate_w[16:32, 1, :], a["w_gate_up_bwd"][0]).then_inc(mix1_in, 16)
            split(0)
            token_scale(0)
            for step in mixer1_steps():
                mixer_step_act(0, step)

            c_par = 0

            def plain_turns(c0, turns, last=True):
                nonlocal c_par
                c_par = c0 + 1
                with act.Fori(0, turns) as i:
                    for s in range(2):
                        c_par = c0 + s + 1
                        split(i * 2 + (c0 + s + 1))

            def squares_of_y(n, e, k0=0):
                for k in range(KT):
                    act.wait_ge(evac_done, e + k + 1)
                    square(n, k, y[:, k, :])

            def out_squares(n, c, e):
                for k in range(KT):
                    if k in (0, 2, 4) and c + 2 + k // 2 < C_END:
                        split(c + 2 + k // 2)
                    act.wait_ge(evac_done, e + k + 1)
                    square(n, k, y[:, k, :])

            out_squares(1, C_WOUT, E_WOUT)
            token_scale(1)
            split(C_UP0 + 1)
            boundary(1, V_PREM)
            token_scale(2)
            for half in range(2):
                cu, cd = (C_UP0, C_DN0) if half == 0 else (C_UP1, C_DN1)
                peeled = half == 0
                m0 = HID * half
                e_off = (E_UP0 if half == 0 else E_UP1 - HID)

                def up_tile(h_slot, idx, hid_ap, static_idx):
                    act.wait_ge(evac_done, idx + (e_off + 1))
                    if static_idx is None or static_idx >= 2:
                        act.wait_ge(hlo_done, idx - 1)
                    act.activation(zq[:, h_slot, :], zt[:, h_slot, :], ACT.Square).then_inc(zq_done, 1)
                    act.wait_ge(zq_done, idx + 1)
                    act.wait_ge(eps_set, 1)
                    act.activation(hid_ap, zq[:, h_slot, :], ACT.Copy).then_inc(hhi_done, 1)

                first = 0
                if half == 0:
                    for s in range(2):
                        if s == 0:
                            split(cu + 2)
                        for j in range(2):
                            up_tile(j, 2 * s + j, hid_hi[:, 2 * s + j, :], 2 * s + j)
                    first = 1
                else:
                    c_par = cu
                with act.Fori(0, 4 - first) as i:
                    for s in range(2):
                        c_par = cu + s + 1
                        split(i * 2 + (cu + 2 * first + s + 1))
                        for j in range(2):
                            up_tile(j, i * 4 + (m0 + 4 * first + 2 * s + j),
                                    hid_hi[:, bass.ds(i * 4 + (4 * first + 2 * s + j), 1), :], None)
                if half == 0:
                    plain_turns(cd, 4)
                else:
                    for p in range(4):
                        split(cd + 2 * p + 1)
                        split(cd + 2 * p + 2)
                        for j in range(2):
                            act.wait_ge(evac_done, E_DN1 + 2 * p + j + 1)
                            square(3, 2 * p + j, y[:, 2 * p + j, :])
            token_scale(3)
            act.dma_start(sink2[:, :], bass.AP(a["a_sinks_2"].tensor, 0, [[0, P], [1, 8]])).then_inc(mix2_in, 16)
            act.dma_start(bias2[:, :, :], a["alibi"]).then_inc(mix2_in, 16)
            act.dma_start(pw[:, :, :], a["b_pool_w_2"][0].rearrange("g c d -> c g d")).then_inc(mix2_in, 16)
            act.dma_start(wcnt[:, :, :], a["shapes"][:, 4 * P + TOK:4 * P + TOK + 64]
                          .rearrange("p (g n) -> p g n", g=4)).then_inc(mix2_in, 16)
            boundary(2, V_PRE2A)
            token_scale(4)
            for step in mixer2_steps():
                mixer_step_act(1, step)
            out_squares(5, C_ABOUT, E_ABOUT)
            token_scale(5)
            split(C_CAB + 1)
            act.dma_start(tap_rows[:, :], a["c_dw_w_2"][0, :, 0, :]).then_inc(taps_in, 16)
            act.wait_ge(taps_ps, 1)
            act.activation(taps[:, :, :], ps6[:, 0:KT * TAPS].rearrange("p (k t) -> p k t", k=KT), ACT.Copy)\
               .then_inc(taps_done, 1)
            boundary(3, V_PRE2B)
            token_scale(6)
            with act.Fori(0, 4) as i:
                for s in range(2):
                    act.wait_ge(evac_done, i * 4 + (E_CAB + 2 * s + 2))
                    act.activation(ab[:, 1, :], ab[:, 1, :], ACT.Sigmoid).then_inc(sig_done, 1)
                    c_par = C_CAB + s + 2
                    split(i * 2 + (C_CAB + s + 2))
                    act.wait_ge(glu_done, i * 2 + (s + 2))
                    act.wait_ge(tapw_done, i * 4 + (2 * s + 2))
                    for m in range(ACT_TAPS):
                        tap = DVE_TAPS + m
                        if m >= 2:
                            act.wait_ge(pacc_step, i * (2 * (ACT_TAPS - 1)) + (s * (ACT_TAPS - 1) + max(1, m - 2)))
                        act.activation(prod[:, m % 2, :], glu[:, s, tap:tap + TOK], ACT.Copy,
                                       scale=tapw[:, s, tap:tap + 1]).then_inc(prod_done, 1)
            for c in range(C_CGATE + 2, C_CGATE + 6):
                split(c)
            act.wait_ge(musum_done, 1)
            act.activation(mu[:, :], ps6[:, :], ACT.Copy, scale=1.0 / D).then_inc(mu_done, 1)
            for k in range(KT):
                act.wait_ge(cen_done, k + 1)
                square(7, k, conv[:, k, :])
            token_scale(7)
            act.wait_ge(evac_done, E_COUT)
            act.activation(gate[:, :, :], gate[:, :, :], ACT.Silu).then_inc(gsilu_done, 1)
            for k in range(KT):
                act.wait_ge(cn_done, k + 1)
                act.activation(conv[:, k, :], conv[:, k, :], ACT.Silu, bias=vec[:, V_LNB + k:V_LNB + k + 1],
                               scale=vec[:, V_LNG + k:V_LNG + k + 1]).then_inc(csilu_done, 1)
                if k >= 1:
                    act.wait_ge(yc_done, k)
                    act.activation(act_hi[:, k - 1, :], yc[:, (k - 1) % 2, :], ACT.Copy).then_inc(act_hi_done, 1)
            act.wait_ge(yc_done, KT)
            act.activation(act_hi[:, KT - 1, :], yc[:, (KT - 1) % 2, :], ACT.Copy).then_inc(act_hi_done, 1)
            out_squares(8, C_COUT, E_COUT)
            token_scale(8)
            for f in range(2 * NBLK):
                act.wait_ge(fT_done, f + 1)
                if f >= 2:
                    act.wait_ge(out_done[f % 2], 16 * (f // 2))
                act.activation(o_tok[:, f % 2, :], psT[:, f % 2, :], ACT.Copy).then_inc(fo_done, 1)

        @block.vector
        def _(dve):
            chain = Chain(dve, dve_step)
            c_par = 0

            def split(c):
                slot = (c if isinstance(c, int) else c_par) % 2
                cols = slice(0, P) if isinstance(c, int) and c == 3 else slice(0, CW)
                dve.wait_ge(hi_done, c + 1)
                dve.tensor_tensor(w_lo[:, slot, :, cols], raw[:, slot, :, cols],
                                  w_hi[:, slot, :, cols].bitcast(F32), ALU.subtract).then_inc(lo_done, 1)

            def evac_scaled(c, j, bank, dst, rows=P):
                dve.wait_ge(tile_done[j], c + 1)
                dve.tensor_tensor(dst, acc[0:rows, bank, :], R[0:rows, :], ALU.mult).then_inc(evac_done, 1)

            def lo_of_scaled(n, k, gain):
                dve.wait_ge(act_hi_done, 8 * (0, 2, 3, 5)[n] + k + 1)
                dve.scalar_tensor_tensor(out=act_lo[:, k, :], in0=resid[:, k, :],
                                         scalar=vec[:, gain + k:gain + k + 1],
                                         in1=act_hi[:, k, :].bitcast(F32), op0=ALU.mult, op1=ALU.subtract)\
                   .then_inc(act_lo_done, 1)

            def boundary(n, post, gain, tmp):
                for k in range(KT):
                    if k == 0:
                        dve.wait_ge(r_done, 2 * n)
                    chain.link(dve.tensor_tensor(tmp[:, k % 2, :], y[:, k, :], R[:, :], ALU.mult))
                    dve.scalar_tensor_tensor(out=resid[:, k, :], in0=tmp[:, k % 2, :],
                                             scalar=vec[:, post + k:post + k + 1], in1=resid[:, k, :],
                                             op0=ALU.mult, op1=ALU.add).then_inc(resid_done, 1)
                    if gain is not None and k >= 1:
                        lo_of_scaled(n, k - 1, gain)
                if gain is not None:
                    lo_of_scaled(n, KT - 1, gain)

            def lower_halves(tensor, order, n, first):
                for m, k in enumerate(order):
                    dve.wait_ge(act_hi_done, 8 * n + first + m + 1)
                    dve.tensor_tensor(act_lo[:, k, :], tensor[:, k, :], act_hi[:, k, :].bitcast(F32), ALU.subtract)\
                       .then_inc(act_lo_done, 1)

            def mixer_tile_dve(c, j):
                e, bank = mixer_tile(c, j)
                if c == 0 and j == 0:
                    dve.wait_ge(r_done, 1)
                if c == C_AIN and j == 0:
                    dve.wait_ge(r_done, 5)
                if c < 2:
                    dst = qs1[:, 2 * c + j, :]
                elif c == 2:
                    dst = (k1, v1)[j][:, :]
                elif c == 3:
                    dst = zz[:, :]
                elif c < 6:
                    if c == 4 and j == 0:
                        dve.wait_ge(relf_out, 16)
                    dst = (qa, ka)[c - 4][:, j, :]
                elif c < 8:
                    h = 2 * (c - 6) + j
                    if h >= 2:
                        dve.wait_ge(vaT_done, h - 1)
                    dst = vaf[:, h % 2, :]
                elif c < 10:
                    dst = ga[:, 2 * (c - 8) + j, :]
                else:
                    i, t = (c - C_AIN) // 2, 2 * ((c - C_AIN) % 2) + j
                    m = c - C_AIN
                    if m < 2:
                        dst = q2[:, 2 * m + j, :]
                    elif m == 2:
                        dst = (k2, v2)[j][:, :]
                    elif m < 5:
                        dst = ga2[:, 2 * (m - 3) + j, :]
                    elif m < 7:
                        dst = uu[:, 2 * (m - 5) + j, UPAD:]
                    else:
                        dst = gb2[:, 2 * (m - 7) + j, :]
                evac_scaled(c, j, bank, dst, 32 if c == 3 else P)

            def mixer_step_dve(layer, step):
                what, i = step[0], step[1]
                k = 16 * layer + i
                if what == "split":
                    split(i)
                elif what == "tile":
                    mixer_tile_dve(step[1], step[2])
                elif what == "softmax":
                    n, hp = i // 4, i % 4
                    kbs, b0 = window(layer, n)
                    w = len(kbs) * P
                    lg, sm = LG[layer][:, i % 3, :, :], SM[layer][:, i % 3, :, :]
                    if i == 0 and layer == 0:
                        dve.wait_ge(bias1_done, 8)
                    if i == 0 and layer == 1:
                        dve.wait_ge(mix2_in, 16 * MIX2_LOADS)
                    dve.wait_ge(qk_done, k + 1)
                    if i >= 3:
                        dve.wait_ge(pT_done, k - 2)
                    dve.scalar_tensor_tensor(out=lg[:, :, 1:1 + w], in0=acc[:, 2:4, 0:w], scalar=QSCALE,
                                             in1=BIAS[layer][:, 2 * hp:2 * hp + 2, b0:b0 + w],
                                             op0=ALU.mult, op1=ALU.add).then_inc(logits_done, 1)
                    dve.wait_ge(logits_done, k + 1)
                    dve.wait_ge(sink_set, k + 1)
                    chain.link(dve.tensor_reduce(sm[:, :, 0], lg[:, :, 0:1 + w], AX.X, ALU.max))
                    dve.tensor_scalar(sm[:, :, 1], sm[:, :, 0], -1.0, None, ALU.mult).then_inc(negmax_done, 1)
                elif what == "normalise":
                    dve.wait_ge(exp_done, 2 * (k + 1))
                    sm = SM[layer][:, i % 3, :, :]
                    dve.reciprocal(sm[:, :, 3], sm[:, :, 2]).then_inc(rden_done, 1)
                elif what == "gla_gate":
                    d, t = i % 2, i // 2
                    rev = slice(None, None, -1 if d else 1)
                    bias = vec[:, (V_BF, V_BB)[d] + t:(V_BF, V_BB)[d] + t + 1]
                    dve.wait_ge(gate_ps, i + 1)
                    if i == 0:
                        dve.wait_ge(o_done, 16)
                        dve.wait_ge(vatok_done, 4)
                        dve.wait_ge(mix1_in, 16 * MIX1_LOADS)
                    else:
                        dve.wait_ge(kint_done, i)
                    dve.tensor_scalar(gx[:, :], ps7[:, :], bias, None, ALU.add).then_inc(gx_done, 1)
                    dve.wait_ge(ln_done, i + 1)
                    chain.link(dve.scalar_tensor_tensor(out=gx[:, :], in0=gx[:, :], scalar=0.0, in1=gl[:, :],
                                                        op0=ALU.min, op1=ALU.subtract))
                    if i >= 1:
                        dve.wait_ge(kT_done, i)
                    dve.tensor_tensor_scan(bb[:, rev], restart[:, :], gx[:, rev], 0.0, ALU.mult, ALU.add)\
                       .then_inc(bb_done, 1)
                    dve.wait_ge(bb_done, i + 1)
                    end = GLA_C - 1 if d == 0 else 0
                    b3 = bb[:, :].rearrange("p (n c) -> p n c", c=GLA_C)
                    dve.tensor_tensor(gl[:, :].rearrange("p (n c) -> p n c", c=GLA_C),
                                      b3[:, :, end:end + 1].to_broadcast([P, NCH, GLA_C]), b3, ALU.subtract)\
                       .then_inc(dk_done, 1)
                    dve.wait_ge(eb_done, i + 1)
                    dve.tensor_copy(decay[:, d, t, :], eb[:, :].rearrange("p (n c) -> p n c", c=GLA_C)[:, :, end])\
                       .then_inc(decay_done, 1)
                    dve.scalar_tensor_tensor(out=qdec[:, d, t, :], in0=qa[:, t, :], scalar=QSCALE, in1=eb[:, :],
                                             op0=ALU.mult, op1=ALU.mult).then_inc(qdec_done, 1)
                elif what == "gla_dS":
                    dve.wait_ge(dS_done, i + 1)
                    dve.wait_ge(decay_done, 4)
                    if i == 1:
                        dve.wait_ge(og_done, 2)
                    count = 14 * i
                    for m in range(NCH - 1):
                        for d in range(2):
                            n = m if d == 0 else NCH - 1 - m
                            to = n + 1 if d == 0 else n - 1
                            src = (acc[:, 2:4, :] if d == 0 else psT)[:, n % 2, (n // 2) * P:(n // 2 + 1) * P]
                            if m == 0:
                                ins = dve.tensor_copy(S[:, d, to, :], src)
                            else:
                                dve.wait_ge(S_done, count - 1)
                                ins = dve.scalar_tensor_tensor(out=S[:, d, to, :], in0=S[:, d, n, :],
                                                               scalar=decay[:, d, i, n:n + 1], in1=src,
                                                               op0=ALU.mult, op1=ALU.add)
                            ins.then_inc(S_done, 1)
                            count += 1
                elif what == "gla_A":
                    for d in range(2):
                        dve.wait_ge(A_done, 2 * i + d + 1)
                        if i == 0:
                            dve.wait_ge(Am_set, 1)
                        else:
                            dve.wait_ge(og_done, i)
                        src = ps6 if d == 0 else acc[:, 1, :]
                        mask = masks[:, d:d + 1, :].bitcast(I32).to_broadcast([P, NBLK, P])
                        dve.copy_predicated(Am[:, d, :].rearrange("p (m c) -> p m c", c=P), mask,
                                            src[:, :].rearrange("p (m c) -> p m c", c=P)).then_inc(Am_done, 1)
                elif what == "gla_out" and i >= 1:
                    gla_normed(i - 1)
                elif what == "gla_gating":
                    split(11)
                    lower_halves(o1, (4, 5, 6, 7), 1, 0)
                    gla_normed(3)
                    for h in range(4):
                        dve.wait_ge(silu_done, h + 1)
                        if h == 0:
                            dve.wait_ge(on_done, 4)
                        dve.scalar_tensor_tensor(out=o1[:, h, :], in0=o1[:, h, :], scalar=vec[:, V_GN:V_GN + 1],
                                                 in1=ga[:, h, :], op0=ALU.mult, op1=ALU.mult).then_inc(og_gated, 1)
                        if h >= 1:
                            lower_halves(o1, (h - 1,), 1, 4 + h - 1)
                    lower_halves(o1, (3,), 1, 7)
                elif what == "pool_window":
                    dve.wait_ge(wsum_done, i + 1)
                    dve.scalar_tensor_tensor(out=pooled[:, i, :], in0=wsum[:, i % 2, UPAD:], scalar=1.0 / POOLW[i],
                                             in1=uu[:, i, UPAD:], op0=ALU.mult, op1=ALU.subtract)\
                       .then_inc(pooled_done, 1)
                elif what == "attention_gate":
                    for h in range(4):
                        dve.wait_ge(silu2_done, h + 1)
                        if h == 0:
                            dve.wait_ge(o_done, 32)
                        dve.tensor_tensor(o2[:, h, :], o2[:, h, :], ga2[:, h, :], ALU.mult).then_inc(ob_done, 1)
                elif what == "pool_out":
                    split(56)
                    lower_halves(o2, range(4), 4, 0)
                    for g in range(4):
                        dve.wait_ge(silu2_done, 5 + g)
                        dve.wait_ge(yb_ps, g + 1)
                        src = (ps6[:, :], ps7[:, :], psT[:, 0, :], psT[:, 1, :])[g]
                        dve.scalar_tensor_tensor(out=o2[:, 4 + g, :], in0=src, scalar=vec[:, V_PSC + g:V_PSC + g + 1],
                                                 in1=gb2[:, g, :], op0=ALU.mult, op1=ALU.mult).then_inc(ob_done, 1)
                        if g >= 1:
                            lower_halves(o2, (3 + g,), 4, 3 + g)
                    lower_halves(o2, (7,), 4, 7)

            def gla_normed(h):
                dve.wait_ge(rr_done, h + 1)
                dve.tensor_tensor(o1[:, h, :], o1[:, h, :], (gx, gl)[h % 2][:, :], ALU.mult).then_inc(on_done, 1)

            def out_tiles(c, e):
                for k in range(KT):
                    if k in (0, 2, 4) and c + 2 + k // 2 < C_END:
                        split(c + 2 + k // 2)
                    dve.wait_ge(tile_done[k % 2], c + k // 2 + 1)
                    dve.tensor_copy(y[:, k, :], acc[:, k % 4, :]).then_inc(evac_done, 1)

            for k in range(KT):
                dve.wait_ge(xT_done, k + 1)
                dve.tensor_copy(resid[:, k, :], acc[:, k % 4, :]).then_inc(resid_done, 1)
                if k == 0:
                    dve.wait_ge(vec_done, 1)
                if k >= 1:
                    lo_of_scaled(0, k - 1, V_PRE1)
            lo_of_scaled(0, KT - 1, V_PRE1)
            split(0)
            for step in mixer1_steps():
                mixer_step_dve(0, step)
            out_tiles(C_WOUT, E_WOUT)
            split(C_UP0 + 1)
            boundary(1, V_POST1, V_PREM, ty)
            dve.wait_ge(r_done, 3)

            def up_tile(j, bank, c, e, m, hid_ap, ring_free):
                dve.wait_ge(tile_done[j], c + 1)
                if ring_free is not None:
                    dve.wait_ge(zq_done, ring_free)
                dve.scalar_tensor_tensor(out=zt[:, j, :], in0=acc[:, bank, :], scalar=0.0, in1=R[:, :],
                                         op0=ALU.max, op1=ALU.mult).then_inc(evac_done, 1)

            for half in range(2):
                cu, cd = (C_UP0, C_DN0) if half == 0 else (C_UP1, C_DN1)
                eu, ed = (E_UP0, E_DN0) if half == 0 else (E_UP1, E_DN1)
                first = 1 if half == 0 else 0
                if half == 0:
                    split(cu + 2)
                    for m in range(4):
                        up_tile(m % 2, m, cu + m // 2, eu + m, m, None, m - 1 if m >= 2 else None)
                        dve.wait_ge(hhi_done, m + 1)
                        dve.tensor_tensor(hid_lo[:, m, :], zq[:, m % 2, :], hid_hi[:, m, :].bitcast(F32), ALU.subtract)\
                           .then_inc(hlo_done, 1)
                with dve.Fori(0, 4 - first) as i:
                    for s in range(2):
                        c_par = cu + s + 1
                        split(i * 2 + (cu + 2 * first + s + 1))
                        for j in range(2):
                            m = i * 4 + (HID * half + 4 * first + 2 * s + j)
                            mh = i * 4 + (4 * first + 2 * s + j)
                            up_tile(j, 2 * s + j, i * 2 + (cu + 2 * first + s), None, m, None, m - 1)
                            dve.wait_ge(hhi_done, m + 1)
                            dve.tensor_tensor(hid_lo[:, bass.ds(mh, 1), :], zq[:, j:j + 1, :],
                                              hid_hi[:, bass.ds(mh, 1), :].bitcast(F32), ALU.subtract)\
                               .then_inc(hlo_done, 1)
                with dve.Fori(0, 2) as i:
                    for pair in range(2):
                        for kg in range(2):
                            c_par = cd + kg + 1
                            split(i * 4 + (cd + 2 * pair + kg + 1))
                        for j in range(2):
                            t = i * 4 + (2 * pair + j)
                            dve.wait_ge(tile_done[j], i * 4 + (cd + 2 * pair + 2))
                            yt = y[:, bass.ds(t, 1), :]
                            bank = acc[:, 2 * pair + j:2 * pair + j + 1, :]
                            if half == 0:
                                dve.tensor_scalar(yt, bank, 1.0, None, ALU.mult).then_inc(evac_done, 1)
                            else:
                                dve.tensor_tensor(yt, bank, yt, ALU.add).then_inc(evac_done, 1)
            boundary(2, V_POSTM, V_PRE2A, ty_e)
            for step in mixer2_steps():
                mixer_step_dve(1, step)
            out_tiles(C_ABOUT, E_ABOUT)
            split(C_CAB + 1)
            boundary(3, V_POST2A, V_PRE2B, ty_c)
            dve.memset(csum[:, :], 0.0).then_inc(conv_step, 1)
            dve.wait_ge(r_done, 7)
            with dve.Fori(0, 4) as i:
                chain.enter(i, 2 * DVE_TAPS)
                for s in range(2):
                    idx = i * 2 + s
                    for j in range(2):
                        dve.wait_ge(tile_done[j], i * 2 + (C_CAB + s + 1))
                        if j == 0:
                            dve.wait_ge(glu_done, i * 2 + (s + 1))
                        dve.tensor_tensor(ab[:, j, :], acc[:, 2 * s + j, :], R[:, :], ALU.mult)\
                           .then_inc(evac_done, 1)
                    c_par = C_CAB + s + 2
                    split(i * 2 + (C_CAB + s + 2))
                    dve.wait_ge(conv_step, i * 4 + (2 * s + 1))
                    dve.wait_ge(taps_done, 1)
                    dve.tensor_copy(tapw[:, s:s + 1, 0:TAPS], taps[:, bass.ds(idx, 1), :]).then_inc(tapw_done, 1)
                    dve.tensor_copy(tapw[:, s, TAPS:TAPS + 1], vec[:, bass.ds(i * 2 + (V_DWB + s), 1)])\
                       .then_inc(tapw_done, 1)
                    dve.wait_ge(tapw_done, i * 4 + (2 * s + 2))
                    dve.wait_ge(glu_done, i * 2 + (s + 2))
                    for m in range(DVE_TAPS):
                        src = glu[:, s, m:m + TOK]
                        if m == 0:
                            chain.link(dve.tensor_scalar(vacc[:, :], src, tapw[:, s, 0:1], tapw[:, s, TAPS:TAPS + 1],
                                                         ALU.mult, ALU.add))
                        else:
                            chain.link(dve.scalar_tensor_tensor(out=vacc[:, :], in0=src, scalar=tapw[:, s, m:m + 1],
                                                                in1=vacc[:, :], op0=ALU.mult, op1=ALU.add))
                    dve.wait_ge(pacc_step, i * (2 * (ACT_TAPS - 1)) + (s + 1) * (ACT_TAPS - 1))
                    dve.tensor_tensor(conv[:, bass.ds(idx, 1), :], vacc[:, :].rearrange("p (a n) -> p a n", a=1),
                                      pacc[:, :].rearrange("p (a n) -> p a n", a=1), ALU.add).then_inc(conv_step, 1)
                    dve.wait_ge(conv_step, i * 4 + (2 * s + 2))
                    dve.tensor_tensor(csum[:, :].rearrange("p (a n) -> p a n", a=1),
                                      csum[:, :].rearrange("p (a n) -> p a n", a=1),
                                      conv[:, bass.ds(idx, 1), :], ALU.add).then_inc(conv_step, 1)
            chain.leave(4)
            with dve.Fori(0, 2) as i:
                for s in range(2):
                    for j in range(2):
                        dve.wait_ge(tile_done[j], i * 2 + (C_CGATE + s + 1))
                        dve.tensor_tensor(gate[:, bass.ds(i * 4 + (2 * s + j), 1), :],
                                          acc[:, 2 * s + j:2 * s + j + 1, :],
                                          R[:, :].rearrange("p (a n) -> p a n", a=1), ALU.mult).then_inc(evac_done, 1)
                    c_par = C_CGATE + s + 2
                    split(i * 2 + (C_CGATE + s + 2))
            dve.wait_ge(mu_done, 1)
            dve.wait_ge(conv_step, 2 * KT + 1)
            for k in range(KT):
                dve.tensor_tensor(conv[:, k, :], conv[:, k, :], mu[:, :], ALU.subtract).then_inc(cen_done, 1)
            dve.wait_ge(r_done, 8)
            dve.wait_ge(cen_done, KT)
            for k in range(KT + 2):
                if k < KT:
                    dve.tensor_tensor(conv[:, k, :], conv[:, k, :], R[:, :], ALU.mult).then_inc(cn_done, 1)
                if 1 <= k <= KT:
                    m = k - 1
                    dve.wait_ge(csilu_done, m + 1)
                    if m == 0:
                        dve.wait_ge(gsilu_done, 1)
                    if m >= 2:
                        dve.wait_ge(act_lo_done, 8 * 6 + m - 1)
                    dve.tensor_tensor(yc[:, m % 2, :], conv[:, m, :], gate[:, m, :], ALU.mult).then_inc(yc_done, 1)
                if k >= 2:
                    m = k - 2
                    dve.wait_ge(act_hi_done, 8 * 6 + m + 1)
                    dve.tensor_tensor(act_lo[:, m, :], yc[:, m % 2, :], act_hi[:, m, :].bitcast(F32), ALU.subtract)\
                       .then_inc(act_lo_done, 1)
            out_tiles(C_COUT, E_COUT)
            dve.wait_ge(r_done, 9)
            boundary(4, V_POST2B, None, ty_c)


_INS = ["x", "norm_mix_pre", "w_in", "w_gate_up_fwd", "b_gate_fwd", "w_gate_up_bwd", "b_gate_bwd", "gla_norm",
        "swa_sink", "rel_bias", "w_out", "norm_mix_post", "norm_mlp_pre", "w_up", "w_down", "norm_mlp_post",
        "pre_norm_2", "post_norm_2", "a_w_in_2", "a_sinks_2", "b_pool_w_2", "b_pool_scale_2", "ab_w_out_2",
        "c_w_in_2", "c_dw_w_2", "c_dw_b_2", "c_ln_g_2", "c_ln_b_2", "c_w_out_2"]


def kernel(**inputs):
    import numpy as _np
    import concourse.bacc as _bacc
    from concourse import mybir as _mybir
    from concourse.bass_utils import run_bass_kernel_spmd as _run

    nc = _bacc.Bacc("TRN2", target_bir_lowering=False, num_devices=1)
    given = {name: _np.ascontiguousarray(inputs[name]) for name in _INS}
    given.update(shapes=shape_constants(), onehot=t5_bucket_onehot(), alibi=alibi_band())
    arrays, args = {}, {}
    for name, v in given.items():
        arrays[f"in_{name}_dram"] = v
        args[name] = nc.dram_tensor(f"in_{name}_dram", v.shape, _mybir.dt.from_np(v.dtype), kind="ExternalInput").ap()
    out = nc.dram_tensor("out_0_dram", (1, TOK, D), F32, kind="ExternalOutput").ap()
    block_kernel(nc, args, out)
    r = _run(nc, [arrays], core_ids=[0])
    return r.results[0]["out_0_dram"]
```

```python
import numpy as np
import concourse.bass as bass
from concourse import mybir
from contextlib import ExitStack

F32 = mybir.dt.float32
F32R = mybir.dt.float32r
I32 = mybir.dt.int32
ALU = mybir.AluOpType
ACT = mybir.ActivationFunctionType
AX = mybir.AxisListType

P = 128
TOK = 512
NBLK = TOK // P
D = 1024
KT = D // P
CW = 256
FF = 4096
HID = FF // P // 2
EPS = 1e-6

QA, KA, VA, GA, ZA, QS, KS, WIN_COLS = 0, 256, 512, 1024, 1536, 1568, 2080, 2336
AQ, AKV, AGA, AU, AGB, AIN_COLS = 0, 512, 768, 1280, 1792, 2304
GATE_RANK = 16
GLA_C = 64
NCH = TOK // GLA_C
STEPS = NBLK * 4
GATE_NORM = 16.0
QSCALE = 0.125
BAND1 = 3 * P
BAND2 = 2 * P
LGW = BAND1 + 1
POOLW = (2, 4, 8, 16)
UPAD = 16
TAPS = 31
CPAD = TAPS - 1
DVE_TAPS = 18
ACT_TAPS = TAPS - DVE_TAPS
ADDS = ACT_TAPS - 1
TURN_TILES, TURN_CHUNKS = 4, 6
GATE_AT = (2, 5)
TURN_WORK = (((0, 0), (9, 1)), ((3, 2), (12, 3)), ((12, 4),), ((9, 5),))
TURN_AB = {0: 0, 1: 1, 3: 2, 4: 3}

V_PRE1, V_POST1, V_PREM, V_POSTM, V_PRE2A, V_POST2A, V_PRE2B, V_POST2B = [8 * i for i in range(8)]
V_DWB, V_LNG, V_LNB = 64, 72, 80
V_PSC, V_GN, V_BF, V_BB, V_N = 88, 92, 93, 95, 97

C_WIN, C_WOUT, C_UP0, C_DN0, C_UP1, C_DN1 = 0, 10, 14, 22, 30, 38
C_AIN, C_ABOUT, C_CAB, C_COUT, C_END = 46, 55, 59, 71, 75
E_WOUT, E_UP0, E_DN0, E_UP1, E_DN1 = 19, 27, 43, 51, 67
E_AIN, E_ABOUT, E_CAB, E_COUT = 75, 93, 101, 125

SLACK = {}


def t5_bucket_onehot():
    rel = np.arange(-255, 256)
    nb, max_exact = 16, 8
    n = np.abs(rel)
    large = max_exact + (np.log(np.maximum(n, 1).astype(np.float32) / max_exact)
                         / np.log(128 / max_exact) * (nb - max_exact)).astype(np.int32)
    bucket = (rel > 0) * nb + np.where(n < max_exact, n, np.minimum(large, nb - 1))
    hot = np.zeros((33, 512), np.float32)
    seen = n <= 128
    hot[bucket[seen], np.arange(511)[seen]] = 1.0
    hot[32, :511] = ~seen
    return hot


def shape_constants():
    i = np.arange(P)
    same = (i[:, None] // GLA_C) == (i[None, :] // GLA_C)
    fwd = same & (i[:, None] <= i[None, :])
    bwd = same & (i[:, None] >= i[None, :])
    restart = np.broadcast_to((np.arange(TOK) % GLA_C != 0), (P, TOK))
    t = np.arange(16)
    cnt = np.concatenate([w / np.minimum(t + 1, w) for w in POOLW])
    return np.concatenate([np.eye(P), np.ones((P, P)), fwd, bwd, restart,
                           np.broadcast_to(cnt, (P, 64)), np.eye(P)[::-1]], axis=1).astype(np.float32)


def alibi_band():
    slopes = np.exp2(-8.0 * np.arange(1, 9, dtype=np.float32) / 8).astype(np.float32)
    dist = (np.arange(P)[:, None] + P - np.arange(BAND2)[None, :]).astype(np.float32)
    bias = -slopes[None, :, None] * dist[:, None, :]
    return np.where(((dist >= 0) & (dist < 128))[:, None, :], bias, np.float32(-1e30)).astype(np.float32)


MIX1_LOADS, MIX2_LOADS, VEC_LOADS = 5, 4, 15


class Chain:

    def __init__(self, eng, sem):
        self.eng, self.sem, self.n, self.reg, self.per = eng, sem, 0, None, 0

    def link(self, ins):
        self.n += 1
        ins.then_inc(self.sem, 1)
        self.eng.wait_ge(self.sem, self.n if self.reg is None else self.reg * self.per + self.n)

    def enter(self, reg, per):
        self.reg, self.per, self.start = reg, per, self.n

    def leave(self, trips):
        assert self.n - self.start == self.per, (self.n - self.start, self.per)
        self.n, self.reg = self.start + trips * self.per, None


def block_kernel(nc, a, out):
    ctx = ExitStack()
    with ctx:
        top = [(nc.sbuf_base + 31) // 32 * 32]

        def at(name, shape, offset, dt=F32):
            return nc.alloc_sbuf_tensor_at(name, shape, dt, offset=offset)

        def sb(name, shape, dt=F32):
            size = 4 * int(np.prod(shape[1:]))
            t = at(name, shape, top[0], dt)
            top[0] += (size + 31) // 32 * 32
            return t

        def sem(name):
            return ctx.enter_context(nc.semaphore(name))

        raw = sb("raw", [P, 2, KT, CW])
        w_hi = sb("w_hi", [P, 2, KT, CW], F32R)
        w_lo = sb("w_lo", [P, 2, KT, CW], F32R)
        resid = sb("resid", [P, KT, TOK])
        act_hi = sb("act_hi", [P, KT, TOK], F32R)
        act_lo = sb("act_lo", [P, KT, TOK], F32R)
        R = sb("R", [P, TOK])
        sq = sb("sq", [P, 2, TOK])
        sq_sum = sb("sq_sum", [P, TOK])
        ident_ones = sb("ident_ones", [P, 2 * P])
        ident, ones = ident_ones[:, 0:P], ident_ones[:, P:2 * P]
        vec = sb("vec", [P, V_N])
        eps = sb("eps", [P, 1])
        arena = top[0]

        def arena_alloc(start):
            at_ = [start]

            def take(name, shape, dt=F32):
                t = at(name, shape, at_[0], dt)
                at_[0] += (4 * int(np.prod(shape[1:])) + 31) // 32 * 32
                SLACK[name] = nc.sbuf_usable_end - at_[0]
                return t
            take.pos = at_
            return take

        m1 = arena_alloc(arena)
        o1 = m1("o1", [P, KT, TOK])
        qa = m1("qa", [P, 2, TOK])
        ka = m1("ka", [P, 2, TOK])
        va_tok = m1("va_tok", [P, NBLK, 512])
        ga = m1("ga", [P, 4, TOK])
        masks = m1("masks", [P, 2, P])
        restart = m1("restart", [P, TOK])
        zz = m1("zz", [32, TOK])
        gate_w = m1("gate_w", [32, 2, 256])
        decay = m1("decay", [P, 2, 2, NCH])
        late = m1.pos[0]
        sA = arena_alloc(late)
        bias1 = sA("bias1", [P, 8, BAND1])
        qs1 = sA("qs1", [P, 4, TOK])
        k1 = sA("k1", [P, TOK])
        k1x = sA("k1x", [P, TOK])
        v1 = sA("v1", [P, TOK])
        v1_tok = sA("v1_tok", [P, NBLK, P])
        lg1 = sA("lg1", [P, 2, 2, LGW])
        pT1 = sA("pT1", [P, 3 * 2 * P])
        sm1 = sA("sm1", [P, 2, 2, 4])
        oq1 = sA("oq1", [P, 4, P])
        sink1 = sA("sink1", [P, 8])
        vaf = sA("vaf", [P, 2, TOK])
        qdec_f = sA("qdec_f", [P, 2, TOK])
        kint_f = sA("kint_f", [P, 2, TOK])
        eb = sA("eb", [P, TOK])
        gx, gl, bb = sq[:, 0, :], sq[:, 1, :], sq_sum
        gA = arena_alloc(late)
        S = gA("S", [P, 2, 2, NCH, P])
        Am = gA("Am", [P, 2, 2, TOK])
        hankel = at("hankel", [P, 8, BAND1], arena + 4 * (KT + 4) * TOK)
        flip = at("flip", [P, P], arena + 4 * (KT + 4) * TOK + 4 * 8 * BAND1)
        x_tok = at("x_tok", [P, NBLK, D], arena)
        relw = at("relw", [33, 8], arena + 4 * NBLK * D)
        hot = at("hot", [33, 512], arena + 4 * NBLK * D + 32)
        relF = at("relF", [8, 512], arena + 4 * NBLK * D + 32 + 2048)
        vec_rows = at("vec_rows", [V_N, P], arena + 4 * NBLK * D + 32 + 4096)
        mA = arena_alloc(arena)
        y = mA("y", [P, KT, TOK])
        hid_hi = mA("hid_hi", [P, HID, TOK], F32R)
        hid_lo = mA("hid_lo", [P, HID, TOK], F32R)
        zt = mA("zt", [P, 2, TOK])
        ty = mA("ty", [P, 2, TOK])
        zq = sq
        eA = arena_alloc(arena + 4 * KT * TOK)
        o2 = eA("o2", [P, KT, TOK])
        q2 = eA("q2", [P, 4, TOK])
        k2 = eA("k2", [P, TOK])
        k2x = eA("k2x", [P, TOK])
        v2 = eA("v2", [P, TOK])
        v2_tok = eA("v2_tok", [P, NBLK, P])
        bias2 = eA("bias2", [P, 8, BAND2])
        lg2 = eA("lg2", [P, 2, 2, BAND2 + 1])
        pT2 = eA("pT2", [P, 2 * 2 * P])
        sm2 = eA("sm2", [P, 2, 2, 4])
        oq2 = eA("oq2", [P, 4, P])
        sink2 = eA("sink2", [P, 8])
        ga2 = eA("ga2", [P, 4, TOK])
        gb2 = at("gb2", [P, 4, TOK], arena + 4 * 2 * KT * TOK)
        uu = eA("uu", [P, 4, UPAD + TOK])
        pw = eA("pw", [P, 4, P])
        wsum = eA("wsum", [P, 2, UPAD + TOK])
        pooled = eA("pooled", [P, 4, TOK])
        ty_e = at("ty_e", [P, 2, TOK], eA.pos[0])
        wcnt = at("wcnt", [P, 4, 16], eA.pos[0] + 4096)
        cA = arena_alloc(arena + 4 * KT * TOK)
        conv = cA("conv", [P, KT, TOK])
        gate = cA("gate", [P, KT, TOK])
        glu = cA("glu", [P, 2, CPAD + TOK])
        ab = cA("ab", [P, 2, TOK])
        taps = cA("taps", [P, KT, TAPS])
        tapw = cA("tapw", [P, TURN_TILES, TAPS + 1])
        prod = cA("prod", [P, 4, TOK])
        pacc = cA("pacc", [P, TOK])
        vacc = cA("vacc", [P, 2, TOK])
        mu = cA("mu", [P, TOK])
        yc = cA("yc", [P, 2, TOK])
        ty_c = cA("ty_c", [P, 2, TOK])
        tap_rows = at("tap_rows", [TAPS, D], cA.pos[0])
        o_tok = at("o_tok", [P, 2, 512], arena + 4 * KT * TOK)

        acc = ctx.enter_context(nc.psum_tensor("acc", [P, 4, 512], F32))
        psT = ctx.enter_context(nc.psum_tensor("psT", [P, 2, 512], F32))
        ps6 = ctx.enter_context(nc.psum_tensor("ps6", [P, 512], F32))
        ps7 = ctx.enter_context(nc.psum_tensor("ps7", [P, 512], F32))
        psTf = psT[:, :, :].rearrange("p a b -> p (a b)")

        relF_dram = nc.dram_tensor("relF_dram", [8, 512], F32, kind="Internal").ap()

        raw_ready = [sem("raw_ready0"), sem("raw_ready1")]
        hi_done = sem("hi_done")
        lo_done = sem("lo_done")
        tile_done = [sem("tile_done0"), sem("tile_done1")]
        evac_done = sem("evac_done")
        x_in = sem("x_in")
        vec_in = sem("vec_in")
        vec_ps = sem("vec_ps")
        vec_done = sem("vec_done")
        taps_ps = sem("taps_ps")
        taps_done = sem("taps_done")
        const_in = sem("const_in")
        rel_in = sem("rel_in")
        gatew_set = sem("gatew_set")
        relf_ps = sem("relf_ps")
        relf_sb = sem("relf_sb")
        relf_out = sem("relf_out")
        bias1_in = sem("bias1_in")
        bias1_ps = sem("bias1_ps")
        bias1_done = sem("bias1_done")
        mix1_in = sem("mix1_in")
        xT_done = sem("xT_done")
        resid_done = sem("resid_done")
        act_hi_done = sem("act_hi_done")
        act_lo_done = sem("act_lo_done")
        sq_done = sem("sq_done")
        sqsum_done = sem("sqsum_done")
        rsum_done = sem("rsum_done")
        r_done = sem("r_done")
        ty_done = sem("ty_done")
        eps_set = sem("eps_set")
        dve_step = sem("dve_step")
        act_step = sem("act_step")
        pool_step = sem("pool_step")
        kx_done = sem("kx_done")
        vT_done = sem("vT_done")
        vtok_done = sem("vtok_done")
        sink_set = sem("sink_set")
        qk_done = sem("qk_done")
        logits_done = sem("logits_done")
        negmax_done = sem("negmax_done")
        exp_done = sem("exp_done")
        rden_done = sem("rden_done")
        pT_done = sem("pT_done")
        pTs_done = sem("pTs_done")
        pv_done = sem("pv_done")
        oq_done = sem("oq_done")
        oT_done = sem("oT_done")
        o_done = sem("o_done")
        vaT_done = sem("vaT_done")
        vatok_done = sem("vatok_done")
        gate_ps = sem("gate_ps")
        gx_done = sem("gx_done")
        ln_done = sem("ln_done")
        ls_done = sem("ls_done")
        bb_done = sem("bb_done")
        eb_done = sem("eb_done")
        enb_done = sem("enb_done")
        qdec_done = sem("qdec_done")
        kint_done = sem("kint_done")
        dk_done = sem("dk_done")
        ek_done = sem("ek_done")
        ks_done = sem("ks_done")
        kT_done = sem("kT_done")
        kst_done = sem("kst_done")
        decay_done = sem("decay_done")
        dS_done = sem("dS_done")
        S_done = sem("S_done")
        A_done = sem("A_done")
        Am_set = sem("Am_set")
        Am_done = sem("Am_done")
        og_done = sem("og_done")
        og_out = sem("og_out")
        ogsq_done = sem("ogsq_done")
        ogsum_done = sem("ogsum_done")
        rr_done = sem("rr_done")
        on_done = sem("on_done")
        silu_done = sem("silu_done")
        og_gated = sem("og_gated")
        zt_done = sem("zt_done")
        zq_done = sem("zq_done")
        hhi_done = sem("hhi_done")
        hlo_done = sem("hlo_done")
        mix2_in = sem("mix2_in")
        upad_set = sem("upad_set")
        pooled_done = sem("pooled_done")
        wsum_done = sem("wsum_done")
        yb_ps = sem("yb_ps")
        o2_done = sem("o2_done")
        ob_done = sem("ob_done")
        silu2_done = sem("silu2_done")
        taps_in = sem("taps_in")
        sig_done = sem("sig_done")
        glu_done = sem("glu_done")
        tapw_done = sem("tapw_done")
        prod_done = sem("prod_done")
        pacc_step = sem("pacc_step")
        pacc_done = sem("pacc_done")
        vacc_step = sem("vacc_step")
        conv_step = sem("conv_step")
        musum_done = sem("musum_done")
        mu_done = sem("mu_done")
        cen_done = sem("cen_done")
        cn_done = sem("cn_done")
        csilu_done = sem("csilu_done")
        gsilu_done = sem("gsilu_done")
        yc_done = sem("yc_done")
        fT_done = sem("fT_done")
        fo_done = sem("fo_done")
        out_done = [sem("out_done0"), sem("out_done1")]

        block = ctx.enter_context(nc.Block())

        def qdec(d, t):
            return (qdec_f, qa)[d][:, t, :]

        def kint(d, t):
            return (kint_f, ka)[d][:, t, :]

        def kst(d, t):
            return o1[:, 2 * t + d, :].rearrange("p (b n) -> p b n", b=NBLK)

        def attention_unit(k, work):
            steps = [("qk", k)] if k < STEPS else []
            steps += [("transpose", k - 1)] if 1 <= k <= STEPS else []
            steps += [("softmax", k)] if k < STEPS else []
            steps += [("turn", (k - 2) // 4)] if k >= 5 and k % 4 == 1 else []
            return steps + work + ([("pv", k - 1)] if 1 <= k <= STEPS else [])

        def half_tiles(c):
            return [("tile", c, j, h) for j in range(2) for h in range(2)]

        def mixer1_steps():
            steps = []
            for c in (0, 1, 2):
                steps += [("split", c + 1), ("tile", c, 0), ("tile", c, 1)]
            steps += [("keys_values", 0), ("split", 4), ("tile", 3, 1)]
            k = 0
            for c in (4, 5, 6, 7, 8):
                for m, half in enumerate(half_tiles(c)[:2 if c == 8 else 4]):
                    work = [half]
                    if m == 0:
                        work.insert(0, ("split_hi", c + 1))
                    if m == 1:
                        work.insert(0, ("split_lo", c + 1))
                    if c in (6, 7) and m % 2:
                        work.append(("gla_values", 2 * (c - 6) + m // 2))
                    if 4 <= k <= 16:
                        if k >= 7 and k % 3 == 1:
                            work.append(("gla_keys", (k - 7) // 3))
                        if k <= 15:
                            work.append((("gla_gate", "gla_decay", "gla_scaled")[(k - 4) % 3], (k - 4) // 3))
                    steps += attention_unit(k, work)
                    k += 1
            rest = half_tiles(8)[2:] + half_tiles(9)
            steps += [("gla_dS", 0), rest[0], ("split_hi", 10), rest[1], ("split_lo", 10), ("gla_dS", 1), rest[2],
                      ("gla_A", 0), rest[3], ("gla_A", 1), ("gla_out", 0), rest[4],
                      ("gla_A", 2), ("gla_out", 1), ("gla_sum", 0), rest[5],
                      ("gla_A", 3), ("gla_out", 2), ("gla_sum", 1), ("attention_halves", 0),
                      ("gla_out", 3), ("gla_sum", 2)]
            return steps

        def mixer2_steps():
            steps = []
            for c in (46, 47, 48):
                steps += [("split", c + 1), ("tile", c, 0), ("tile", c, 1)]
            steps += [("keys_values", 1)]
            k = 0
            for c in (49, 50, 51, 52, 53):
                for m, half in enumerate(half_tiles(c)):
                    work = [half]
                    if m == 0:
                        work.insert(0, ("split_hi", c + 1))
                    if m == 1:
                        work.insert(0, ("split_lo", c + 1))
                    if c in (51, 52) and m % 2:
                        work.append(("pool_window", 2 * (c - 51) + m // 2))
                    steps += attention_unit(k, work) if k < STEPS + 2 else work
                    k += 1
            steps += [("attention_gate", 0)]
            steps += [("split", 55), ("tile", 54, 0), ("tile", 54, 1), ("pool_out", 0)]
            return steps

        def window(layer, n):
            kbs = [b for b in (range(n - 1, n + 2) if layer == 0 else range(n - 1, n + 1)) if 0 <= b < NBLK]
            return kbs, (kbs[0] - (n - 1)) * P

        LG, PT, SM, SINK, BIAS = (lg1, lg2), (pT1, pT2), (sm1, sm2), (sink1, sink2), (bias1, bias2)
        OQ = (oq1, oq2)
        QH, KH, KX, VT, VTOK, OO = (qs1, q2), (k1, k2), (k1x, k2x), (v1, v2), (v1_tok, v2_tok), (o1, o2)

        def o_tile(layer, hp):
            return (4 if layer == 0 else 0) + hp

        STEPS_OF = (mixer1_steps(), mixer2_steps())

        def before(layer, at, what):
            return sum(step[0] == what for step in STEPS_OF[layer][:at])

        def mixer_tile(c, j):
            if c < C_WOUT:
                e = 2 * c + j if c < 3 else (6 if c == 3 else 2 * c - 1 + j)
                return e, j if c != 3 else 0
            return E_AIN + 2 * (c - C_AIN) + j, j

        @block.sync
        def _(sp):
            for b in range(NBLK):
                sp.dma_start(x_tok[:, b, :], a["x"][0, b * P:(b + 1) * P, :]).then_inc(x_in, 16)

            def wait_slot(c):
                if isinstance(c, int) and c < 2:
                    return
                sp.wait_ge(lo_done, c - 1)

            def load(slot, w, n0, rows0=0, width=CW):
                rows = w[rows0:rows0 + D, :].rearrange("(k p) n -> p k n", p=P)
                for kk in (slice(0, KT // 2), slice(KT // 2, KT)):
                    sp.dma_start(raw[:, slot, kk, 0:width], rows[:, kk, bass.ds(n0, width)])\
                      .then_inc(raw_ready[slot], 16)

            def load_plain(w, c0, n, n0=0):
                with sp.Fori(0, n // 2) as i:
                    for s in range(2):
                        wait_slot(i * 2 + (c0 + s))
                        load((c0 + s) % 2, w, i * (2 * CW) + (n0 + s * CW))

            w_in, w_out, w_up, w_down = a["w_in"][0], a["w_out"][0], a["w_up"][0], a["w_down"][0]
            for c, n0 in enumerate((QS, QS + CW, KS, ZA, QA, KA, VA, VA + CW, GA, GA + CW)):
                wait_slot(c)
                load(c % 2, w_in, n0, 0, P if n0 == ZA else CW)
            load_plain(w_out, C_WOUT, 4)
            for half in range(2):
                cu, cd = (C_UP0, C_DN0) if half == 0 else (C_UP1, C_DN1)
                load_plain(w_up, cu, 8, half * FF // 2)
                with sp.Fori(0, 4) as i:
                    for s in range(2):
                        wait_slot(i * 2 + (cd + s))
                        load(s, w_down, i * CW, half * FF // 2 + s * D)
            for i in range(9):
                wait_slot(C_AIN + i)
                load((C_AIN + i) % 2, a["a_w_in_2"][0], i * CW)
            load_plain(a["ab_w_out_2"][0], C_ABOUT, 4)
            c_w_in = a["c_w_in_2"][0]
            ab_cols = c_w_in.rearrange("(k p) n -> p k n", p=P)
            with sp.Fori(0, 2) as i:
                for s in range(TURN_CHUNKS):
                    slot = (C_CAB + s) % 2
                    wait_slot(i * TURN_CHUNKS + (C_CAB + s))
                    if s in GATE_AT:
                        load(slot, c_w_in, i * (2 * CW) + (2 * D + CW * GATE_AT.index(s)))
                        continue
                    for g in range(2):
                        sp.dma_start(raw[:, slot, :, g * P:(g + 1) * P],
                                     ab_cols[:, :, bass.ds(i * (TURN_TILES * P) + (g * D + TURN_AB[s] * P), P)])\
                          .then_inc(raw_ready[slot], 16)
            load_plain(a["c_w_out_2"][0], C_COUT, 4)
            for f in range(2 * NBLK):
                sp.wait_ge(fo_done, f + 1)
                sp.dma_start(out[0, (f // 2) * P:(f // 2 + 1) * P, (f % 2) * 512:(f % 2 + 1) * 512],
                             o_tok[:, f % 2, :]).then_inc(out_done[f % 2], 16)
            for s in range(2):
                sp.wait_ge(out_done[s], 16 * NBLK)

        @block.tensor
        def _(pe):
            def mm3(dst, hi, lo, x_hi, x_lo, first, last):
                pe.matmul(dst, hi, x_hi, start=first, stop=False)
                pe.matmul(dst, hi, x_lo, start=False, stop=False)
                return pe.matmul(dst, lo, x_hi, start=False, stop=last)

            def w_tiles(slot, k, j):
                return w_hi[:, slot, k, j * P:(j + 1) * P], w_lo[:, slot, k, j * P:(j + 1) * P]

            def project(dst, slot, j):
                for k in range(KT):
                    last = mm3(dst, *w_tiles(slot, k, j), act_hi[:, k, :], act_lo[:, k, :], k == 0, k == KT - 1)
                last.then_inc(tile_done[j], 1)

            def project_pair(c, e, n, order=range(KT), between={}):
                pe.wait_ge(evac_done, e)
                pe.wait_ge(lo_done, c + 2)
                for i, k in enumerate(order):
                    if i in between:
                        between[i]()
                    pe.wait_ge(act_lo_done, 8 * n + i + 1)
                    for s in range(2):
                        for j in range(2):
                            last = mm3(acc[:, 2 * s + j, :], *w_tiles((c + s) % 2, k, j),
                                       act_hi[:, k, :], act_lo[:, k, :], i == 0, i == KT - 1)
                            if i == KT - 1:
                                last.then_inc(tile_done[j], 1)

            def project_chunks(c, e, order=range(KT)):
                for s in range(2):
                    pe.wait_ge(lo_done, c + (s + 1))
                    for j in range(2):
                        pe.wait_ge(evac_done, e + (2 * s + j - 3))
                        for i, k in enumerate(order):
                            last = mm3(acc[:, 2 * s + j, :], *w_tiles((c_par + s) % 2, k, j),
                                       act_hi[:, k, :], act_lo[:, k, :], i == 0, i == KT - 1)
                        last.then_inc(tile_done[j], 1)

            pe.wait_ge(const_in, 16)
            pe.wait_ge(vec_in, 16 * VEC_LOADS)
            pe.transpose(ps7[:, 0:V_N], vec_rows[:, :], ident[0:V_N, 0:V_N]).then_inc(vec_ps, 1)
            for k in range(KT):
                if k == 0:
                    pe.wait_ge(x_in, 16 * NBLK)
                if k >= 4:
                    pe.wait_ge(resid_done, k - 3)
                for b in range(NBLK):
                    last = pe.transpose(acc[:, k % 4, b * P:(b + 1) * P], x_tok[:, b, k * P:(k + 1) * P], ident[:, :])
                last.then_inc(xT_done, 1)
            pe.wait_ge(rel_in, 2 * 16)
            pe.wait_ge(gatew_set, 1)
            pe.matmul(ps6[0:8, :], relw[:, :], hot[:, :], start=True, stop=True).then_inc(relf_ps, 1)

            def token_sums(n):
                pe.wait_ge(sqsum_done, 8 * (n + 1))
                pe.matmul(ps7[:, :], ones[:, :], sq_sum[:, :], start=True, stop=True).then_inc(rsum_done, 1)

            last_in_bank = {}

            def mixer_tile_pe(c, j, half=None):
                e, bank = mixer_tile(c, j)
                ks = range(KT) if half is None else range(4 * half, 4 * half + 4)
                if half == 1:
                    for k in ks:
                        last = mm3(acc[:, bank, :], *w_tiles(c % 2, k, j), act_hi[:, k, :], act_lo[:, k, :],
                                   False, k == KT - 1)
                    last.then_inc(tile_done[j], 1)
                    return
                if j == 0 or c == 3:
                    pe.wait_ge(lo_done, c + 1)
                if c == C_AIN and j == 0:
                    last_in_bank.clear()
                if bank in last_in_bank:
                    pe.wait_ge(evac_done, last_in_bank[bank] + 1)
                elif c == C_AIN:
                    pe.wait_ge(evac_done, E_AIN)
                elif c == 0:
                    pe.wait_ge(resid_done, KT)
                last_in_bank[bank] = e
                n = 0 if c < C_WOUT else 3
                for k in ks:
                    if c in (0, C_AIN) and j == 0:
                        pe.wait_ge(act_lo_done, 8 * n + k + 1)
                    if c == 3:
                        wh, wl = w_hi[:, 1, k, 0:P], w_lo[:, 1, k, 0:P]
                    else:
                        wh, wl = w_tiles(c % 2, k, j)
                    last = mm3(acc[:, bank, :], wh, wl, act_hi[:, k, :], act_lo[:, k, :], k == 0, k == KT - 1)
                    if c == 3 and k == KT - 2:
                        last.then_inc(tile_done[0], 1)
                if half is None:
                    last.then_inc(tile_done[j], 1)
                if c == 0 and j == 0:
                    token_sums(0)
                if c == C_AIN and j == 0:
                    token_sums(4)

            def gla_sum(h):
                pe.wait_ge(ogsq_done, h + 1)
                if h >= 2:
                    pe.wait_ge(rr_done, h - 1)
                elif h == 0:
                    pe.wait_ge(kst_done, 4)
                else:
                    pe.wait_ge(o_done, 4)
                pe.matmul((ps6, ps7)[h % 2][:, :], ones[:, :], sq[:, h % 2, :], start=True, stop=True)\
                  .then_inc(ogsum_done, 1)

            def ps6_free(layer, at):
                pvs, keys = 16 * layer + before(layer, at, "pv"), before(layer, at, "gla_keys")
                if pvs:
                    pe.wait_ge(oq_done, pvs)
                if keys:
                    pe.wait_ge(kst_done, keys)

            def ps7_free(layer, at):
                turns, values = 4 * layer + before(layer, at, "turn"), before(layer, at, "gla_values")
                gates = before(layer, at, "gla_gate")
                pe.wait_ge(vtok_done, layer + 1)
                if turns:
                    pe.wait_ge(o_done, turns)
                if values:
                    pe.wait_ge(vatok_done, values)
                if gates:
                    pe.wait_ge(gx_done, gates)

            def mixer_step_pe(layer, step, at):
                what, i = step[0], step[1]
                if what == "tile":
                    mixer_tile_pe(*step[1:])
                elif what == "keys_values":
                    if layer == 0:
                        pe.wait_ge(bias1_in, 2 * 16)
                        for h in range(8):
                            if h >= 2:
                                pe.wait_ge(bias1_done, h - 1)
                            pe.matmul(psT[:, h % 2, 0:BAND1], flip[:, :], hankel[:, h, :], start=True, stop=True)\
                              .then_inc(bias1_ps, 1)
                    pe.wait_ge(evac_done, 6 if layer == 0 else E_AIN + 6)
                    pe.wait_ge(r_done, 1 if layer == 0 else 5)
                    for b in range(NBLK):
                        last = pe.transpose(ps7[:, b * P:(b + 1) * P], VT[layer][:, b * P:(b + 1) * P], ident[:, :])
                    last.then_inc(vT_done, 1)
                elif what == "qk":
                    n, hp, k = i // 4, i % 4, 16 * layer + i
                    kbs, _ = window(layer, n)
                    if i == 0:
                        pe.wait_ge(kx_done, 2 * (layer + 1))
                    if k >= 1:
                        pe.wait_ge(logits_done, k)
                    for j in range(2):
                        keys = KH[layer] if hp // 2 == j else KX[layer]
                        h64 = slice(64 * j, 64 * j + 64)
                        last = pe.matmul(acc[:, 2 + j, 0:len(kbs) * P], QH[layer][h64, hp, n * P:(n + 1) * P],
                                         keys[h64, kbs[0] * P:(kbs[-1] + 1) * P], start=True, stop=True)
                    last.then_inc(qk_done, 1)
                elif what == "transpose":
                    n, k = i // 4, 16 * layer + i
                    kbs, _ = window(layer, n)
                    pe.wait_ge(exp_done, 2 * (k + 1))
                    if k >= 1:
                        pe.wait_ge(pTs_done, k)
                    for b in range(len(kbs)):
                        for j in range(2):
                            last = pe.transpose(psTf[:, (2 * b + j) * P:(2 * b + j + 1) * P],
                                                LG[layer][:, i % 2, j, 1 + b * P:1 + (b + 1) * P], ident[:, :])
                    last.then_inc(pT_done, 1)
                elif what == "pv":
                    n, hp, k = i // 4, i % 4, 16 * layer + i
                    g = hp // 2
                    kbs, _ = window(layer, n)
                    pe.wait_ge(pTs_done, k + 1)
                    if i == 0:
                        pe.wait_ge(vtok_done, layer + 1)
                    ps6_free(layer, at)
                    if k == 0:
                        pe.wait_ge(relf_sb, 1)
                    for j in range(2):
                        for b, kb in enumerate(kbs):
                            last = pe.matmul(ps6[:, 64 * j:64 * j + 64],
                                             PT[layer][:, (2 * b + j) * P:(2 * b + j + 1) * P],
                                             VTOK[layer][:, kb, 64 * g:64 * g + 64],
                                             start=b == 0, stop=b == len(kbs) - 1)
                    last.then_inc(pv_done, 1)
                elif what == "turn":
                    pe.wait_ge(oq_done, 16 * layer + 4 * (i + 1))
                    ps7_free(layer, at)
                    for hp in range(4):
                        last = pe.transpose(ps7[:, hp * P:(hp + 1) * P], OQ[layer][:, hp, :], ident[:, :])
                    last.then_inc(oT_done, 1)
                elif what == "gla_values":
                    pe.wait_ge(evac_done, mixer_tile(6 + i // 2, i % 2)[0] + 1)
                    ps7_free(layer, at)
                    for b in range(NBLK):
                        last = pe.transpose(ps7[:, b * P:(b + 1) * P], vaf[:, i % 2, b * P:(b + 1) * P], ident[:, :])
                    last.then_inc(vaT_done, 1)
                elif what == "gla_gate":
                    d, t = i % 2, i // 2
                    if i == 0:
                        pe.wait_ge(mix1_in, 16 * MIX1_LOADS)
                        pe.wait_ge(evac_done, 7)
                    ps7_free(layer, at)
                    pe.matmul(ps7[:, :], gate_w[:, d, t * P:(t + 1) * P], zz[:, :], start=True, stop=True)\
                      .then_inc(gate_ps, 1)
                elif what == "gla_keys":
                    pe.wait_ge(ks_done, i + 1)
                    ps6_free(layer, at)
                    for b in range(NBLK):
                        last = pe.transpose(ps6[:, b * P:(b + 1) * P], bb[:, b * P:(b + 1) * P], ident[:, :])
                    last.then_inc(kT_done, 1)
                elif what == "gla_dS":
                    pe.wait_ge(kst_done, 4)
                    pe.wait_ge(vatok_done, 4)
                    pe.wait_ge(pTs_done, STEPS)
                    pe.wait_ge(logits_done, STEPS)
                    if i == 1:
                        pe.wait_ge(S_done, 14)
                    for d in range(2):
                        dst = acc[:, 2:4, :] if d == 0 else psT
                        for n in range(NCH):
                            if n == (NCH - 1 if d == 0 else 0):
                                continue
                            s64 = slice(64 * (n % 2), 64 * (n % 2) + 64)
                            for hh in range(2):
                                h = 2 * i + hh
                                last = pe.matmul(dst[64 * hh:64 * hh + 64, n % 2, (n // 2) * P:(n // 2 + 1) * P],
                                                 kst(d, i)[s64, n // 2, 64 * hh:64 * hh + 64],
                                                 va_tok[s64, n // 2, h * P:(h + 1) * P], start=True, stop=True)
                    last.then_inc(dS_done, 1)
                elif what == "gla_A":
                    t, h64 = i // 2, slice(64 * (i % 2), 64 * (i % 2) + 64)
                    pe.wait_ge(kint_done, 4)
                    pe.wait_ge(qdec_done, 4)
                    pe.wait_ge(S_done, 28)
                    for d in range(2):
                        if i >= 1:
                            pe.wait_ge(Am_done, 2 * (i - 1) + d + 1)
                        for m in range(NBLK):
                            mm = slice(m * P, (m + 1) * P)
                            last = pe.matmul(acc[:, 2 + d, mm], kint(d, t)[h64, mm], qdec(d, t)[h64, mm],
                                             start=True, stop=True)
                        last.then_inc(A_done, 1)
                elif what == "gla_out":
                    t, h64 = i // 2, slice(64 * (i % 2), 64 * (i % 2) + 64)
                    bank = i % 2
                    pe.wait_ge(Am_done, 2 * i + 2)
                    if i >= 2:
                        pe.wait_ge(og_out, i - 1)
                    for m in range(NBLK):
                        mm = slice(m * P, (m + 1) * P)
                        for d in range(2):
                            pe.matmul(psT[:, bank, mm], va_tok[:, m, i * P:(i + 1) * P], Am[:, i % 2, d, mm],
                                      start=m == 0 and d == 0, stop=False)
                    for n in range(NCH):
                        nn = slice(n * GLA_C, (n + 1) * GLA_C)
                        for d in range(2):
                            if n == (0 if d == 0 else NCH - 1):
                                continue
                            last = pe.matmul(psT[:, bank, nn], S[h64, t, d, n, :], qdec(d, t)[h64, nn],
                                             start=False, stop=n == NCH - 1)
                    last.then_inc(og_done, 1)
                elif what == "gla_sum":
                    gla_sum(i)
                elif what == "pool_out":
                    pe.wait_ge(mix2_in, 16 * MIX2_LOADS)
                    pe.wait_ge(o_done, 8)
                    pe.wait_ge(vtok_done, 2)
                    for g in range(4):
                        pe.wait_ge(pooled_done, g + 1)
                        dst = (ps6[:, :], ps7[:, :], psT[:, 0, :], psT[:, 1, :])[g]
                        pe.matmul(dst, pw[:, g, :], pooled[:, g, :], start=True, stop=True).then_inc(yb_ps, 1)

            for at, step in enumerate(STEPS_OF[0]):
                mixer_step_pe(0, step, at)
            order = (4, 5, 6, 7, 0, 1, 2, 3)
            c_par = 0
            pe.wait_ge(Am_done, 8)
            project_pair(C_WOUT, E_WOUT, 1, order, {1: lambda: gla_sum(3)})
            project_chunks(C_WOUT + 2, E_WOUT + 4, order)
            token_sums(1)
            project_pair(C_UP0, E_UP0, 2)
            for half in range(2):
                if half == 0:
                    token_sums(2)
                    with pe.Fori(0, 3) as i:
                        project_chunks(i * 2 + (C_UP0 + 2), i * 4 + (E_UP0 + 4))
                else:
                    with pe.Fori(0, 4) as i:
                        project_chunks(i * 2 + C_UP1, i * 4 + E_UP1)
                c0, e0 = (C_DN0, E_DN0) if half == 0 else (C_DN1, E_DN1)
                with pe.Fori(0, 2) as i:
                    for pair in range(2):
                        for kg in range(2):
                            pe.wait_ge(hlo_done, HID * half + 8 * (kg + 1))
                            pe.wait_ge(lo_done, i * 4 + (c0 + 2 * pair + kg + 1))
                            for j in range(2):
                                bank = 2 * pair + j
                                if kg == 0:
                                    pe.wait_ge(evac_done, i * 4 + (e0 + bank - 3))
                                for k in range(KT):
                                    last = mm3(acc[:, bank, :], *w_tiles(kg, k, j), hid_hi[:, 8 * kg + k, :],
                                               hid_lo[:, 8 * kg + k, :], kg == 0 and k == 0, kg == 1 and k == KT - 1)
                                last.then_inc(tile_done[j], 1)
            token_sums(3)
            for at, step in enumerate(STEPS_OF[1]):
                mixer_step_pe(1, step, at)
            c_par = C_ABOUT
            project_pair(C_ABOUT, E_ABOUT, 4)
            project_chunks(C_ABOUT + 2, E_ABOUT + 4)
            token_sums(5)
            c_par = C_CAB
            pe.wait_ge(taps_in, 16)
            for k in range(KT):
                last = pe.transpose(ps6[:, k * TAPS:(k + 1) * TAPS], tap_rows[:, k * P:(k + 1) * P],
                                    ident[0:TAPS, 0:TAPS])
            last.then_inc(taps_ps, 1)
            project_pair(C_CAB, E_CAB, 5)
            token_sums(6)
            with pe.Fori(0, TURN_CHUNKS - 1) as i:
                project_chunks(i * 2 + (C_CAB + 2), i * 4 + (E_CAB + 4))
            for k in range(KT):
                pe.wait_ge(conv_step, k + 2)
                last = pe.matmul(ps6[:, :], ones[:, :], conv[:, k, :], start=k == 0, stop=k == KT - 1)
            last.then_inc(musum_done, 1)
            for k in range(KT):
                pe.wait_ge(sq_done, 8 * 7 + k + 1)
                pe.matmul(ps7[:, :], ones[:, :], sq[:, k % 2, :], start=k == 0, stop=k == KT - 1)\
                  .then_inc(sqsum_done, 1)
            project_pair(C_COUT, E_COUT, 6)
            project_chunks(C_COUT + 2, E_COUT + 4)
            token_sums(8)
            for f in range(2 * NBLK):
                b, half = f // 2, f % 2
                pe.wait_ge(resid_done, 5 * KT if b else 4 * KT + 4 * (half + 1))
                if f >= 2:
                    pe.wait_ge(fo_done, f - 1)
                for k in range(4):
                    last = pe.transpose(psT[:, f % 2, k * P:(k + 1) * P],
                                        resid[:, 4 * half + k, b * P:(b + 1) * P], ident[:, :])
                last.then_inc(fT_done, 1)

        @block.gpsimd
        def _(pool):
            chain = Chain(pool, pool_step)
            pool.memset(eps[:, :], EPS).then_inc(eps_set, 1)
            pool.wait_ge(eps_set, 1)
            chain.link(pool.memset(relw[32:33, :], -1e30))
            pool.memset(gate_w[:, :, :], 0.0).then_inc(gatew_set, 1)
            pool.wait_ge(gatew_set, 1)

            def sum_squares(n, src=None):
                for k in range(KT):
                    pool.wait_ge(sq_done, 8 * n + k + 1)
                    if k == 0:
                        if n >= 1:
                            pool.wait_ge(rsum_done, min(n, 7))
                        pool.tensor_copy(sq_sum[:, :], sq[:, k % 2, :]).then_inc(sqsum_done, 1)
                    else:
                        pool.wait_ge(sqsum_done, 8 * n + k)
                        pool.tensor_tensor(sq_sum[:, :], sq_sum[:, :], sq[:, k % 2, :], ALU.add)\
                            .then_inc(sqsum_done, 1)

            def sink_columns(layer, i):
                k, hp = 16 * layer + i, i % 4
                if i == 0:
                    pool.wait_ge(*((mix1_in, 16 * MIX1_LOADS) if layer == 0 else (mix2_in, 16 * MIX2_LOADS)))
                if i >= 2:
                    pool.wait_ge(pT_done, k - 1)
                pool.tensor_copy(LG[layer][:, i % 2, :, 0], SINK[layer][:, 2 * hp:2 * hp + 2]).then_inc(sink_set, 1)

            def mixer_step_pool(layer, step):
                what, i = step[0], step[1]
                k = 16 * layer + i
                if what == "keys_values":
                    for m in range(2):
                        sink_columns(layer, m)
                elif what == "transpose":
                    if i + 2 < STEPS:
                        sink_columns(layer, i + 2)
                elif what == "gla_scaled":
                    d, t = i % 2, i // 2
                    pool.wait_ge(evac_done, 11)
                    pool.wait_ge(eb_done, i + 1)
                    if d == 0:
                        pool.wait_ge(enb_done, i + 1)
                        pool.tensor_tensor(kint(d, t), ka[:, t, :], gx[:, :], ALU.mult).then_inc(kint_done, 1)
                    pool.wait_ge(ek_done, i + 1)
                    pool.tensor_tensor(bb[:, :], ka[:, t, :], gl[:, :], ALU.mult).then_inc(ks_done, 1)
                    if d == 1:
                        pool.wait_ge(ks_done, i + 1)
                        pool.tensor_tensor(kint(d, t), ka[:, t, :], gx[:, :], ALU.mult).then_inc(kint_done, 1)
                elif what == "gla_dS" and i == 0:
                    pool.wait_ge(vtok_done, 1)
                    pool.wait_ge(pv_done, STEPS)
                    pool.memset(Am[:, :, :, :], 0.0).then_inc(Am_set, 1)
                elif what == "pool_window":
                    pool.wait_ge(evac_done, E_AIN + 2 * (5 + i // 2) + i % 2 + 1)
                    if i == 0:
                        pool.wait_ge(upad_set, 1)
                        pool.wait_ge(mix2_in, 16 * MIX2_LOADS)
                    else:
                        pool.wait_ge(pooled_done, i)
                    src = uu[:, i, :]
                    for m in range(i + 1):
                        sh, lo = 1 << m, (2 << m) - 1
                        dst = wsum[:, m % 2, :]
                        chain.link(pool.tensor_tensor(dst[:, lo:], src[:, lo:], src[:, lo - sh:UPAD + TOK - sh], ALU.add))
                        src = dst
                    pool.tensor_tensor(src[:, UPAD:UPAD + 16], src[:, UPAD:UPAD + 16], wcnt[:, i, :], ALU.mult)\
                        .then_inc(wsum_done, 1)

            sum_squares(0)
            for step in STEPS_OF[0]:
                mixer_step_pool(0, step)
            for n in (1, 2, 3, 4):
                sum_squares(n)
            pool.memset(uu[:, :, 0:UPAD], 0.0).then_inc(upad_set, 1)
            for step in STEPS_OF[1]:
                mixer_step_pool(1, step)
            sum_squares(5)
            pool.memset(glu[:, 0, 0:CPAD], 0.0).then_inc(glu_done, 1)
            pool.memset(glu[:, 1, 0:CPAD], 0.0).then_inc(pacc_step, ADDS)
            sum_squares(6)
            with pool.Fori(0, 2) as i:
                def gated(t):
                    pool.wait_ge(sig_done, i * TURN_TILES + (t + 1))
                    pool.wait_ge(conv_step, i * TURN_TILES + (max(t - 1, 0) + 1))
                    pool.tensor_tensor(glu[:, t % 2, CPAD:], ab[:, 0, :], ab[:, 1, :], ALU.mult).then_inc(glu_done, 1)

                for t in range(TURN_TILES):
                    work = [(x * ADDS // DVE_TAPS + 1, TURN_AB[s]) for x, s in TURN_WORK[t] if s in TURN_AB]
                    for m in range(1, ACT_TAPS):
                        for x, tile in work:
                            if m == x:
                                gated(tile)
                        g = ACT_TAPS * t + m
                        pool.wait_ge(prod_done, i * (TURN_TILES * ACT_TAPS) + (g + 2))
                        if m == 1:
                            pool.wait_ge(conv_step, i * TURN_TILES + (t + 1))
                            pool.tensor_tensor(pacc[:, :], prod[:, (g - 1) % 4, :], prod[:, g % 4, :], ALU.add)\
                                .then_inc(pacc_step, 1)
                        else:
                            pool.wait_ge(pacc_step, i * (TURN_TILES * ADDS) + (ADDS * (t + 1) + m - 1))
                            pool.tensor_tensor(pacc[:, :], pacc[:, :], prod[:, g % 4, :], ALU.add)\
                                .then_inc(pacc_step, 1)
            sum_squares(8)

        @block.scalar
        def _(act):
            chain = Chain(act, act_step)

            def col(v):
                return v.rearrange("(k p) -> k p", p=P)

            def exp_ln_tables():
                nc.scalar.preload_act_table_set("natural_log_exp_and_others")

            exp_ln_tables()
            act.dma_start(ident_ones[:, :], a["shapes"][:, 0:2 * P]).then_inc(const_in, 16)
            for off, name in ((V_PRE1, "norm_mix_pre"), (V_POST1, "norm_mix_post"), (V_PREM, "norm_mlp_pre"),
                              (V_POSTM, "norm_mlp_post"), (V_DWB, "c_dw_b_2"), (V_LNG, "c_ln_g_2"),
                              (V_LNB, "c_ln_b_2")):
                act.dma_start(vec_rows[off:off + KT, :], col(a[name][0])).then_inc(vec_in, 16)
            for layer, (pre, post) in enumerate(((V_PRE2A, V_POST2A), (V_PRE2B, V_POST2B))):
                act.dma_start(vec_rows[pre:pre + KT, :], col(a["pre_norm_2"][layer])).then_inc(vec_in, 16)
                act.dma_start(vec_rows[post:post + KT, :], col(a["post_norm_2"][layer])).then_inc(vec_in, 16)
            act.dma_start(vec_rows[V_PSC:V_PSC + 4, :], col(a["b_pool_scale_2"][0])).then_inc(vec_in, 16)
            act.dma_start(vec_rows[V_GN:V_GN + 1, :], col(a["gla_norm"][0])).then_inc(vec_in, 16)
            act.dma_start(vec_rows[V_BF:V_BF + 2, :], col(a["b_gate_fwd"][0])).then_inc(vec_in, 16)
            act.dma_start(vec_rows[V_BB:V_BB + 2, :], col(a["b_gate_bwd"][0])).then_inc(vec_in, 16)
            act.dma_start(relw[0:32, :], a["rel_bias"]).then_inc(rel_in, 16)
            act.dma_start(hot[:, :], a["onehot"]).then_inc(rel_in, 16)

            def split(c):
                slot = (c if isinstance(c, int) else c_par) % 2
                if isinstance(c, int):
                    act.wait_ge(raw_ready[slot], 32 * (c // 2 + 1))
                    if c >= 2:
                        act.wait_ge(tile_done[1], c - 1)
                else:
                    act.wait_ge(raw_ready[slot], c * 16 + 16 * (2 - slot))
                    act.wait_ge(tile_done[1], c - 1)
                if isinstance(c, int) and c == 3:
                    act.activation(w_hi[:, slot, :, 0:P], raw[:, slot, :, 0:P], ACT.Copy).then_inc(hi_done, 1)
                else:
                    act.activation(w_hi[:, slot, :, :], raw[:, slot, :, :], ACT.Copy).then_inc(hi_done, 1)

            def square(n, k, src):
                if 8 * n + k >= 2:
                    act.wait_ge(sqsum_done, 8 * n + k - 1)
                act.activation(sq[:, k % 2, :], src, ACT.Square).then_inc(sq_done, 1)

            def token_scale(n, src=None):
                if n == 7:
                    act.wait_ge(sqsum_done, 8 * (n + 1))
                else:
                    act.wait_ge(rsum_done, min(n, 7) + 1)
                chain.link(act.activation(R[:, :], ps7[:, :], ACT.Ln, bias=eps[:, 0:1], scale=1.0 / D))
                act.activation(R[:, :], R[:, :], ACT.Exp, scale=-0.5).then_inc(r_done, 1)

            def boundary(n, gain):
                for k in range(KT):
                    act.wait_ge(resid_done, 8 * n + k + 1)
                    act.activation(act_hi[:, k, :], resid[:, k, :], ACT.Copy, scale=vec[:, gain + k:gain + k + 1])\
                       .then_inc(act_hi_done, 1)
                    square((0, 2, 4, 6)[n], k, resid[:, k, :])

            def halves(tensor, order, wait):
                for k in order:
                    wait(act, k)
                    act.activation(act_hi[:, k, :], tensor[:, k, :], ACT.Copy).then_inc(act_hi_done, 1)

            def mixer_step_act(layer, step):
                what, i = step[0], step[1]
                k = 16 * layer + i
                if what in ("split", "split_hi"):
                    split(i)
                elif what == "keys_values":
                    for h in range(8 if layer == 0 else 0):
                        act.wait_ge(bias1_ps, h + 1)
                        act.activation(bias1[:, h, :], psT[:, h % 2, 0:BAND1], ACT.Copy).then_inc(bias1_done, 1)
                    act.wait_ge(evac_done, 6 if layer == 0 else E_AIN + 6)
                    act.activation(KX[layer][64:128, :], KH[layer][0:64, :], ACT.Copy).then_inc(kx_done, 1)
                    act.activation(KX[layer][0:64, :], KH[layer][64:128, :], ACT.Copy).then_inc(kx_done, 1)
                    act.wait_ge(vT_done, layer + 1)
                    act.activation(VTOK[layer][:, :, :], ps7[:, :].rearrange("p (b n) -> p b n", b=NBLK), ACT.Copy)\
                       .then_inc(vtok_done, 1)
                elif what == "softmax":
                    w = len(window(layer, i // 4)[0]) * P + 1
                    act.wait_ge(negmax_done, k + 1)
                    for j in range(2):
                        row = LG[layer][:, i % 2, j, 0:w]
                        act.activation(row, row, ACT.Exp, bias=SM[layer][:, i % 2, j, 1:2],
                                       accum_out=SM[layer][:, i % 2, j, 2:3]).then_inc(exp_done, 1)
                elif what == "transpose":
                    w = len(window(layer, i // 4)[0]) * 2 * P
                    act.wait_ge(pT_done, k + 1)
                    if k >= 1:
                        act.wait_ge(pv_done, k)
                    act.activation(PT[layer][:, 0:w], psTf[:, 0:w], ACT.Copy).then_inc(pTs_done, 1)
                elif what == "turn":
                    o0 = o_tile(layer, 0)
                    act.wait_ge(oT_done, 4 * layer + i + 1)
                    act.activation(OO[layer][:, o0:o0 + 4, i * P:(i + 1) * P],
                                   ps7[:, :].rearrange("p (h n) -> p h n", h=4), ACT.Copy).then_inc(o_done, 1)
                elif what == "gla_values":
                    act.wait_ge(vaT_done, i + 1)
                    act.activation(va_tok[:, :, i * P:(i + 1) * P], ps7[:, :].rearrange("p (b n) -> p b n", b=NBLK),
                                   ACT.Copy).then_inc(vatok_done, 1)
                elif what == "gla_gate":
                    d, t = i % 2, i // 2
                    act.wait_ge(gx_done, i + 1)
                    if i >= 1:
                        act.wait_ge(ks_done, i)
                    chain.link(act.activation(gl[:, :], gx[:, :], ACT.Abs))
                    chain.link(act.activation(gl[:, :], gl[:, :], ACT.Exp, scale=-1.0))
                    act.activation(gl[:, :], gl[:, :], ACT.Ln, bias=1.0).then_inc(ln_done, 1)
                elif what == "gla_decay":
                    act.wait_ge(bb_done, i + 1)
                    if i >= 1:
                        act.wait_ge(qdec_done, i)
                        act.wait_ge(decay_done, i)
                    act.activation(eb[:, :], bb[:, :], ACT.Exp, scale=1.0 / GATE_NORM).then_inc(eb_done, 1)
                    act.activation(gx[:, :], bb[:, :], ACT.Exp, scale=-1.0 / GATE_NORM).then_inc(enb_done, 1)
                    act.wait_ge(dk_done, i + 1)
                    act.activation(gl[:, :], gl[:, :], ACT.Exp, scale=1.0 / GATE_NORM).then_inc(ek_done, 1)
                elif what == "gla_keys":
                    act.wait_ge(kT_done, i + 1)
                    act.activation(kst(i % 2, i // 2), ps6[:, :].rearrange("p (b n) -> p b n", b=NBLK), ACT.Copy)\
                       .then_inc(kst_done, 1)
                elif what == "gla_out":
                    act.wait_ge(og_done, i + 1)
                    act.activation(o1[:, i, :], psT[:, i % 2, :], ACT.Copy).then_inc(og_out, 1)
                    act.wait_ge(og_out, i + 1)
                    if i >= 2:
                        act.wait_ge(ogsum_done, i - 1)
                    act.activation(sq[:, i % 2, :], o1[:, i, :], ACT.Square).then_inc(ogsq_done, 1)
                elif what == "gla_sum":
                    head_scale(i)
                elif what == "attention_halves":
                    split(11)
                    act.wait_ge(evac_done, E_WOUT)
                    halves(o1, (4, 5, 6, 7), lambda e, k: e.wait_ge(o_done, 4))
                elif what == "attention_gate":
                    act.wait_ge(evac_done, E_AIN + 10)
                    for h in range(4):
                        act.activation(ga2[:, h, :], ga2[:, h, :], ACT.Silu).then_inc(silu2_done, 1)
                elif what == "pool_out":
                    act.wait_ge(evac_done, E_ABOUT)
                    for h in range(4):
                        act.activation(gb2[:, h, :], gb2[:, h, :], ACT.Silu).then_inc(silu2_done, 1)
                    exp_ln_tables()
                    split(56)
                    halves(o2, range(KT), lambda e, k: e.wait_ge(ob_done, k + 1))

            def head_scale(h):
                rr = (bb, eb)[h % 2]
                act.wait_ge(ogsum_done, h + 1)
                if h >= 2:
                    act.wait_ge(on_done, h - 1)
                chain.link(act.activation(rr[:, :], (ps6, ps7)[h % 2][:, :], ACT.Ln, bias=eps[:, 0:1], scale=1.0 / P))
                act.activation(rr[:, :], rr[:, :], ACT.Exp, scale=-0.5).then_inc(rr_done, 1)

            act.wait_ge(vec_ps, 1)
            act.activation(vec[:, :], ps7[:, 0:V_N], ACT.Copy).then_inc(vec_done, 1)
            act.wait_ge(vec_done, 1)
            boundary(0, V_PRE1)
            act.wait_ge(relf_ps, 1)
            act.activation(relF[:, :], ps6[0:8, :], ACT.Copy).then_inc(relf_sb, 1)
            act.wait_ge(relf_sb, 1)
            act.dma_start(relF_dram, relF[:, :]).then_inc(relf_out, 16)
            act.wait_ge(relf_out, 16)
            act.dma_start(hankel[:, :, :], bass.AP(relF_dram.tensor, 0, [[1, P], [512, 8], [1, BAND1]]))\
               .then_inc(bias1_in, 16)
            act.dma_start(flip[:, :], a["shapes"][:, 4 * P + TOK + 64:5 * P + TOK + 64]).then_inc(bias1_in, 16)
            act.dma_start(sink1[:, :], bass.AP(a["swa_sink"].tensor, 0, [[0, P], [1, 8]])).then_inc(mix1_in, 16)
            act.dma_start(masks[:, :, :], a["shapes"][:, 2 * P:4 * P].rearrange("p (d n) -> p d n", d=2))\
               .then_inc(mix1_in, 16)
            act.dma_start(restart[:, :], a["shapes"][:, 4 * P:4 * P + TOK]).then_inc(mix1_in, 16)
            act.wait_ge(gatew_set, 1)
            act.dma_start(gate_w[0:16, 0, :], a["w_gate_up_fwd"][0]).then_inc(mix1_in, 16)
            act.dma_start(gate_w[16:32, 1, :], a["w_gate_up_bwd"][0]).then_inc(mix1_in, 16)
            split(0)
            token_scale(0)
            for step in STEPS_OF[0]:
                mixer_step_act(0, step)
            head_scale(3)
            for h in range(4):
                act.activation(ga[:, h, :], ga[:, h, :], ACT.Silu).then_inc(silu_done, 1)
            exp_ln_tables()
            halves(o1, (0, 1, 2, 3), lambda e, k: e.wait_ge(og_gated, k + 1))

            c_par = 0

            def plain_turns(c0, turns, last=True):
                nonlocal c_par
                c_par = c0 + 1
                with act.Fori(0, turns) as i:
                    for s in range(2):
                        c_par = c0 + s + 1
                        split(i * 2 + (c0 + s + 1))

            def squares_of_y(n, e, k0=0):
                for k in range(KT):
                    act.wait_ge(evac_done, e + k + 1)
                    square(n, k, y[:, k, :])

            def out_squares(n, c, e):
                for k in range(KT):
                    if k in (0, 2, 4) and c + 2 + k // 2 < C_END:
                        split(c + 2 + k // 2)
                    act.wait_ge(evac_done, e + k + 1)
                    square(n, k, y[:, k, :])

            out_squares(1, C_WOUT, E_WOUT)
            token_scale(1)
            split(C_UP0 + 1)
            boundary(1, V_PREM)
            token_scale(2)
            for half in range(2):
                cu, cd = (C_UP0, C_DN0) if half == 0 else (C_UP1, C_DN1)
                peeled = half == 0
                m0 = HID * half
                e_off = (E_UP0 if half == 0 else E_UP1 - HID)

                def up_tile(h_slot, idx, hid_ap, static_idx):
                    act.wait_ge(evac_done, idx + (e_off + 1))
                    if static_idx is None or static_idx >= 2:
                        act.wait_ge(hlo_done, idx - 1)
                    act.activation(zq[:, h_slot, :], zt[:, h_slot, :], ACT.Square).then_inc(zq_done, 1)
                    act.wait_ge(zq_done, idx + 1)
                    act.wait_ge(eps_set, 1)
                    act.activation(hid_ap, zq[:, h_slot, :], ACT.Copy).then_inc(hhi_done, 1)

                first = 0
                if half == 0:
                    for s in range(2):
                        if s == 0:
                            split(cu + 2)
                        for j in range(2):
                            up_tile(j, 2 * s + j, hid_hi[:, 2 * s + j, :], 2 * s + j)
                    first = 1
                else:
                    c_par = cu
                with act.Fori(0, 4 - first) as i:
                    for s in range(2):
                        c_par = cu + s + 1
                        split(i * 2 + (cu + 2 * first + s + 1))
                        for j in range(2):
                            up_tile(j, i * 4 + (m0 + 4 * first + 2 * s + j),
                                    hid_hi[:, bass.ds(i * 4 + (4 * first + 2 * s + j), 1), :], None)
                if half == 0:
                    plain_turns(cd, 4)
                else:
                    for p in range(4):
                        split(cd + 2 * p + 1)
                        split(cd + 2 * p + 2)
                        for j in range(2):
                            act.wait_ge(evac_done, E_DN1 + 2 * p + j + 1)
                            square(3, 2 * p + j, y[:, 2 * p + j, :])
            token_scale(3)
            act.dma_start(sink2[:, :], bass.AP(a["a_sinks_2"].tensor, 0, [[0, P], [1, 8]])).then_inc(mix2_in, 16)
            act.dma_start(bias2[:, :, :], a["alibi"]).then_inc(mix2_in, 16)
            act.dma_start(pw[:, :, :], a["b_pool_w_2"][0].rearrange("g c d -> c g d")).then_inc(mix2_in, 16)
            act.dma_start(wcnt[:, :, :], a["shapes"][:, 4 * P + TOK:4 * P + TOK + 64]
                          .rearrange("p (g n) -> p g n", g=4)).then_inc(mix2_in, 16)
            boundary(2, V_PRE2A)
            token_scale(4)
            for step in STEPS_OF[1]:
                mixer_step_act(1, step)
            out_squares(5, C_ABOUT, E_ABOUT)
            token_scale(5)
            split(C_CAB + 1)
            act.dma_start(tap_rows[:, :], a["c_dw_w_2"][0, :, 0, :]).then_inc(taps_in, 16)
            act.wait_ge(taps_ps, 1)
            act.activation(taps[:, :, :], ps6[:, 0:KT * TAPS].rearrange("p (k t) -> p k t", k=KT), ACT.Copy)\
               .then_inc(taps_done, 1)
            boundary(3, V_PRE2B)
            token_scale(6)
            with act.Fori(0, 2) as i:
                for t in range(TURN_TILES):
                    work = [(x * ACT_TAPS // DVE_TAPS, s) for x, s in TURN_WORK[t]]
                    for m in range(ACT_TAPS):
                        for x, s in work:
                            if m == x:
                                if s in TURN_AB:
                                    act.wait_ge(evac_done, i * (2 * TURN_CHUNKS) + (E_CAB + 2 * s + 2))
                                    act.activation(ab[:, 1, :], ab[:, 1, :], ACT.Sigmoid).then_inc(sig_done, 1)
                                c_par = C_CAB + s + 2
                                split(i * TURN_CHUNKS + (C_CAB + s + 2))
                        if m == 0:
                            act.wait_ge(glu_done, i * TURN_TILES + (t + 2))
                            act.wait_ge(tapw_done, i * 2 + 2)
                        g = ACT_TAPS * t + m - 4
                        act.wait_ge(pacc_step, i * (TURN_TILES * ADDS)
                                    + (ADDS * (g // ACT_TAPS + 1) + max(1, g % ACT_TAPS)))
                        act.activation(prod[:, (g + 4) % 4, :], glu[:, t % 2, DVE_TAPS + m:DVE_TAPS + m + TOK],
                                       ACT.Copy, scale=tapw[:, t, DVE_TAPS + m:DVE_TAPS + m + 1])\
                           .then_inc(prod_done, 1)
            act.wait_ge(evac_done, E_COUT)
            act.activation(gate[:, :, :], gate[:, :, :], ACT.Silu).then_inc(gsilu_done, 1)
            exp_ln_tables()
            act.wait_ge(musum_done, 1)
            act.activation(mu[:, :], ps6[:, :], ACT.Copy, scale=1.0 / D).then_inc(mu_done, 1)
            for k in range(KT):
                act.wait_ge(cen_done, k + 1)
                square(7, k, conv[:, k, :])
            token_scale(7)
            for k in range(KT):
                act.wait_ge(cn_done, k + 1)
                act.activation(conv[:, k, :], conv[:, k, :], ACT.Silu, bias=vec[:, V_LNB + k:V_LNB + k + 1],
                               scale=vec[:, V_LNG + k:V_LNG + k + 1]).then_inc(csilu_done, 1)
                if k >= 1:
                    act.wait_ge(yc_done, k)
                    act.activation(act_hi[:, k - 1, :], yc[:, (k - 1) % 2, :], ACT.Copy).then_inc(act_hi_done, 1)
            act.wait_ge(yc_done, KT)
            act.activation(act_hi[:, KT - 1, :], yc[:, (KT - 1) % 2, :], ACT.Copy).then_inc(act_hi_done, 1)
            out_squares(8, C_COUT, E_COUT)
            token_scale(8)
            for f in range(2 * NBLK):
                act.wait_ge(fT_done, f + 1)
                if f >= 2:
                    act.wait_ge(out_done[f % 2], 16 * (f // 2))
                act.activation(o_tok[:, f % 2, :], psT[:, f % 2, :], ACT.Copy).then_inc(fo_done, 1)

        @block.vector
        def _(dve):
            chain = Chain(dve, dve_step)
            c_par = 0

            def split(c):
                slot = (c if isinstance(c, int) else c_par) % 2
                cols = slice(0, P) if isinstance(c, int) and c == 3 else slice(0, CW)
                dve.wait_ge(hi_done, c + 1)
                dve.tensor_tensor(w_lo[:, slot, :, cols], raw[:, slot, :, cols],
                                  w_hi[:, slot, :, cols].bitcast(F32), ALU.subtract).then_inc(lo_done, 1)

            def evac_scaled(c, j, bank, dst, rows=P):
                dve.wait_ge(tile_done[j], c + 1)
                dve.tensor_tensor(dst, acc[0:rows, bank, :], R[0:rows, :], ALU.mult).then_inc(evac_done, 1)

            def lo_of_scaled(n, k, gain):
                dve.wait_ge(act_hi_done, 8 * (0, 2, 3, 5)[n] + k + 1)
                dve.scalar_tensor_tensor(out=act_lo[:, k, :], in0=resid[:, k, :],
                                         scalar=vec[:, gain + k:gain + k + 1],
                                         in1=act_hi[:, k, :].bitcast(F32), op0=ALU.mult, op1=ALU.subtract)\
                   .then_inc(act_lo_done, 1)

            def boundary(n, post, gain, tmp):
                for k in range(KT):
                    if k == 0:
                        dve.wait_ge(r_done, 2 * n)
                    chain.link(dve.tensor_tensor(tmp[:, k % 2, :], y[:, k, :], R[:, :], ALU.mult))
                    dve.scalar_tensor_tensor(out=resid[:, k, :], in0=tmp[:, k % 2, :],
                                             scalar=vec[:, post + k:post + k + 1], in1=resid[:, k, :],
                                             op0=ALU.mult, op1=ALU.add).then_inc(resid_done, 1)
                    if gain is not None and k >= 1:
                        lo_of_scaled(n, k - 1, gain)
                if gain is not None:
                    lo_of_scaled(n, KT - 1, gain)

            def lower_halves(tensor, order, n, first):
                for m, k in enumerate(order):
                    dve.wait_ge(act_hi_done, 8 * n + first + m + 1)
                    dve.tensor_tensor(act_lo[:, k, :], tensor[:, k, :], act_hi[:, k, :].bitcast(F32), ALU.subtract)\
                       .then_inc(act_lo_done, 1)

            def mixer_tile_dve(c, j):
                e, bank = mixer_tile(c, j)
                if c == 0 and j == 0:
                    dve.wait_ge(r_done, 1)
                if c == C_AIN and j == 0:
                    dve.wait_ge(r_done, 5)
                if c < 2:
                    dst = qs1[:, 2 * c + j, :]
                elif c == 2:
                    dst = (k1, v1)[j][:, :]
                elif c == 3:
                    dst = zz[:, :]
                elif c < 6:
                    if c == 4 and j == 0:
                        dve.wait_ge(relf_out, 16)
                    dst = (qa, ka)[c - 4][:, j, :]
                elif c < 8:
                    h = 2 * (c - 6) + j
                    if h >= 2:
                        dve.wait_ge(vaT_done, h - 1)
                    dst = vaf[:, h % 2, :]
                elif c < 10:
                    dst = ga[:, 2 * (c - 8) + j, :]
                else:
                    i, t = (c - C_AIN) // 2, 2 * ((c - C_AIN) % 2) + j
                    m = c - C_AIN
                    if m < 2:
                        dst = q2[:, 2 * m + j, :]
                    elif m == 2:
                        dst = (k2, v2)[j][:, :]
                    elif m < 5:
                        dst = ga2[:, 2 * (m - 3) + j, :]
                    elif m < 7:
                        dst = uu[:, 2 * (m - 5) + j, UPAD:]
                    else:
                        dst = gb2[:, 2 * (m - 7) + j, :]
                evac_scaled(c, j, bank, dst, 32 if c == 3 else P)

            def mixer_step_dve(layer, step):
                what, i = step[0], step[1]
                k = 16 * layer + i
                if what in ("split", "split_lo"):
                    split(i)
                elif what == "tile":
                    if step[3:] != (0,):
                        mixer_tile_dve(step[1], step[2])
                elif what == "softmax":
                    n, hp = i // 4, i % 4
                    kbs, b0 = window(layer, n)
                    w = len(kbs) * P
                    lg, sm = LG[layer][:, i % 2, :, :], SM[layer][:, i % 2, :, :]
                    if i == 0 and layer == 0:
                        dve.wait_ge(bias1_done, 8)
                    if i == 0 and layer == 1:
                        dve.wait_ge(mix2_in, 16 * MIX2_LOADS)
                    dve.wait_ge(qk_done, k + 1)
                    if i >= 2:
                        dve.wait_ge(pT_done, k - 1)
                    dve.scalar_tensor_tensor(out=lg[:, :, 1:1 + w], in0=acc[:, 2:4, 0:w], scalar=QSCALE,
                                             in1=BIAS[layer][:, 2 * hp:2 * hp + 2, b0:b0 + w],
                                             op0=ALU.mult, op1=ALU.add).then_inc(logits_done, 1)
                    dve.wait_ge(logits_done, k + 1)
                    dve.wait_ge(sink_set, k + 1)
                    chain.link(dve.tensor_reduce(sm[:, :, 0], lg[:, :, 0:1 + w], AX.X, ALU.max))
                    dve.tensor_scalar(sm[:, :, 1], sm[:, :, 0], -1.0, None, ALU.mult).then_inc(negmax_done, 1)
                elif what == "pv":
                    dve.wait_ge(exp_done, 2 * (k + 1))
                    sm = SM[layer][:, i % 2, :, :]
                    chain.link(dve.reciprocal(sm[:, :, 3:4], sm[:, :, 2:3]))
                    dve.wait_ge(pv_done, k + 1)
                    if i % 4 == 0 and k >= 4:
                        dve.wait_ge(oT_done, k // 4)
                    dve.tensor_tensor(OQ[layer][:, i % 4, :].rearrange("p (j d) -> p j d", j=2),
                                      ps6[:, 0:P].rearrange("p (j d) -> p j d", j=2),
                                      sm[:, :, 3:4].to_broadcast([P, 2, 64]), ALU.mult).then_inc(oq_done, 1)
                elif what == "gla_gate":
                    d, t = i % 2, i // 2
                    bias = vec[:, (V_BF, V_BB)[d] + t:(V_BF, V_BB)[d] + t + 1]
                    dve.wait_ge(gate_ps, i + 1)
                    if i >= 1:
                        dve.wait_ge(kint_done, i)
                    dve.tensor_scalar(gx[:, :], ps7[:, :], bias, None, ALU.add).then_inc(gx_done, 1)
                elif what == "gla_decay":
                    d, t = i % 2, i // 2
                    rev = slice(None, None, -1 if d else 1)
                    dve.wait_ge(ln_done, i + 1)
                    chain.link(dve.scalar_tensor_tensor(out=gx[:, :], in0=gx[:, :], scalar=0.0, in1=gl[:, :],
                                                        op0=ALU.min, op1=ALU.subtract))
                    if i == 0:
                        dve.wait_ge(mix1_in, 16 * MIX1_LOADS)
                    else:
                        dve.wait_ge(kT_done, i)
                    dve.tensor_tensor_scan(bb[:, rev], restart[:, :], gx[:, rev], 0.0, ALU.mult, ALU.add)\
                       .then_inc(bb_done, 1)
                    dve.wait_ge(bb_done, i + 1)
                    end = GLA_C - 1 if d == 0 else 0
                    b3 = bb[:, :].rearrange("p (n c) -> p n c", c=GLA_C)
                    dve.tensor_tensor(gl[:, :].rearrange("p (n c) -> p n c", c=GLA_C),
                                      b3[:, :, end:end + 1].to_broadcast([P, NCH, GLA_C]), b3, ALU.subtract)\
                       .then_inc(dk_done, 1)
                elif what == "gla_scaled":
                    d, t = i % 2, i // 2
                    end = GLA_C - 1 if d == 0 else 0
                    dve.wait_ge(eb_done, i + 1)
                    dve.tensor_copy(decay[:, d, t, :], eb[:, :].rearrange("p (n c) -> p n c", c=GLA_C)[:, :, end])\
                       .then_inc(decay_done, 1)
                    if d == 1:
                        dve.wait_ge(qdec_done, i)
                    dve.scalar_tensor_tensor(out=qdec(d, t), in0=qa[:, t, :], scalar=QSCALE, in1=eb[:, :],
                                             op0=ALU.mult, op1=ALU.mult).then_inc(qdec_done, 1)
                elif what == "gla_dS":
                    dve.wait_ge(dS_done, i + 1)
                    dve.wait_ge(decay_done, 4)
                    count = 14 * i
                    for m in range(NCH - 1):
                        for d in range(2):
                            n = m if d == 0 else NCH - 1 - m
                            to = n + 1 if d == 0 else n - 1
                            src = (acc[:, 2:4, :] if d == 0 else psT)[:, n % 2, (n // 2) * P:(n // 2 + 1) * P]
                            if m == 0:
                                ins = dve.tensor_copy(S[:, i, d, to, :], src)
                            else:
                                dve.wait_ge(S_done, count - 1)
                                ins = dve.scalar_tensor_tensor(out=S[:, i, d, to, :], in0=S[:, i, d, n, :],
                                                               scalar=decay[:, d, i, n:n + 1], in1=src,
                                                               op0=ALU.mult, op1=ALU.add)
                            ins.then_inc(S_done, 1)
                            count += 1
                elif what == "gla_A":
                    for d in range(2):
                        dve.wait_ge(A_done, 2 * i + d + 1)
                        if i == 0:
                            dve.wait_ge(Am_set, 1)
                        if i >= 2:
                            dve.wait_ge(og_done, i - 1)
                        mask = masks[:, d:d + 1, :].bitcast(I32).to_broadcast([P, NBLK, P])
                        dve.copy_predicated(Am[:, i % 2, d, :].rearrange("p (m c) -> p m c", c=P), mask,
                                            acc[:, 2 + d, :].rearrange("p (m c) -> p m c", c=P)).then_inc(Am_done, 1)
                elif what == "gla_sum" and i >= 1:
                    gla_normed(i - 1)
                elif what == "attention_halves":
                    split(11)
                    lower_halves(o1, (4, 5, 6, 7), 1, 0)
                elif what == "pool_window":
                    dve.wait_ge(wsum_done, i + 1)
                    dve.scalar_tensor_tensor(out=pooled[:, i, :], in0=wsum[:, i % 2, UPAD:], scalar=1.0 / POOLW[i],
                                             in1=uu[:, i, UPAD:], op0=ALU.mult, op1=ALU.subtract)\
                       .then_inc(pooled_done, 1)
                elif what == "attention_gate":
                    for h in range(4):
                        dve.wait_ge(silu2_done, h + 1)
                        if h == 0:
                            dve.wait_ge(o_done, 8)
                        dve.tensor_tensor(o2[:, h, :], o2[:, h, :], ga2[:, h, :], ALU.mult).then_inc(ob_done, 1)
                elif what == "pool_out":
                    split(56)
                    lower_halves(o2, range(4), 4, 0)
                    for g in range(4):
                        dve.wait_ge(silu2_done, 5 + g)
                        dve.wait_ge(yb_ps, g + 1)
                        src = (ps6[:, :], ps7[:, :], psT[:, 0, :], psT[:, 1, :])[g]
                        dve.scalar_tensor_tensor(out=o2[:, 4 + g, :], in0=src, scalar=vec[:, V_PSC + g:V_PSC + g + 1],
                                                 in1=gb2[:, g, :], op0=ALU.mult, op1=ALU.mult).then_inc(ob_done, 1)
                        if g >= 1:
                            lower_halves(o2, (3 + g,), 4, 3 + g)
                    lower_halves(o2, (7,), 4, 7)

            def gla_normed(h):
                dve.wait_ge(rr_done, h + 1)
                dve.tensor_tensor(o1[:, h, :], o1[:, h, :], (bb, eb)[h % 2][:, :], ALU.mult).then_inc(on_done, 1)

            def out_tiles(c, e):
                for k in range(KT):
                    if k in (0, 2, 4) and c + 2 + k // 2 < C_END:
                        split(c + 2 + k // 2)
                    dve.wait_ge(tile_done[k % 2], c + k // 2 + 1)
                    dve.tensor_copy(y[:, k, :], acc[:, k % 4, :]).then_inc(evac_done, 1)

            for k in range(KT):
                dve.wait_ge(xT_done, k + 1)
                dve.tensor_copy(resid[:, k, :], acc[:, k % 4, :]).then_inc(resid_done, 1)
                if k == 0:
                    dve.wait_ge(vec_done, 1)
                if k >= 1:
                    lo_of_scaled(0, k - 1, V_PRE1)
            lo_of_scaled(0, KT - 1, V_PRE1)
            split(0)
            for step in STEPS_OF[0]:
                mixer_step_dve(0, step)
            gla_normed(2)
            gla_normed(3)
            for h in range(4):
                dve.wait_ge(silu_done, h + 1)
                if h == 0:
                    dve.wait_ge(on_done, 4)
                dve.scalar_tensor_tensor(out=o1[:, h, :], in0=o1[:, h, :], scalar=vec[:, V_GN:V_GN + 1],
                                         in1=ga[:, h, :], op0=ALU.mult, op1=ALU.mult).then_inc(og_gated, 1)
                if h >= 1:
                    lower_halves(o1, (h - 1,), 1, 4 + h - 1)
            lower_halves(o1, (3,), 1, 7)
            out_tiles(C_WOUT, E_WOUT)
            split(C_UP0 + 1)
            boundary(1, V_POST1, V_PREM, ty)
            dve.wait_ge(r_done, 3)

            def up_tile(j, bank, c, e, m, hid_ap, ring_free):
                dve.wait_ge(tile_done[j], c + 1)
                if ring_free is not None:
                    dve.wait_ge(zq_done, ring_free)
                dve.scalar_tensor_tensor(out=zt[:, j, :], in0=acc[:, bank, :], scalar=0.0, in1=R[:, :],
                                         op0=ALU.max, op1=ALU.mult).then_inc(evac_done, 1)

            for half in range(2):
                cu, cd = (C_UP0, C_DN0) if half == 0 else (C_UP1, C_DN1)
                eu, ed = (E_UP0, E_DN0) if half == 0 else (E_UP1, E_DN1)
                first = 1 if half == 0 else 0
                if half == 0:
                    split(cu + 2)
                    for m in range(4):
                        up_tile(m % 2, m, cu + m // 2, eu + m, m, None, m - 1 if m >= 2 else None)
                        dve.wait_ge(hhi_done, m + 1)
                        dve.tensor_tensor(hid_lo[:, m, :], zq[:, m % 2, :], hid_hi[:, m, :].bitcast(F32), ALU.subtract)\
                           .then_inc(hlo_done, 1)
                with dve.Fori(0, 4 - first) as i:
                    for s in range(2):
                        c_par = cu + s + 1
                        split(i * 2 + (cu + 2 * first + s + 1))
                        for j in range(2):
                            m = i * 4 + (HID * half + 4 * first + 2 * s + j)
                            mh = i * 4 + (4 * first + 2 * s + j)
                            up_tile(j, 2 * s + j, i * 2 + (cu + 2 * first + s), None, m, None, m - 1)
                            dve.wait_ge(hhi_done, m + 1)
                            dve.tensor_tensor(hid_lo[:, bass.ds(mh, 1), :], zq[:, j:j + 1, :],
                                              hid_hi[:, bass.ds(mh, 1), :].bitcast(F32), ALU.subtract)\
                               .then_inc(hlo_done, 1)
                with dve.Fori(0, 2) as i:
                    for pair in range(2):
                        for kg in range(2):
                            c_par = cd + kg + 1
                            split(i * 4 + (cd + 2 * pair + kg + 1))
                        for j in range(2):
                            t = i * 4 + (2 * pair + j)
                            dve.wait_ge(tile_done[j], i * 4 + (cd + 2 * pair + 2))
                            yt = y[:, bass.ds(t, 1), :]
                            bank = acc[:, 2 * pair + j:2 * pair + j + 1, :]
                            if half == 0:
                                dve.tensor_scalar(yt, bank, 1.0, None, ALU.mult).then_inc(evac_done, 1)
                            else:
                                dve.tensor_tensor(yt, bank, yt, ALU.add).then_inc(evac_done, 1)
            boundary(2, V_POSTM, V_PRE2A, ty_e)
            for step in STEPS_OF[1]:
                mixer_step_dve(1, step)
            out_tiles(C_ABOUT, E_ABOUT)
            split(C_CAB + 1)
            boundary(3, V_POST2A, V_PRE2B, ty_c)
            dve.wait_ge(r_done, 7)
            dve.wait_ge(taps_done, 1)
            dve.memset(vacc[:, 0, :], 0.0).then_inc(conv_step, 1)
            dve.memset(vacc[:, 1, :], 0.0).then_inc(prod_done, 1)
            with dve.Fori(0, 2) as i:
                def chunk_out(s):
                    c = C_CAB + s
                    for j in range(2):
                        dve.wait_ge(tile_done[j], i * TURN_CHUNKS + (c + 1))
                        bank = acc[:, (2 * s + j) % 4:(2 * s + j) % 4 + 1, :]
                        R3 = R[:, :].rearrange("p (a n) -> p a n", a=1)
                        if s in TURN_AB:
                            if j == 0:
                                dve.wait_ge(glu_done, i * TURN_TILES + (TURN_AB[s] + 1))
                            dst = ab[:, j:j + 1, :]
                        else:
                            dst = gate[:, bass.ds(i * 4 + (2 * GATE_AT.index(s) + j), 1), :]
                        dve.tensor_tensor(dst, bank, R3, ALU.mult).then_inc(evac_done, 1)
                    nonlocal c_par
                    c_par = c + 2
                    split(i * TURN_CHUNKS + (c + 2))

                dve.wait_ge(prod_done, i * (TURN_TILES * ACT_TAPS) + 1)
                dve.tensor_copy(tapw[:, :, 0:TAPS], taps[:, bass.ds(i * TURN_TILES, TURN_TILES), :])\
                   .then_inc(tapw_done, 1)
                dve.tensor_copy(tapw[:, :, TAPS], vec[:, bass.ds(i * TURN_TILES + V_DWB, TURN_TILES)])\
                   .then_inc(tapw_done, 1)
                for t in range(TURN_TILES):
                    vsteps = DVE_TAPS + 1
                    for m in range(DVE_TAPS):
                        for x, s in TURN_WORK[t]:
                            if m == x:
                                chunk_out(s)
                        if m == 0:
                            dve.wait_ge(tapw_done, i * 2 + 2)
                            dve.wait_ge(glu_done, i * TURN_TILES + (t + 2))
                            dve.wait_ge(conv_step, i * TURN_TILES + (t + 1))
                        src, sums = glu[:, t % 2, m:m + TOK], vacc[:, m % 2, :]
                        if m >= 2:
                            dve.wait_ge(vacc_step, i * (TURN_TILES * vsteps) + (vsteps * t + m - 1))
                        if m == 0:
                            ins = dve.tensor_scalar(sums, src, tapw[:, t, 0:1], tapw[:, t, TAPS:TAPS + 1],
                                                    ALU.mult, ALU.add)
                        elif m == 1:
                            ins = dve.tensor_scalar(sums, src, tapw[:, t, 1:2], None, ALU.mult)
                        else:
                            ins = dve.scalar_tensor_tensor(out=sums, in0=src, scalar=tapw[:, t, m:m + 1], in1=sums,
                                                           op0=ALU.mult, op1=ALU.add)
                        ins.then_inc(vacc_step, 1)
                    dve.wait_ge(vacc_step, i * (TURN_TILES * vsteps) + (vsteps * t + DVE_TAPS))
                    dve.tensor_tensor(vacc[:, 0, :], vacc[:, 0, :], vacc[:, 1, :], ALU.add).then_inc(vacc_step, 1)
                    dve.wait_ge(vacc_step, i * (TURN_TILES * vsteps) + vsteps * (t + 1))
                    dve.wait_ge(pacc_step, i * (TURN_TILES * ADDS) + ADDS * (t + 2))
                    dve.tensor_tensor(conv[:, bass.ds(i * TURN_TILES + t, 1), :], vacc[:, 0:1, :],
                                      pacc[:, :].rearrange("p (a n) -> p a n", a=1), ALU.add).then_inc(conv_step, 1)
            dve.wait_ge(mu_done, 1)
            dve.wait_ge(conv_step, KT + 1)
            for k in range(KT):
                dve.tensor_tensor(conv[:, k, :], conv[:, k, :], mu[:, :], ALU.subtract).then_inc(cen_done, 1)
            dve.wait_ge(r_done, 8)
            dve.wait_ge(cen_done, KT)
            for k in range(KT + 2):
                if k < KT:
                    dve.tensor_tensor(conv[:, k, :], conv[:, k, :], R[:, :], ALU.mult).then_inc(cn_done, 1)
                if 1 <= k <= KT:
                    m = k - 1
                    dve.wait_ge(csilu_done, m + 1)
                    if m == 0:
                        dve.wait_ge(gsilu_done, 1)
                    if m >= 2:
                        dve.wait_ge(act_lo_done, 8 * 6 + m - 1)
                    dve.tensor_tensor(yc[:, m % 2, :], conv[:, m, :], gate[:, m, :], ALU.mult).then_inc(yc_done, 1)
                if k >= 2:
                    m = k - 2
                    dve.wait_ge(act_hi_done, 8 * 6 + m + 1)
                    dve.tensor_tensor(act_lo[:, m, :], yc[:, m % 2, :], act_hi[:, m, :].bitcast(F32), ALU.subtract)\
                       .then_inc(act_lo_done, 1)
            out_tiles(C_COUT, E_COUT)
            dve.wait_ge(r_done, 9)
            boundary(4, V_POST2B, None, ty_c)


_INS = ["x", "norm_mix_pre", "w_in", "w_gate_up_fwd", "b_gate_fwd", "w_gate_up_bwd", "b_gate_bwd", "gla_norm",
        "swa_sink", "rel_bias", "w_out", "norm_mix_post", "norm_mlp_pre", "w_up", "w_down", "norm_mlp_post",
        "pre_norm_2", "post_norm_2", "a_w_in_2", "a_sinks_2", "b_pool_w_2", "b_pool_scale_2", "ab_w_out_2",
        "c_w_in_2", "c_dw_w_2", "c_dw_b_2", "c_ln_g_2", "c_ln_b_2", "c_w_out_2"]


def kernel(**inputs):
    import numpy as _np
    import concourse.bacc as _bacc
    from concourse import mybir as _mybir
    from concourse.bass_utils import run_bass_kernel_spmd as _run

    nc = _bacc.Bacc("TRN2", target_bir_lowering=False, num_devices=1)
    given = {name: _np.ascontiguousarray(inputs[name]) for name in _INS}
    given.update(shapes=shape_constants(), onehot=t5_bucket_onehot(), alibi=alibi_band())
    arrays, args = {}, {}
    for name, v in given.items():
        arrays[f"in_{name}_dram"] = v
        args[name] = nc.dram_tensor(f"in_{name}_dram", v.shape, _mybir.dt.from_np(v.dtype), kind="ExternalInput").ap()
    out = nc.dram_tensor("out_0_dram", (1, TOK, D), F32, kind="ExternalOutput").ap()
    block_kernel(nc, args, out)
    r = _run(nc, [arrays], core_ids=[0])
    return r.results[0]["out_0_dram"]
```

```python
import numpy as np
import concourse.bass as bass
from concourse import mybir
from contextlib import ExitStack

F32 = mybir.dt.float32
F32R = mybir.dt.float32r
I32 = mybir.dt.int32
ALU = mybir.AluOpType
ACT = mybir.ActivationFunctionType
AX = mybir.AxisListType

P = 128
TOK = 512
NBLK = TOK // P
D = 1024
KT = D // P
CW = 256
FF = 4096
HID = FF // P // 2
EPS = 1e-6

QA, KA, VA, GA, ZA, QS, KS, WIN_COLS = 0, 256, 512, 1024, 1536, 1568, 2080, 2336
AQ, AKV, AGA, AU, AGB, AIN_COLS = 0, 512, 768, 1280, 1792, 2304
GLA_C = 64
NCH = TOK // GLA_C
STEPS = NBLK * 4
GATE_NORM = 16.0
QSCALE = 0.125
BAND1 = 3 * P
REPEAT = 16
BAND2 = 2 * P
LGW = BAND1 + 1
POOLW = (2, 4, 8, 16)
BOUNDARY_FILL = 10
PAIRED = 4
UPAD = 16
TAPS = 31
CPAD = TAPS - 1
DVE_TAPS = 18
ACT_TAPS = TAPS - DVE_TAPS
ADDS = ACT_TAPS - 1
TURN_TILES, TURN_CHUNKS = 4, 6
GATE_AT = (2, 5)
TURN_WORK = (((0, 0), (9, 1)), ((3, 2), (12, 3)), ((12, 4),), ((9, 5),))
TURN_AB = {0: 0, 1: 1, 3: 2, 4: 3}

V_PRE1, V_POST1, V_PREM, V_POSTM, V_PRE2A, V_POST2A, V_PRE2B, V_POST2B = [8 * i for i in range(8)]
V_DWB, V_LNG, V_LNB = 64, 72, 80
V_PSC, V_GN, V_BF, V_BB, V_N = 88, 92, 93, 95, 97

C_WIN, C_WOUT, C_UP0, C_DN0, C_UP1, C_DN1 = 0, 10, 14, 22, 30, 38
C_AIN, C_ABOUT, C_CAB, C_COUT, C_END = 46, 55, 59, 71, 75
E_WOUT, E_UP0, E_DN0, E_UP1, E_DN1 = 19, 27, 43, 51, 67
E_AIN, E_ABOUT, E_CAB, E_COUT = 75, 93, 101, 125

def t5_bucket_onehot():
    rel = np.arange(-255, 256)
    nb, max_exact = 16, 8
    n = np.abs(rel)
    large = max_exact + (np.log(np.maximum(n, 1).astype(np.float32) / max_exact)
                         / np.log(128 / max_exact) * (nb - max_exact)).astype(np.int32)
    bucket = (rel > 0) * nb + np.where(n < max_exact, n, np.minimum(large, nb - 1))
    hot = np.zeros((33, 512), np.float32)
    seen = n <= 128
    hot[bucket[seen], np.arange(511)[seen]] = 1.0
    hot[32, :511] = ~seen
    return hot


def shape_constants():
    i = np.arange(P)
    same = (i[:, None] // GLA_C) == (i[None, :] // GLA_C)
    fwd = same & (i[:, None] <= i[None, :])
    bwd = same & (i[:, None] >= i[None, :])
    restart = np.broadcast_to((np.arange(TOK) % GLA_C != 0), (P, TOK))
    t = np.arange(16)
    cnt = np.concatenate([w / np.minimum(t + 1, w) for w in POOLW])
    return np.concatenate([np.eye(P), np.ones((P, P)), fwd, bwd, restart,
                           np.broadcast_to(cnt, (P, 64))], axis=1).astype(np.float32)


def alibi_band():
    slopes = np.exp2(-8.0 * np.arange(1, 9, dtype=np.float32) / 8).astype(np.float32)
    dist = (np.arange(P)[:, None] + P - np.arange(BAND2)[None, :]).astype(np.float32)
    bias = -slopes[None, :, None] * dist[:, None, :]
    return np.where(((dist >= 0) & (dist < 128))[:, None, :], bias, np.float32(-1e30)).astype(np.float32)


def vector_rows(given):
    parts = [given["norm_mix_pre"][0], given["norm_mix_post"][0], given["norm_mlp_pre"][0], given["norm_mlp_post"][0],
             given["pre_norm_2"][0], given["post_norm_2"][0], given["pre_norm_2"][1], given["post_norm_2"][1],
             given["c_dw_b_2"][0], given["c_ln_g_2"][0], given["c_ln_b_2"][0], given["b_pool_scale_2"][0],
             given["gla_norm"][0], given["b_gate_fwd"][0], given["b_gate_bwd"][0]]
    return np.concatenate(parts).reshape(V_N, P)


MIX1_LOADS, MIX2_LOADS = 5, 4


class Chain:

    def __init__(self, eng, sem):
        self.eng, self.sem, self.n, self.reg, self.per = eng, sem, 0, None, 0

    def link(self, ins):
        self.n += 1
        ins.then_inc(self.sem, 1)
        self.eng.wait_ge(self.sem, self.n if self.reg is None else self.reg * self.per + self.n)

    def enter(self, reg, per):
        self.reg, self.per, self.start = reg, per, self.n

    def leave(self, trips):
        assert self.n - self.start == self.per, (self.n - self.start, self.per)
        self.n, self.reg = self.start + trips * self.per, None


def block_kernel(nc, a, out):
    ctx = ExitStack()
    with ctx:
        top = [(nc.sbuf_base + 31) // 32 * 32]

        def at(name, shape, offset, dt=F32):
            return nc.alloc_sbuf_tensor_at(name, shape, dt, offset=offset)

        def sb(name, shape, dt=F32):
            size = 4 * int(np.prod(shape[1:]))
            t = at(name, shape, top[0], dt)
            top[0] += (size + 31) // 32 * 32
            return t

        def sem(name):
            return ctx.enter_context(nc.semaphore(name))

        raw = sb("raw", [P, 2, KT, CW])
        w_hi = sb("w_hi", [P, 2, KT, CW], F32R)
        w_lo = sb("w_lo", [P, 2, KT, CW], F32R)
        resid = sb("resid", [P, KT, TOK])
        act_hi = sb("act_hi", [P, KT, TOK], F32R)
        act_lo = sb("act_lo", [P, KT, TOK], F32R)
        R = sb("R", [P, TOK])
        sq = sb("sq", [P, 2, TOK])
        sq_sum = sb("sq_sum", [P, TOK])
        ident_ones = sb("ident_ones", [P, 2 * P])
        ident, ones = ident_ones[:, 0:P], ident_ones[:, P:2 * P]
        vec = sb("vec", [P, V_N])
        eps = sb("eps", [P, 1])
        arena = top[0]

        def arena_alloc(start):
            at_ = [start]

            def take(name, shape, dt=F32):
                t = at(name, shape, at_[0], dt)
                at_[0] += (4 * int(np.prod(shape[1:])) + 31) // 32 * 32
                return t
            take.pos = at_
            return take

        m1 = arena_alloc(arena)
        o1 = m1("o1", [P, KT, TOK])
        qa = m1("qa", [P, 2, TOK])
        ka = m1("ka", [P, 2, TOK])
        va_tok = m1("va_tok", [P, NBLK, 512])
        ga = m1("ga", [P, 4, TOK])
        masks = m1("masks", [P, 2, P])
        restart = m1("restart", [P, TOK])
        zz = m1("zz", [32, TOK])
        gate_w = m1("gate_w", [32, 2, 256])
        decay = m1("decay", [P, 2, 2, NCH])
        late = m1.pos[0]
        sA = arena_alloc(late)
        bias1 = sA("bias1", [P, 8, BAND1])
        qs1 = sA("qs1", [P, 4, TOK])
        k1 = sA("k1", [P, TOK])
        k1x = sA("k1x", [P, TOK])
        v1 = sA("v1", [P, TOK])
        v1_tok = sA("v1_tok", [P, NBLK, P])
        lg1 = sA("lg1", [P, 2, 2, LGW])
        pT1 = sA("pT1", [P, 3 * 2 * P])
        sm1 = sA("sm1", [P, 2, 2, 4])
        oq1 = sA("oq1", [P, 4, P])
        sink1 = sA("sink1", [P, 8])
        vaf = sA("vaf", [P, 2, TOK])
        qdec_f = sA("qdec_f", [P, 2, TOK])
        kint_f = sA("kint_f", [P, 2, TOK])
        eb = sA("eb", [P, TOK])
        gx, gl, bb = sq[:, 0, :], sq[:, 1, :], sq_sum
        gA = arena_alloc(late)
        S = gA("S", [P, 2, 2, NCH, P])
        Am = gA("Am", [P, 2, 2, TOK])
        x_tok = at("x_tok", [P, NBLK, D], arena)
        relw = at("relw", [33, 8], arena + 4 * NBLK * D)
        hot = at("hot", [33, 512], arena + 4 * NBLK * D + 32)
        relF = at("relF", [8, 512], arena + 4 * NBLK * D + 32 + 2048)
        vec_rows = at("vec_rows", [V_N, P], arena + 4 * NBLK * D + 32 + 4096)
        mA = arena_alloc(arena)
        y = mA("y", [P, KT, TOK])
        hid_hi = mA("hid_hi", [P, HID, TOK], F32R)
        hid_lo = mA("hid_lo", [P, HID, TOK], F32R)
        zt = mA("zt", [P, 2, TOK])
        ty = mA("ty", [P, 2, TOK])
        zq = sq
        eA = arena_alloc(arena + 4 * KT * TOK)
        o2 = eA("o2", [P, KT, TOK])
        q2 = eA("q2", [P, 4, TOK])
        k2 = eA("k2", [P, TOK])
        k2x = eA("k2x", [P, TOK])
        v2 = eA("v2", [P, TOK])
        v2_tok = eA("v2_tok", [P, NBLK, P])
        bias2 = eA("bias2", [P, 8, BAND2])
        lg2 = eA("lg2", [P, 2, 2, BAND2 + 1])
        pT2 = eA("pT2", [P, 2 * 2 * P])
        sm2 = eA("sm2", [P, 2, 2, 4])
        oq2 = eA("oq2", [P, 4, P])
        sink2 = eA("sink2", [P, 8])
        ga2 = eA("ga2", [P, 4, TOK])
        gb2 = at("gb2", [P, 4, TOK], arena + 4 * 2 * KT * TOK)
        uu = eA("uu", [P, 4, UPAD + TOK])
        pw = eA("pw", [P, 4, P])
        wsum = eA("wsum", [P, 2, UPAD + TOK])
        pooled = eA("pooled", [P, 4, TOK])
        ty_e = at("ty_e", [P, 2, TOK], eA.pos[0])
        wcnt = at("wcnt", [P, 4, 16], eA.pos[0] + 4096)
        cA = arena_alloc(arena + 4 * KT * TOK)
        conv = cA("conv", [P, KT, TOK])
        gate = cA("gate", [P, KT, TOK])
        glu = cA("glu", [P, 2, CPAD + TOK])
        ab = cA("ab", [P, 2, TOK])
        taps = cA("taps", [P, KT, TAPS])
        tapw = cA("tapw", [P, TURN_TILES, TAPS + 1])
        prod = cA("prod", [P, 4, TOK])
        pacc = cA("pacc", [P, TOK])
        vacc = cA("vacc", [P, 2, TOK])
        mu = cA("mu", [P, TOK])
        yc = cA("yc", [P, 2, TOK])
        ty_c = cA("ty_c", [P, 4, TOK])
        tap_rows = at("tap_rows", [TAPS, D], cA.pos[0])
        o_tok = at("o_tok", [P, 2 * NBLK, 512], arena + 4 * KT * TOK)

        acc = ctx.enter_context(nc.psum_tensor("acc", [P, 4, 512], F32))
        psT = ctx.enter_context(nc.psum_tensor("psT", [P, 2, 512], F32))
        ps6 = ctx.enter_context(nc.psum_tensor("ps6", [P, 512], F32))
        ps7 = ctx.enter_context(nc.psum_tensor("ps7", [P, 512], F32))
        psTf = psT[:, :, :].rearrange("p a b -> p (a b)")

        relF_dram = nc.dram_tensor("relF_dram", [8, REPEAT, 512], F32, kind="Internal").ap()

        raw_ready = [sem("raw_ready0"), sem("raw_ready1")]
        hi_done = sem("hi_done")
        lo_done = sem("lo_done")
        tile_done = [sem("tile_done0"), sem("tile_done1")]
        evac_done = sem("evac_done")
        x_in = [sem(f"x_in{b}") for b in range(NBLK)]
        vec_in = sem("vec_in")
        vec_ps = sem("vec_ps")
        vec_done = sem("vec_done")
        taps_ps = sem("taps_ps")
        taps_done = sem("taps_done")
        const_in = sem("const_in")
        rel_in = sem("rel_in")
        gatew_set = sem("gatew_set")
        relf_ps = sem("relf_ps")
        relf_sb = sem("relf_sb")
        relf_out = sem("relf_out")
        bias1_in = sem("bias1_in")
        mix1_in = sem("mix1_in")
        xT_done = sem("xT_done")
        resid_done = sem("resid_done")
        act_hi_done = sem("act_hi_done")
        act_lo_done = sem("act_lo_done")
        sq_done = sem("sq_done")
        sqsum_done = sem("sqsum_done")
        rsum_done = sem("rsum_done")
        r_done = sem("r_done")
        ty_done = sem("ty_done")
        eps_set = sem("eps_set")
        dve_step = sem("dve_step")
        act_step = sem("act_step")
        pool_step = sem("pool_step")
        kx_done = sem("kx_done")
        vT_done = sem("vT_done")
        vtok_done = sem("vtok_done")
        sink_set = sem("sink_set")
        qk_done = sem("qk_done")
        logits_done = sem("logits_done")
        negmax_done = sem("negmax_done")
        exp_done = sem("exp_done")
        pT_done = sem("pT_done")
        pTs_done = sem("pTs_done")
        pv_done = sem("pv_done")
        oq_done = sem("oq_done")
        oT_done = sem("oT_done")
        o_done = sem("o_done")
        vaT_done = sem("vaT_done")
        vatok_done = sem("vatok_done")
        gate_ps = sem("gate_ps")
        gx_done = sem("gx_done")
        ln_done = sem("ln_done")
        bb_done = sem("bb_done")
        eb_done = sem("eb_done")
        enb_done = sem("enb_done")
        qdec_done = sem("qdec_done")
        kint_done = sem("kint_done")
        dk_done = sem("dk_done")
        ek_done = sem("ek_done")
        ks_done = sem("ks_done")
        kT_done = sem("kT_done")
        kst_done = sem("kst_done")
        decay_done = sem("decay_done")
        dS_done = sem("dS_done")
        S_done = sem("S_done")
        A_done = sem("A_done")
        Am_set = sem("Am_set")
        Am_done = sem("Am_done")
        og_done = sem("og_done")
        og_out = sem("og_out")
        ogsq_done = sem("ogsq_done")
        ogsum_done = sem("ogsum_done")
        rr_done = sem("rr_done")
        on_done = sem("on_done")
        silu_done = sem("silu_done")
        og_gated = sem("og_gated")
        zq_done = sem("zq_done")
        hhi_done = sem("hhi_done")
        hlo_done = sem("hlo_done")
        mix2_in = sem("mix2_in")
        upad_set = sem("upad_set")
        pooled_done = sem("pooled_done")
        wsum_done = sem("wsum_done")
        yb_ps = sem("yb_ps")
        ob_done = sem("ob_done")
        silu2_done = sem("silu2_done")
        taps_in = sem("taps_in")
        sig_done = sem("sig_done")
        glu_done = sem("glu_done")
        tapw_done = sem("tapw_done")
        prod_done = sem("prod_done")
        pacc_step = sem("pacc_step")
        vacc_step = sem("vacc_step")
        conv_step = sem("conv_step")
        musum_done = sem("musum_done")
        mu_done = sem("mu_done")
        cen_done = sem("cen_done")
        cn_done = sem("cn_done")
        csilu_done = sem("csilu_done")
        gsilu_done = sem("gsilu_done")
        yc_done = sem("yc_done")
        fT_done = sem("fT_done")
        fo_done = [sem("fo_done0"), sem("fo_done1")]
        out_done = sem("out_done")

        block = ctx.enter_context(nc.Block())

        def qdec(d, t):
            return (qdec_f, qa)[d][:, t, :]

        def kint(d, t):
            return (kint_f, ka)[d][:, t, :]

        def kst(d, t):
            return o1[:, 2 * t + d, :].rearrange("p (b n) -> p b n", b=NBLK)

        def attention_unit(k, work):
            steps = [("qk", k)] if k < STEPS else []
            steps += [("transpose", k - 1)] if 1 <= k <= STEPS else []
            steps += [("softmax", k)] if k < STEPS else []
            steps += [("turn", (k - 2) // 4)] if k >= 5 and k % 4 == 1 else []
            return steps + work + ([("pv", k - 1)] if 1 <= k <= STEPS else [])

        def half_tiles(c):
            return [("tile", c, j, h) for j in range(2) for h in range(2)]

        def first_steps(c):
            return [("pair", c), ("evacuate", c, 0), ("evacuate", c, 1), ("split", c + 2),
                    ("evacuate", c + 1, 0), ("evacuate", c + 1, 1), ("split", c + 3),
                    ("tile", c + 2, 0), ("tile", c + 2, 1)]

        def mixer1_steps():
            steps = first_steps(0)
            steps += [("keys_values", 0), ("split", 4), ("tile", 3, 1)]
            k = 0
            for c in (4, 5, 6, 7, 8):
                for m, half in enumerate(half_tiles(c)[:2 if c == 8 else 4]):
                    work = [half]
                    if m == 0:
                        work.insert(0, ("split_hi", c + 1))
                    if m == 1:
                        work.insert(0, ("split_lo", c + 1))
                    if c in (6, 7) and m % 2:
                        work.append(("gla_values", 2 * (c - 6) + m // 2))
                    if k >= 8 and k % 3 == 2:
                        work.insert(0, ("gla_keys", (k - 8) // 3))
                    if 4 <= k <= 15:
                        work.append((("gla_gate", "gla_decay", "gla_scaled")[(k - 4) % 3], (k - 4) // 3))
                    steps += attention_unit(k, work)
                    k += 1
            rest = half_tiles(8)[2:] + half_tiles(9)
            steps += [("gla_dS", 0), rest[0], ("split_hi", 10), rest[1], ("split_lo", 10), ("gla_dS", 1), rest[2],
                      ("gla_A", 0), rest[3], ("gla_A", 1), ("gla_out", 0), rest[4],
                      ("gla_A", 2), ("gla_out", 1), ("gla_sum", 0), rest[5],
                      ("gla_A", 3), ("gla_out", 2), ("gla_sum", 1), ("attention_halves", 0),
                      ("gla_out", 3), ("gla_sum", 2)]
            return steps

        def mixer2_steps():
            steps = first_steps(C_AIN)
            steps += [("keys_values", 1)]
            k = 0
            for c in (49, 50, 51, 52, 53):
                for m, half in enumerate(half_tiles(c)):
                    work = [half]
                    if m == 0:
                        work.insert(0, ("split_hi", c + 1))
                    if m == 1:
                        work.insert(0, ("split_lo", c + 1))
                    if c in (51, 52) and m % 2:
                        work.append(("pool_window", 2 * (c - 51) + m // 2))
                    if k in (11, 13, 15, 19):
                        work.append(("pooled", (11, 13, 15, 19).index(k)))
                    steps += attention_unit(k, work) if k < STEPS + 2 else work
                    k += 1
            steps += [("attention_gate", 0)]
            steps += [("split", 55), ("tile", 54, 0), ("tile", 54, 1), ("pool_out", 0)]
            return steps

        def window(layer, n):
            kbs = [b for b in (range(n - 1, n + 2) if layer == 0 else range(n - 1, n + 1)) if 0 <= b < NBLK]
            return kbs, (kbs[0] - (n - 1)) * P

        LG, PT, SM, SINK, BIAS = (lg1, lg2), (pT1, pT2), (sm1, sm2), (sink1, sink2), (bias1, bias2)
        OQ = (oq1, oq2)
        QH, KH, KX, VT, VTOK, OO = (qs1, q2), (k1, k2), (k1x, k2x), (v1, v2), (v1_tok, v2_tok), (o1, o2)

        def o_tile(layer, hp):
            return (4 if layer == 0 else 0) + hp

        STEPS_OF = (mixer1_steps(), mixer2_steps())

        def before(layer, at, what):
            return sum(step[0] == what for step in STEPS_OF[layer][:at])

        def mixer_tile(c, j):
            if c < C_WOUT:
                e = 2 * c + j if c < 3 else (6 if c == 3 else 2 * c - 1 + j)
                return e, 2 + j if c == 1 else (0 if c == 3 else j)
            return E_AIN + 2 * (c - C_AIN) + j, 2 + j if c == C_AIN + 1 else j

        @block.sync
        def _(sp):
            def wait_slot(c):
                if isinstance(c, int) and c < 2:
                    return
                sp.wait_ge(lo_done, c - 1)

            def load(slot, w, n0, rows0=0, width=CW):
                rows = w[rows0:rows0 + D, :].rearrange("(k p) n -> p k n", p=P)
                for kk in (slice(0, KT // 2), slice(KT // 2, KT)):
                    sp.dma_start(raw[:, slot, kk, 0:width], rows[:, kk, bass.ds(n0, width)])\
                      .then_inc(raw_ready[slot], 16)

            def load_plain(w, c0, n, n0=0):
                with sp.Fori(0, n // 2) as i:
                    for s in range(2):
                        wait_slot(i * 2 + (c0 + s))
                        load((c0 + s) % 2, w, i * (2 * CW) + (n0 + s * CW))

            w_in, w_out, w_up, w_down = a["w_in"][0], a["w_out"][0], a["w_up"][0], a["w_down"][0]
            for c, n0 in enumerate((QS, QS + CW, KS, ZA, QA, KA, VA, VA + CW, GA, GA + CW)):
                wait_slot(c)
                load(c % 2, w_in, n0, 0, P if n0 == ZA else CW)
                if c == 0:
                    for b in range(NBLK):
                        sp.dma_start(x_tok[:, b, :], a["x"][0, b * P:(b + 1) * P, :]).then_inc(x_in[b], 16)
            load_plain(w_out, C_WOUT, 4)
            for half in range(2):
                cu, cd = (C_UP0, C_DN0) if half == 0 else (C_UP1, C_DN1)
                load_plain(w_up, cu, 8, half * FF // 2)
                with sp.Fori(0, 4) as i:
                    for s in range(2):
                        wait_slot(i * 2 + (cd + s))
                        load(s, w_down, i * CW, half * FF // 2 + s * D)
            for i in range(9):
                wait_slot(C_AIN + i)
                load((C_AIN + i) % 2, a["a_w_in_2"][0], i * CW)
            load_plain(a["ab_w_out_2"][0], C_ABOUT, 4)
            c_w_in = a["c_w_in_2"][0]
            ab_cols = c_w_in.rearrange("(k p) n -> p k n", p=P)
            with sp.Fori(0, 2) as i:
                for s in range(TURN_CHUNKS):
                    slot = (C_CAB + s) % 2
                    wait_slot(i * TURN_CHUNKS + (C_CAB + s))
                    if s in GATE_AT:
                        load(slot, c_w_in, i * (2 * CW) + (2 * D + CW * GATE_AT.index(s)))
                        continue
                    for g in range(2):
                        sp.dma_start(raw[:, slot, :, g * P:(g + 1) * P],
                                     ab_cols[:, :, bass.ds(i * (TURN_TILES * P) + (g * D + TURN_AB[s] * P), P)])\
                          .then_inc(raw_ready[slot], 16)
            load_plain(a["c_w_out_2"][0], C_COUT, 4)
            for f in range(2 * NBLK):
                sp.wait_ge(fo_done[f % 2], f // 2 + 1)
                sp.dma_start(out[0, (f // 2) * P:(f // 2 + 1) * P, (f % 2) * 512:(f % 2 + 1) * 512],
                             o_tok[:, f, :]).then_inc(out_done, 16)
            sp.wait_ge(out_done, 16 * 2 * NBLK)

        @block.tensor
        def _(pe):
            def mm3(dst, hi, lo, x_hi, x_lo, first, last):
                pe.matmul(dst, hi, x_hi, start=first, stop=False)
                pe.matmul(dst, hi, x_lo, start=False, stop=False)
                return pe.matmul(dst, lo, x_hi, start=False, stop=last)

            def w_tiles(slot, k, j):
                return w_hi[:, slot, k, j * P:(j + 1) * P], w_lo[:, slot, k, j * P:(j + 1) * P]

            def keep_clock(n):
                for m in range(n):
                    pe.matmul(psT[:, 1, 0:2 * P], ones[:, :], ident_ones[:, :], start=m == 0, stop=m == n - 1)

            def project_pair(c, e, n, order=range(KT), between={}):
                if e:
                    pe.wait_ge(evac_done, e)
                order = list(order)

                def part(i, k, s):
                    if i == 0:
                        pe.wait_ge(lo_done, c + s + 1)
                    if s == 0 or i >= PAIRED:
                        pe.wait_ge(act_lo_done, 8 * n + i + 1)
                    for j in range(2):
                        last = mm3(acc[:, 2 * s + j, :], *w_tiles((c + s) % 2, k, j),
                                   act_hi[:, k, :], act_lo[:, k, :], i == 0, i == KT - 1)
                        if i == KT - 1:
                            last.then_inc(tile_done[j], 1)

                for i in range(PAIRED):
                    if i in between:
                        between[i]()
                    for s in range(2):
                        part(i, order[i], s)
                for s in range(2):
                    if PAIRED + s in between:
                        between[PAIRED + s]()
                    for i in range(PAIRED, KT):
                        part(i, order[i], s)

            def project_chunks(c, e, order=range(KT)):
                for s in range(2):
                    pe.wait_ge(lo_done, c + (s + 1))
                    for j in range(2):
                        pe.wait_ge(evac_done, e + (2 * s + j - 3))
                        for i, k in enumerate(order):
                            last = mm3(acc[:, 2 * s + j, :], *w_tiles((c_par + s) % 2, k, j),
                                       act_hi[:, k, :], act_lo[:, k, :], i == 0, i == KT - 1)
                        last.then_inc(tile_done[j], 1)

            pe.wait_ge(const_in, 16)
            for b in range(NBLK):
                pe.wait_ge(x_in[b], 16)
                for g in range(2):
                    m = 2 * b + g
                    if m >= 4:
                        pe.wait_ge(resid_done, m - 3)
                    for k in range(4):
                        last = pe.transpose(acc[:, m % 4, k * P:(k + 1) * P],
                                            x_tok[:, b, (4 * g + k) * P:(4 * g + k + 1) * P], ident[:, :])
                    last.then_inc(xT_done, 1)
                if b == 0:
                    pe.wait_ge(vec_in, 16)
                    pe.transpose(ps7[:, 0:V_N], vec_rows[:, :], ident[0:V_N, 0:V_N]).then_inc(vec_ps, 1)
            pe.wait_ge(rel_in, 2 * 16)
            pe.wait_ge(gatew_set, 1)
            pe.matmul(ps6[0:8, :], relw[:, :], hot[:, :], start=True, stop=True).then_inc(relf_ps, 1)

            def token_sums(n):
                pe.wait_ge(sqsum_done, 7 * (n + 1))
                pe.matmul(ps7[:, :], ones[:, :], sq_sum[:, :], start=True, stop=False)
                pe.wait_ge(sq_done, 8 * (n + 1))
                pe.matmul(ps7[:, :], ones[:, :], sq[:, 1, :], start=False, stop=True).then_inc(rsum_done, 1)

            last_in_bank = {}

            def mixer_tile_pe(c, j, half=None):
                e, bank = mixer_tile(c, j)
                ks = range(KT) if half is None else range(4 * half, 4 * half + 4)
                if half == 1:
                    for k in ks:
                        last = mm3(acc[:, bank, :], *w_tiles(c % 2, k, j), act_hi[:, k, :], act_lo[:, k, :],
                                   False, k == KT - 1)
                    last.then_inc(tile_done[j], 1)
                    return
                if j == 0 or c == 3:
                    pe.wait_ge(lo_done, c + 1)
                if bank in last_in_bank:
                    pe.wait_ge(evac_done, last_in_bank[bank] + 1)
                last_in_bank[bank] = e
                for k in ks:
                    if c == 3:
                        wh, wl = w_hi[:, 1, k, 0:P], w_lo[:, 1, k, 0:P]
                    else:
                        wh, wl = w_tiles(c % 2, k, j)
                    last = mm3(acc[:, bank, :], wh, wl, act_hi[:, k, :], act_lo[:, k, :], k == 0, k == KT - 1)
                    if c == 3 and k == KT - 2:
                        last.then_inc(tile_done[0], 1)
                if half is None:
                    last.then_inc(tile_done[j], 1)

            def gla_sum(h):
                pe.wait_ge(ogsq_done, h + 1)
                if h >= 2:
                    pe.wait_ge(rr_done, h - 1)
                elif h == 0:
                    pe.wait_ge(kst_done, 4)
                else:
                    pe.wait_ge(o_done, 4)
                pe.matmul((ps6, ps7)[h % 2][:, :], ones[:, :], sq[:, h % 2, :], start=True, stop=True)\
                  .then_inc(ogsum_done, 1)

            def ps6_free(layer, at):
                pvs, keys = 16 * layer + before(layer, at, "pv"), before(layer, at, "gla_keys")
                if pvs:
                    pe.wait_ge(oq_done, pvs)
                if keys:
                    pe.wait_ge(kst_done, keys)

            def ps7_free(layer, at):
                turns, values = 4 * layer + before(layer, at, "turn"), before(layer, at, "gla_values")
                gates = before(layer, at, "gla_gate")
                pe.wait_ge(vtok_done, layer + 1)
                if turns:
                    pe.wait_ge(o_done, turns)
                if values:
                    pe.wait_ge(vatok_done, values)
                if gates:
                    pe.wait_ge(gx_done, gates)

            def mixer_step_pe(layer, step, at):
                what, i = step[0], step[1]
                if what == "tile":
                    mixer_tile_pe(*step[1:])
                elif what == "pair":
                    if layer == 0:
                        pe.wait_ge(resid_done, KT)
                    project_pair(i, (0, E_AIN)[layer], (0, 3)[layer], between={PAIRED: lambda: token_sums((0, 4)[layer])})
                    last_in_bank.update({0: (0, E_AIN)[layer], 1: (0, E_AIN)[layer] + 1})
                elif what == "keys_values":
                    pe.wait_ge(evac_done, 6 if layer == 0 else E_AIN + 6)
                    pe.wait_ge(r_done, 1 if layer == 0 else 5)
                    for b in range(NBLK):
                        last = pe.transpose(ps7[:, b * P:(b + 1) * P], VT[layer][:, b * P:(b + 1) * P], ident[:, :])
                    last.then_inc(vT_done, 1)
                elif what == "qk":
                    n, hp, k = i // 4, i % 4, 16 * layer + i
                    kbs, _ = window(layer, n)
                    if i == 0:
                        pe.wait_ge(kx_done, 2 * (layer + 1))
                    if k >= 1:
                        pe.wait_ge(logits_done, k)
                    for j in range(2):
                        keys = KH[layer] if hp // 2 == j else KX[layer]
                        h64 = slice(64 * j, 64 * j + 64)
                        last = pe.matmul(acc[:, 2 + j, 0:len(kbs) * P], QH[layer][h64, hp, n * P:(n + 1) * P],
                                         keys[h64, kbs[0] * P:(kbs[-1] + 1) * P], start=True, stop=True)
                    last.then_inc(qk_done, 1)
                elif what == "transpose":
                    n, k = i // 4, 16 * layer + i
                    kbs, _ = window(layer, n)
                    pe.wait_ge(exp_done, 2 * (k + 1))
                    if k >= 1:
                        pe.wait_ge(pTs_done, k)
                    for b in range(len(kbs)):
                        for j in range(2):
                            last = pe.transpose(psTf[:, (2 * b + j) * P:(2 * b + j + 1) * P],
                                                LG[layer][:, i % 2, j, 1 + b * P:1 + (b + 1) * P], ident[:, :])
                    last.then_inc(pT_done, 1)
                elif what == "pv":
                    n, hp, k = i // 4, i % 4, 16 * layer + i
                    g = hp // 2
                    kbs, _ = window(layer, n)
                    pe.wait_ge(pTs_done, k + 1)
                    if i == 0:
                        pe.wait_ge(vtok_done, layer + 1)
                    ps6_free(layer, at)
                    if k == 0:
                        pe.wait_ge(relf_sb, 1)
                    for j in range(2):
                        for b, kb in enumerate(kbs):
                            last = pe.matmul(ps6[:, 64 * j:64 * j + 64],
                                             PT[layer][:, (2 * b + j) * P:(2 * b + j + 1) * P],
                                             VTOK[layer][:, kb, 64 * g:64 * g + 64],
                                             start=b == 0, stop=b == len(kbs) - 1)
                    last.then_inc(pv_done, 1)
                elif what == "turn":
                    pe.wait_ge(oq_done, 16 * layer + 4 * (i + 1))
                    ps7_free(layer, at)
                    for hp in range(4):
                        last = pe.transpose(ps7[:, hp * P:(hp + 1) * P], OQ[layer][:, hp, :], ident[:, :])
                    last.then_inc(oT_done, 1)
                elif what == "gla_values":
                    pe.wait_ge(evac_done, mixer_tile(6 + i // 2, i % 2)[0] + 1)
                    ps7_free(layer, at)
                    for b in range(NBLK):
                        last = pe.transpose(ps7[:, b * P:(b + 1) * P], vaf[:, i % 2, b * P:(b + 1) * P], ident[:, :])
                    last.then_inc(vaT_done, 1)
                elif what == "gla_gate":
                    d, t = i % 2, i // 2
                    if i == 0:
                        pe.wait_ge(mix1_in, 16 * MIX1_LOADS)
                        pe.wait_ge(evac_done, 7)
                    ps7_free(layer, at)
                    pe.matmul(ps7[:, :], gate_w[:, d, t * P:(t + 1) * P], zz[:, :], start=True, stop=True)\
                      .then_inc(gate_ps, 1)
                elif what == "gla_keys":
                    pe.wait_ge(ks_done, i + 1)
                    ps6_free(layer, at)
                    for b in range(NBLK):
                        last = pe.transpose(ps6[:, b * P:(b + 1) * P], bb[:, b * P:(b + 1) * P], ident[:, :])
                    last.then_inc(kT_done, 1)
                elif what == "gla_dS":
                    pe.wait_ge(kst_done, 4)
                    pe.wait_ge(vatok_done, 4)
                    pe.wait_ge(pTs_done, STEPS)
                    pe.wait_ge(logits_done, STEPS)
                    if i == 1:
                        pe.wait_ge(S_done, 14)
                    for d in range(2):
                        dst = acc[:, 2:4, :] if d == 0 else psT
                        for n in range(NCH):
                            if n == (NCH - 1 if d == 0 else 0):
                                continue
                            s64 = slice(64 * (n % 2), 64 * (n % 2) + 64)
                            for hh in range(2):
                                h = 2 * i + hh
                                last = pe.matmul(dst[64 * hh:64 * hh + 64, n % 2, (n // 2) * P:(n // 2 + 1) * P],
                                                 kst(d, i)[s64, n // 2, 64 * hh:64 * hh + 64],
                                                 va_tok[s64, n // 2, h * P:(h + 1) * P], start=True, stop=True)
                    last.then_inc(dS_done, 1)
                elif what == "gla_A":
                    t, h64 = i // 2, slice(64 * (i % 2), 64 * (i % 2) + 64)
                    pe.wait_ge(kint_done, 4)
                    pe.wait_ge(qdec_done, 4)
                    pe.wait_ge(S_done, 28)
                    for d in range(2):
                        if i >= 1:
                            pe.wait_ge(Am_done, 2 * (i - 1) + d + 1)
                        for m in range(NBLK):
                            mm = slice(m * P, (m + 1) * P)
                            last = pe.matmul(acc[:, 2 + d, mm], kint(d, t)[h64, mm], qdec(d, t)[h64, mm],
                                             start=True, stop=True)
                        last.then_inc(A_done, 1)
                elif what == "gla_out":
                    t, h64 = i // 2, slice(64 * (i % 2), 64 * (i % 2) + 64)
                    bank = i % 2
                    pe.wait_ge(Am_done, 2 * i + 2)
                    if i >= 2:
                        pe.wait_ge(og_out, i - 1)
                    for m in range(NBLK):
                        mm = slice(m * P, (m + 1) * P)
                        for d in range(2):
                            pe.matmul(psT[:, bank, mm], va_tok[:, m, i * P:(i + 1) * P], Am[:, i % 2, d, mm],
                                      start=m == 0 and d == 0, stop=False)
                    for n in range(NCH):
                        nn = slice(n * GLA_C, (n + 1) * GLA_C)
                        for d in range(2):
                            if n == (0 if d == 0 else NCH - 1):
                                continue
                            last = pe.matmul(psT[:, bank, nn], S[h64, t, d, n, :], qdec(d, t)[h64, nn],
                                             start=False, stop=n == NCH - 1)
                    last.then_inc(og_done, 1)
                elif what == "gla_sum":
                    gla_sum(i)
                elif what == "pool_out":
                    pe.wait_ge(mix2_in, 16 * MIX2_LOADS)
                    pe.wait_ge(o_done, 8)
                    pe.wait_ge(vtok_done, 2)
                    for g in range(4):
                        pe.wait_ge(pooled_done, g + 1)
                        dst = (ps6[:, :], ps7[:, :], psT[:, 0, :], psT[:, 1, :])[g]
                        pe.matmul(dst, pw[:, g, :], pooled[:, g, :], start=True, stop=True).then_inc(yb_ps, 1)

            for at, step in enumerate(STEPS_OF[0]):
                mixer_step_pe(0, step, at)
            order = (4, 5, 6, 7, 0, 1, 2, 3)
            c_par = 0
            pe.wait_ge(Am_done, 8)
            project_pair(C_WOUT, E_WOUT, 1, order, {1: lambda: gla_sum(3)})
            project_chunks(C_WOUT + 2, E_WOUT + 4, order)
            token_sums(1)
            keep_clock(BOUNDARY_FILL)
            project_pair(C_UP0, E_UP0, 2, between={PAIRED: lambda: token_sums(2)})
            for half in range(2):
                if half == 0:
                    with pe.Fori(0, 3) as i:
                        project_chunks(i * 2 + (C_UP0 + 2), i * 4 + (E_UP0 + 4))
                else:
                    with pe.Fori(0, 4) as i:
                        project_chunks(i * 2 + C_UP1, i * 4 + E_UP1)
                c0, e0 = (C_DN0, E_DN0) if half == 0 else (C_DN1, E_DN1)
                with pe.Fori(0, 2) as i:
                    for pair in range(2):
                        for kg in range(2):
                            pe.wait_ge(hlo_done, HID * half + 8 * (kg + 1))
                            pe.wait_ge(lo_done, i * 4 + (c0 + 2 * pair + kg + 1))
                            for j in range(2):
                                bank = 2 * pair + j
                                if kg == 0:
                                    pe.wait_ge(evac_done, i * 4 + (e0 + bank - 3))
                                for k in range(KT):
                                    last = mm3(acc[:, bank, :], *w_tiles(kg, k, j), hid_hi[:, 8 * kg + k, :],
                                               hid_lo[:, 8 * kg + k, :], kg == 0 and k == 0, kg == 1 and k == KT - 1)
                                last.then_inc(tile_done[j], 1)
            token_sums(3)
            keep_clock(BOUNDARY_FILL)
            for at, step in enumerate(STEPS_OF[1]):
                mixer_step_pe(1, step, at)
            c_par = C_ABOUT
            project_pair(C_ABOUT, E_ABOUT, 4)
            project_chunks(C_ABOUT + 2, E_ABOUT + 4)
            token_sums(5)
            keep_clock(BOUNDARY_FILL)
            c_par = C_CAB

            def turn_taps():
                pe.wait_ge(taps_in, 16)
                for k in range(KT):
                    last = pe.transpose(ps6[:, k * TAPS:(k + 1) * TAPS], tap_rows[:, k * P:(k + 1) * P],
                                        ident[0:TAPS, 0:TAPS])
                last.then_inc(taps_ps, 1)

            project_pair(C_CAB, E_CAB, 5, between={PAIRED: lambda: token_sums(6), PAIRED + 1: turn_taps})
            with pe.Fori(0, TURN_CHUNKS - 1) as i:
                project_chunks(i * 2 + (C_CAB + 2), i * 4 + (E_CAB + 4))
            for k in range(KT):
                if k == KT - 1:
                    pe.wait_ge(vacc_step, KT * (DVE_TAPS + 1) - 5)
                    keep_clock(8)
                pe.wait_ge(conv_step, k + 2)
                last = pe.matmul(ps6[:, :], ones[:, :], conv[:, k, :], start=k == 0, stop=k == KT - 1)
            last.then_inc(musum_done, 1)
            for k in range(KT):
                pe.wait_ge(sq_done, 8 * 7 + k + 1)
                pe.matmul(ps7[:, :], ones[:, :], sq[:, k % 2, :], start=k == 0, stop=k == KT - 1)\
                  .then_inc(sqsum_done if k < KT - 1 else rsum_done, 1)
            keep_clock(BOUNDARY_FILL)
            project_pair(C_COUT, E_COUT, 6)
            project_chunks(C_COUT + 2, E_COUT + 4)
            token_sums(8)
            keep_clock(BOUNDARY_FILL)
            for f in range(2 * NBLK):
                b, half = f // 2, f % 2
                pe.wait_ge(resid_done, 5 * KT if b else 4 * KT + 4 * (half + 1))
                if f >= 4:
                    pe.wait_ge(fo_done[f % 2], f // 2 - 1)
                for k in range(4):
                    last = pe.transpose(acc[:, f % 4, k * P:(k + 1) * P],
                                        resid[:, 4 * half + k, b * P:(b + 1) * P], ident[:, :])
                last.then_inc(fT_done, 1)

        @block.gpsimd
        def _(pool):
            chain = Chain(pool, pool_step)
            pool.memset(eps[:, :], EPS).then_inc(eps_set, 1)
            pool.wait_ge(eps_set, 1)
            chain.link(pool.memset(relw[32:33, :], -1e30))
            pool.memset(gate_w[:, :, :], 0.0).then_inc(gatew_set, 1)
            pool.wait_ge(gatew_set, 1)

            def sum_squares(n):
                for k in range(KT - 1):
                    pool.wait_ge(sq_done, 8 * n + k + 1)
                    if k == 0:
                        if n >= 1:
                            pool.wait_ge(rsum_done, n)
                        pool.tensor_copy(sq_sum[:, :], sq[:, k % 2, :]).then_inc(sqsum_done, 1)
                    else:
                        pool.wait_ge(sqsum_done, 7 * n + k)
                        pool.tensor_tensor(sq_sum[:, :], sq_sum[:, :], sq[:, k % 2, :], ALU.add)\
                            .then_inc(sqsum_done, 1)

            def split(c):
                pool.wait_ge(hi_done, c + 1)
                pool.wait_ge(lo_done, c)
                pool.tensor_tensor(w_lo[:, c % 2, :, :], raw[:, c % 2, :, :], w_hi[:, c % 2, :, :].bitcast(F32),
                                   ALU.subtract).then_inc(lo_done, 1)

            def mixer_step_pool(layer, step):
                what, i = step[0], step[1]
                k = 16 * layer + i
                if what == "gla_scaled":
                    d, t = i % 2, i // 2
                    pool.wait_ge(evac_done, 10 + t)
                    pool.wait_ge(eb_done, i + 1)
                    if d == 0:
                        pool.wait_ge(enb_done, i + 1)
                        pool.tensor_tensor(kint(d, t), ka[:, t, :], gx[:, :], ALU.mult).then_inc(kint_done, 1)
                    pool.wait_ge(ek_done, i + 1)
                    pool.tensor_tensor(bb[:, :], ka[:, t, :], gl[:, :], ALU.mult).then_inc(ks_done, 1)
                    if d == 1:
                        pool.wait_ge(ks_done, i + 1)
                        pool.tensor_tensor(kint(d, t), ka[:, t, :], gx[:, :], ALU.mult).then_inc(kint_done, 1)
                elif what == "gla_dS" and i == 0:
                    pool.wait_ge(vtok_done, 1)
                    pool.wait_ge(pv_done, STEPS)
                    pool.memset(Am[:, :, :, :], 0.0).then_inc(Am_set, 1)
                elif what == "pool_window":
                    pool.wait_ge(evac_done, E_AIN + 2 * (5 + i // 2) + i % 2 + 1)
                    if i == 0:
                        pool.wait_ge(upad_set, 1)
                        pool.wait_ge(mix2_in, 16 * MIX2_LOADS)
                    else:
                        pool.wait_ge(pooled_done, i)
                    src = uu[:, i, :]
                    for m in range(i + 1):
                        sh, lo = 1 << m, (2 << m) - 1
                        dst = wsum[:, m % 2, :]
                        chain.link(pool.tensor_tensor(dst[:, lo:], src[:, lo:], src[:, lo - sh:UPAD + TOK - sh], ALU.add))
                        src = dst
                    pool.tensor_tensor(src[:, UPAD:UPAD + 16], src[:, UPAD:UPAD + 16], wcnt[:, i, :], ALU.mult)\
                        .then_inc(wsum_done, 1)

            split(1)
            sum_squares(0)
            for step in STEPS_OF[0]:
                mixer_step_pool(0, step)
            sum_squares(1)
            split(C_UP0 + 1)
            sum_squares(2)
            sum_squares(3)
            split(C_AIN + 1)
            sum_squares(4)
            pool.memset(uu[:, :, 0:UPAD], 0.0).then_inc(upad_set, 1)
            for step in STEPS_OF[1]:
                mixer_step_pool(1, step)
            sum_squares(5)
            split(C_CAB + 1)
            pool.memset(glu[:, 0, 0:CPAD], 0.0).then_inc(glu_done, 1)
            pool.memset(glu[:, 1, 0:CPAD], 0.0).then_inc(pacc_step, ADDS)
            sum_squares(6)
            with pool.Fori(0, 2) as i:
                def gated(t):
                    pool.wait_ge(sig_done, i * TURN_TILES + (t + 1))
                    pool.wait_ge(conv_step, i * TURN_TILES + (max(t - 1, 0) + 1))
                    pool.tensor_tensor(glu[:, t % 2, CPAD:], ab[:, 0, :], ab[:, 1, :], ALU.mult).then_inc(glu_done, 1)

                for t in range(TURN_TILES):
                    work = [(x * ADDS // DVE_TAPS + 1, TURN_AB[s]) for x, s in TURN_WORK[t] if s in TURN_AB]
                    for m in range(1, ACT_TAPS):
                        for x, tile in work:
                            if m == (x + 3 if x > 1 else 1):
                                gated(tile)
                        g = ACT_TAPS * t + m
                        pool.wait_ge(prod_done, i * (TURN_TILES * ACT_TAPS) + (g + 2))
                        if m == 1:
                            pool.wait_ge(conv_step, i * TURN_TILES + (t + 1))
                            pool.tensor_tensor(pacc[:, :], prod[:, (g - 1) % 4, :], prod[:, g % 4, :], ALU.add)\
                                .then_inc(pacc_step, 1)
                        else:
                            pool.wait_ge(pacc_step, i * (TURN_TILES * ADDS) + (ADDS * (t + 1) + m - 1))
                            pool.tensor_tensor(pacc[:, :], pacc[:, :], prod[:, g % 4, :], ALU.add)\
                                .then_inc(pacc_step, 1)
            sum_squares(8)
            pool.wait_ge(r_done, 9)
            for k in range(1, KT, 2):
                if k >= 5:
                    pool.wait_ge(resid_done, 4 * KT + k - 3)
                pool.tensor_tensor(ty_c[:, 2 * (k // 2 % 2) + 1, :], y[:, k, :], R[:, :], ALU.mult).then_inc(ty_done, 1)

        @block.scalar
        def _(act):
            chain = Chain(act, act_step)

            def exp_ln_tables():
                nc.scalar.preload_act_table_set("natural_log_exp_and_others")

            exp_ln_tables()
            act.dma_start(ident_ones[:, :], a["shapes"][:, 0:2 * P]).then_inc(const_in, 16)
            act.dma_start(vec_rows[:, :], a["vectors"]).then_inc(vec_in, 16)
            act.dma_start(relw[0:32, :], a["rel_bias"]).then_inc(rel_in, 16)
            act.dma_start(hot[:, :], a["onehot"]).then_inc(rel_in, 16)

            def split(c):
                slot = (c if isinstance(c, int) else c_par) % 2
                if isinstance(c, int):
                    act.wait_ge(raw_ready[slot], 32 * (c // 2 + 1))
                    if c >= 2:
                        act.wait_ge(tile_done[1], c - 1)
                else:
                    act.wait_ge(raw_ready[slot], c * 16 + 16 * (2 - slot))
                    act.wait_ge(tile_done[1], c - 1)
                if isinstance(c, int) and c == 3:
                    act.activation(w_hi[:, slot, :, 0:P], raw[:, slot, :, 0:P], ACT.Copy).then_inc(hi_done, 1)
                else:
                    act.activation(w_hi[:, slot, :, :], raw[:, slot, :, :], ACT.Copy).then_inc(hi_done, 1)

            def square(n, k, src):
                if k >= 2 or (k == 0 and n >= 1):
                    act.wait_ge(sqsum_done, 7 * n + max(k - 1, 0))
                elif n >= 1:
                    act.wait_ge(rsum_done, n)
                act.activation(sq[:, k % 2, :], src, ACT.Square).then_inc(sq_done, 1)

            def token_scale(n):
                act.wait_ge(rsum_done, n + 1)
                chain.link(act.activation(R[:, :], ps7[:, :], ACT.Ln, bias=eps[:, 0:1], scale=1.0 / D))
                act.activation(R[:, :], R[:, :], ACT.Exp, scale=-0.5).then_inc(r_done, 1)

            def boundary(n, gain):
                for k in range(KT):
                    act.wait_ge(resid_done, 8 * n + k + 1 if n else KT)
                    if n == 0 and k == 0:
                        split(1)
                    act.activation(act_hi[:, k, :], resid[:, k, :], ACT.Copy, scale=vec[:, gain + k:gain + k + 1])\
                       .then_inc(act_hi_done, 1)
                    square((0, 2, 4, 6)[n], k, resid[:, k, :])

            def halves(tensor, order, wait):
                for k in order:
                    wait(act, k)
                    act.activation(act_hi[:, k, :], tensor[:, k, :], ACT.Copy).then_inc(act_hi_done, 1)

            def mixer_step_act(layer, step):
                what, i = step[0], step[1]
                k = 16 * layer + i
                if what in ("split", "split_hi"):
                    split(i)
                elif what == "keys_values":
                    act.wait_ge(evac_done, 6 if layer == 0 else E_AIN + 6)
                    act.activation(KX[layer][64:128, :], KH[layer][0:64, :], ACT.Copy).then_inc(kx_done, 1)
                    act.activation(KX[layer][0:64, :], KH[layer][64:128, :], ACT.Copy).then_inc(kx_done, 1)
                    act.wait_ge(vT_done, layer + 1)
                    act.activation(VTOK[layer][:, :, :], ps7[:, :].rearrange("p (b n) -> p b n", b=NBLK), ACT.Copy)\
                       .then_inc(vtok_done, 1)
                elif what == "softmax":
                    w = len(window(layer, i // 4)[0]) * P + 1
                    act.wait_ge(negmax_done, k + 1)
                    for j in range(2):
                        row = LG[layer][:, i % 2, j, 0:w]
                        act.activation(row, row, ACT.Exp, bias=SM[layer][:, i % 2, j, 1:2],
                                       accum_out=SM[layer][:, i % 2, j, 2:3]).then_inc(exp_done, 1)
                elif what == "transpose":
                    w = len(window(layer, i // 4)[0]) * 2 * P
                    act.wait_ge(pT_done, k + 1)
                    if k >= 1:
                        act.wait_ge(pv_done, k)
                    act.activation(PT[layer][:, 0:w], psTf[:, 0:w], ACT.Copy).then_inc(pTs_done, 1)
                elif what == "turn":
                    o0 = o_tile(layer, 0)
                    act.wait_ge(oT_done, 4 * layer + i + 1)
                    act.activation(OO[layer][:, o0:o0 + 4, i * P:(i + 1) * P],
                                   ps7[:, :].rearrange("p (h n) -> p h n", h=4), ACT.Copy).then_inc(o_done, 1)
                elif what == "gla_values":
                    act.wait_ge(vaT_done, i + 1)
                    act.activation(va_tok[:, :, i * P:(i + 1) * P], ps7[:, :].rearrange("p (b n) -> p b n", b=NBLK),
                                   ACT.Copy).then_inc(vatok_done, 1)
                elif what == "gla_gate":
                    d, t = i % 2, i // 2
                    act.wait_ge(gx_done, i + 1)
                    if i >= 1:
                        act.wait_ge(ks_done, i)
                    chain.link(act.activation(gl[:, :], gx[:, :], ACT.Abs))
                    chain.link(act.activation(gl[:, :], gl[:, :], ACT.Exp, scale=-1.0))
                    act.activation(gl[:, :], gl[:, :], ACT.Ln, bias=1.0).then_inc(ln_done, 1)
                elif what == "gla_decay":
                    act.wait_ge(bb_done, i + 1)
                    if i >= 1:
                        act.wait_ge(qdec_done, i)
                        act.wait_ge(decay_done, i)
                    act.activation(eb[:, :], bb[:, :], ACT.Exp, scale=1.0 / GATE_NORM).then_inc(eb_done, 1)
                    act.activation(gx[:, :], bb[:, :], ACT.Exp, scale=-1.0 / GATE_NORM).then_inc(enb_done, 1)
                    act.wait_ge(dk_done, i + 1)
                    act.activation(gl[:, :], gl[:, :], ACT.Exp, scale=1.0 / GATE_NORM).then_inc(ek_done, 1)
                elif what == "gla_keys":
                    act.wait_ge(kT_done, i + 1)
                    act.activation(kst(i % 2, i // 2), ps6[:, :].rearrange("p (b n) -> p b n", b=NBLK), ACT.Copy)\
                       .then_inc(kst_done, 1)
                elif what == "gla_out":
                    act.wait_ge(og_done, i + 1)
                    act.activation(o1[:, i, :], psT[:, i % 2, :], ACT.Copy).then_inc(og_out, 1)
                    act.wait_ge(og_out, i + 1)
                    if i >= 2:
                        act.wait_ge(ogsum_done, i - 1)
                    act.activation(sq[:, i % 2, :], o1[:, i, :], ACT.Square).then_inc(ogsq_done, 1)
                elif what == "gla_sum":
                    head_scale(i)
                elif what == "attention_halves":
                    act.wait_ge(evac_done, E_WOUT)
                    halves(o1, (4, 5), lambda e, k: e.wait_ge(o_done, 4))
                    split(11)
                    halves(o1, (6, 7), lambda e, k: e.wait_ge(o_done, 4))
                elif what == "attention_gate":
                    act.wait_ge(evac_done, E_AIN + 10)
                    for h in range(4):
                        act.activation(ga2[:, h, :], ga2[:, h, :], ACT.Silu).then_inc(silu2_done, 1)
                elif what == "pool_out":
                    act.wait_ge(evac_done, E_ABOUT)
                    halves(o2, (0, 1), lambda e, k: e.wait_ge(ob_done, k + 1))
                    split(56)
                    halves(o2, (2, 3), lambda e, k: e.wait_ge(ob_done, k + 1))
                    for h in range(4):
                        act.activation(gb2[:, h, :], gb2[:, h, :], ACT.Silu).then_inc(silu2_done, 1)
                    exp_ln_tables()
                    halves(o2, (4, 5, 6, 7), lambda e, k: e.wait_ge(ob_done, k + 1))

            def head_scale(h):
                rr = (bb, eb)[h % 2]
                act.wait_ge(ogsum_done, h + 1)
                if h >= 2:
                    act.wait_ge(on_done, h - 1)
                chain.link(act.activation(rr[:, :], (ps6, ps7)[h % 2][:, :], ACT.Ln, bias=eps[:, 0:1], scale=1.0 / P))
                act.activation(rr[:, :], rr[:, :], ACT.Exp, scale=-0.5).then_inc(rr_done, 1)

            split(0)
            act.wait_ge(vec_ps, 1)
            act.activation(vec[:, :], ps7[:, 0:V_N], ACT.Copy).then_inc(vec_done, 1)
            act.wait_ge(vec_done, 1)
            boundary(0, V_PRE1)
            act.wait_ge(relf_ps, 1)
            act.activation(relF[:, :], ps6[0:8, :], ACT.Copy).then_inc(relf_sb, 1)
            act.wait_ge(relf_sb, 1)
            act.dma_start(relF_dram, relF[:, :].rearrange("h (r n) -> h r n", r=1).to_broadcast([8, REPEAT, TOK]))\
               .then_inc(relf_out, 16)
            act.wait_ge(relf_out, 16)
            for group in range(P // REPEAT):
                act.dma_start(bias1[group * REPEAT:(group + 1) * REPEAT, :, :],
                              bass.AP(relF_dram.tensor, P - 1 - group * REPEAT,
                                      [[TOK - 1, REPEAT], [REPEAT * TOK, 8], [1, BAND1]])).then_inc(bias1_in, 16)
            act.dma_start(sink1[:, :], bass.AP(a["swa_sink"].tensor, 0, [[0, P], [1, 8]])).then_inc(mix1_in, 16)
            act.dma_start(masks[:, :, :], a["shapes"][:, 2 * P:4 * P].rearrange("p (d n) -> p d n", d=2))\
               .then_inc(mix1_in, 16)
            act.dma_start(restart[:, :], a["shapes"][:, 4 * P:4 * P + TOK]).then_inc(mix1_in, 16)
            act.wait_ge(gatew_set, 1)
            act.dma_start(gate_w[0:16, 0, :], a["w_gate_up_fwd"][0]).then_inc(mix1_in, 16)
            act.dma_start(gate_w[16:32, 1, :], a["w_gate_up_bwd"][0]).then_inc(mix1_in, 16)
            token_scale(0)
            for step in STEPS_OF[0]:
                mixer_step_act(0, step)
            head_scale(3)
            for h in range(4):
                act.activation(ga[:, h, :], ga[:, h, :], ACT.Silu).then_inc(silu_done, 1)
            exp_ln_tables()
            halves(o1, (0, 1, 2, 3), lambda e, k: e.wait_ge(og_gated, k + 1))

            c_par = 0

            def plain_turns(c0, turns):
                nonlocal c_par
                c_par = c0 + 1
                with act.Fori(0, turns) as i:
                    for s in range(2):
                        c_par = c0 + s + 1
                        split(i * 2 + (c0 + s + 1))

            def out_squares(n, c, e):
                for k in range(KT):
                    if k in (0, 2, 4) and c + 2 + k // 2 < C_END:
                        split(c + 2 + k // 2)
                    if k < KT - 1:
                        act.wait_ge(evac_done, e + k + 1)
                        square(n, k, y[:, k, :])
                    else:
                        act.wait_ge(tile_done[1], c + 4)
                        square(n, k, acc[:, 3, :])
                if c + 5 < C_END:
                    split(c + 5)

            out_squares(1, C_WOUT, E_WOUT)
            token_scale(1)
            boundary(1, V_PREM)
            token_scale(2)
            for half in range(2):
                cu, cd = (C_UP0, C_DN0) if half == 0 else (C_UP1, C_DN1)
                peeled = half == 0
                m0 = HID * half
                e_off = (E_UP0 if half == 0 else E_UP1 - HID)

                def up_tile(h_slot, idx, hid_ap, ring_used):
                    act.wait_ge(evac_done, idx + (e_off + 1))
                    if ring_used:
                        act.wait_ge(hlo_done, idx - 1)
                    act.activation(zq[:, h_slot, :], zt[:, h_slot, :], ACT.Square).then_inc(zq_done, 1)
                    act.wait_ge(zq_done, idx + 1)
                    act.wait_ge(eps_set, 1)
                    act.activation(hid_ap, zq[:, h_slot, :], ACT.Copy).then_inc(hhi_done, 1)

                first = 0
                if half == 0:
                    for s in range(2):
                        if s == 0:
                            split(cu + 2)
                        for j in range(2):
                            up_tile(j, 2 * s + j, hid_hi[:, 2 * s + j, :], 2 * s + j >= 2)
                    first = 1
                else:
                    c_par = cu
                with act.Fori(0, 4 - first) as i:
                    for s in range(2):
                        c_par = cu + s + 1
                        split(i * 2 + (cu + 2 * first + s + 1))
                        for j in range(2):
                            up_tile(j, i * 4 + (m0 + 4 * first + 2 * s + j),
                                    hid_hi[:, bass.ds(i * 4 + (4 * first + 2 * s + j), 1), :], True)
                if half == 0:
                    plain_turns(cd, 4)
                else:
                    for p in range(4):
                        split(cd + 2 * p + 1)
                        split(cd + 2 * p + 2)
                        for j in range(2):
                            act.wait_ge(evac_done, E_DN1 + 2 * p + j + 1)
                            square(3, 2 * p + j, y[:, 2 * p + j, :])
                    split(C_AIN + 1)
            token_scale(3)
            boundary(2, V_PRE2A)
            token_scale(4)
            act.dma_start(sink2[:, :], bass.AP(a["a_sinks_2"].tensor, 0, [[0, P], [1, 8]])).then_inc(mix2_in, 16)
            act.dma_start(bias2[:, :, :], a["alibi"]).then_inc(mix2_in, 16)
            act.dma_start(pw[:, :, :], a["b_pool_w_2"][0].rearrange("g c d -> c g d")).then_inc(mix2_in, 16)
            act.dma_start(wcnt[:, :, :], a["shapes"][:, 4 * P + TOK:4 * P + TOK + 64]
                          .rearrange("p (g n) -> p g n", g=4)).then_inc(mix2_in, 16)
            for step in STEPS_OF[1]:
                mixer_step_act(1, step)
            out_squares(5, C_ABOUT, E_ABOUT)
            token_scale(5)
            act.dma_start(tap_rows[:, :], a["c_dw_w_2"][0, :, 0, :]).then_inc(taps_in, 16)
            boundary(3, V_PRE2B)
            token_scale(6)
            act.wait_ge(taps_ps, 1)
            act.activation(taps[:, :, :], ps6[:, 0:KT * TAPS].rearrange("p (k t) -> p k t", k=KT), ACT.Copy)\
               .then_inc(taps_done, 1)
            with act.Fori(0, 2) as i:
                for t in range(TURN_TILES):
                    work = [(x * ACT_TAPS // DVE_TAPS, s) for x, s in TURN_WORK[t]]
                    for m in range(ACT_TAPS):
                        for x, s in work:
                            if m == (x + 3 if x else 0) and s in TURN_AB:
                                act.wait_ge(evac_done, i * (2 * TURN_CHUNKS) + (E_CAB + 2 * s + 2))
                                act.activation(ab[:, 1, :], ab[:, 1, :], ACT.Sigmoid).then_inc(sig_done, 1)
                            if m == (x + 1 if x else 0):
                                c_par = C_CAB + s + 2
                                split(i * TURN_CHUNKS + (C_CAB + s + 2))
                        if m == 0:
                            act.wait_ge(glu_done, i * TURN_TILES + (t + 2))
                            act.wait_ge(tapw_done, i * 2 + 2)
                        g = ACT_TAPS * t + m - 4
                        act.wait_ge(pacc_step, i * (TURN_TILES * ADDS)
                                    + (ADDS * (g // ACT_TAPS + 1) + max(1, g % ACT_TAPS)))
                        act.activation(prod[:, (g + 4) % 4, :], glu[:, t % 2, DVE_TAPS + m:DVE_TAPS + m + TOK],
                                       ACT.Copy, scale=tapw[:, t, DVE_TAPS + m:DVE_TAPS + m + 1])\
                           .then_inc(prod_done, 1)
            act.wait_ge(evac_done, E_COUT)
            act.activation(gate[:, :, :], gate[:, :, :], ACT.Silu).then_inc(gsilu_done, 1)
            exp_ln_tables()
            act.wait_ge(musum_done, 1)
            act.activation(mu[:, :], ps6[:, :], ACT.Copy, scale=1.0 / D).then_inc(mu_done, 1)
            for k in range(KT):
                act.wait_ge(cen_done, k + 1)
                square(7, k, conv[:, k, :])
            token_scale(7)
            for k in range(KT):
                act.wait_ge(cn_done, k + 1)
                act.activation(conv[:, k, :], conv[:, k, :], ACT.Silu, bias=vec[:, V_LNB + k:V_LNB + k + 1],
                               scale=vec[:, V_LNG + k:V_LNG + k + 1]).then_inc(csilu_done, 1)
                if k >= 1:
                    act.wait_ge(yc_done, k)
                    act.activation(act_hi[:, k - 1, :], yc[:, (k - 1) % 2, :], ACT.Copy).then_inc(act_hi_done, 1)
            act.wait_ge(yc_done, KT)
            act.activation(act_hi[:, KT - 1, :], yc[:, (KT - 1) % 2, :], ACT.Copy).then_inc(act_hi_done, 1)
            exp_ln_tables()
            out_squares(8, C_COUT, E_COUT)
            token_scale(8)
            for f in range(0, 2 * NBLK, 2):
                act.wait_ge(fT_done, f + 1)
                act.activation(o_tok[:, f, :], acc[:, f % 4, :], ACT.Copy).then_inc(fo_done[0], 1)

        @block.vector
        def _(dve):
            chain = Chain(dve, dve_step)
            c_par = 0

            def split(c):
                slot = (c if isinstance(c, int) else c_par) % 2
                cols = slice(0, P) if isinstance(c, int) and c == 3 else slice(0, CW)
                dve.wait_ge(hi_done, c + 1)
                dve.tensor_tensor(w_lo[:, slot, :, cols], raw[:, slot, :, cols],
                                  w_hi[:, slot, :, cols].bitcast(F32), ALU.subtract).then_inc(lo_done, 1)

            def evac_scaled(c, j, bank, dst, rows=P):
                dve.wait_ge(tile_done[j], c + 1)
                dve.tensor_tensor(dst, acc[0:rows, bank, :], R[0:rows, :], ALU.mult).then_inc(evac_done, 1)

            def lo_of_scaled(n, k, gain):
                dve.wait_ge(act_hi_done, 8 * (0, 2, 3, 5)[n] + k + 1)
                dve.scalar_tensor_tensor(out=act_lo[:, k, :], in0=resid[:, k, :],
                                         scalar=vec[:, gain + k:gain + k + 1],
                                         in1=act_hi[:, k, :].bitcast(F32), op0=ALU.mult, op1=ALU.subtract)\
                   .then_inc(act_lo_done, 1)

            def boundary(n, post, gain, tmp):
                for k in range(KT):
                    if k == 0:
                        dve.wait_ge(r_done, 2 * n)
                    slot = k % 2 if n < 4 else k % 4
                    if n == 4 and k % 2:
                        dve.wait_ge(ty_done, k // 2 + 1)
                    else:
                        chain.link(dve.tensor_tensor(tmp[:, slot, :], y[:, k, :], R[:, :], ALU.mult))
                    dve.scalar_tensor_tensor(out=resid[:, k, :], in0=tmp[:, slot, :],
                                             scalar=vec[:, post + k:post + k + 1], in1=resid[:, k, :],
                                             op0=ALU.mult, op1=ALU.add).then_inc(resid_done, 1)
                    if gain is not None and k >= 1:
                        lo_of_scaled(n, k - 1, gain)
                if gain is not None:
                    lo_of_scaled(n, KT - 1, gain)

            def lower_halves(tensor, order, n, first):
                for m, k in enumerate(order):
                    dve.wait_ge(act_hi_done, 8 * n + first + m + 1)
                    dve.tensor_tensor(act_lo[:, k, :], tensor[:, k, :], act_hi[:, k, :].bitcast(F32), ALU.subtract)\
                       .then_inc(act_lo_done, 1)

            def mixer_tile_dve(c, j):
                e, bank = mixer_tile(c, j)
                if c == 0 and j == 0:
                    dve.wait_ge(r_done, 1)
                if c == C_AIN and j == 0:
                    dve.wait_ge(r_done, 5)
                if c < 2:
                    dst = qs1[:, 2 * c + j, :]
                elif c == 2:
                    dst = (k1, v1)[j][:, :]
                elif c == 3:
                    dst = zz[:, :]
                elif c < 6:
                    if c == 4 and j == 0:
                        dve.wait_ge(relf_out, 16)
                    dst = (qa, ka)[c - 4][:, j, :]
                elif c < 8:
                    h = 2 * (c - 6) + j
                    if h >= 2:
                        dve.wait_ge(vaT_done, h - 1)
                    dst = vaf[:, h % 2, :]
                elif c < 10:
                    dst = ga[:, 2 * (c - 8) + j, :]
                else:
                    i, t = (c - C_AIN) // 2, 2 * ((c - C_AIN) % 2) + j
                    m = c - C_AIN
                    if m < 2:
                        dst = q2[:, 2 * m + j, :]
                    elif m == 2:
                        dst = (k2, v2)[j][:, :]
                    elif m < 5:
                        dst = ga2[:, 2 * (m - 3) + j, :]
                    elif m < 7:
                        dst = uu[:, 2 * (m - 5) + j, UPAD:]
                    else:
                        dst = gb2[:, 2 * (m - 7) + j, :]
                evac_scaled(c, j, bank, dst, 32 if c == 3 else P)

            def mixer_step_dve(layer, step):
                what, i = step[0], step[1]
                k = 16 * layer + i
                if what in ("split", "split_lo"):
                    split(i)
                elif what in ("tile", "evacuate"):
                    if step[3:] != (0,):
                        mixer_tile_dve(step[1], step[2])
                elif what == "softmax":
                    n, hp = i // 4, i % 4
                    kbs, b0 = window(layer, n)
                    w = len(kbs) * P
                    lg, sm = LG[layer][:, i % 2, :, :], SM[layer][:, i % 2, :, :]
                    if i == 0 and layer == 0:
                        dve.wait_ge(bias1_in, 16 * (P // REPEAT))
                        dve.wait_ge(mix1_in, 16 * MIX1_LOADS)
                    if i == 0 and layer == 1:
                        dve.wait_ge(mix2_in, 16 * MIX2_LOADS)
                    dve.wait_ge(qk_done, k + 1)
                    if i >= 2:
                        dve.wait_ge(pT_done, k - 1)
                    dve.tensor_copy(lg[:, :, 0], SINK[layer][:, 2 * hp:2 * hp + 2]).then_inc(sink_set, 1)
                    dve.scalar_tensor_tensor(out=lg[:, :, 1:1 + w], in0=acc[:, 2:4, 0:w], scalar=QSCALE,
                                             in1=BIAS[layer][:, 2 * hp:2 * hp + 2, b0:b0 + w],
                                             op0=ALU.mult, op1=ALU.add).then_inc(logits_done, 1)
                    dve.wait_ge(logits_done, k + 1)
                    dve.wait_ge(sink_set, k + 1)
                    chain.link(dve.tensor_reduce(sm[:, :, 0], lg[:, :, 0:1 + w], AX.X, ALU.max))
                    dve.tensor_scalar(sm[:, :, 1], sm[:, :, 0], -1.0, None, ALU.mult).then_inc(negmax_done, 1)
                elif what == "pv":
                    dve.wait_ge(exp_done, 2 * (k + 1))
                    sm = SM[layer][:, i % 2, :, :]
                    chain.link(dve.reciprocal(sm[:, :, 3:4], sm[:, :, 2:3]))
                    dve.wait_ge(pv_done, k + 1)
                    if i % 4 == 0 and k >= 4:
                        dve.wait_ge(oT_done, k // 4)
                    dve.tensor_tensor(OQ[layer][:, i % 4, :].rearrange("p (j d) -> p j d", j=2),
                                      ps6[:, 0:P].rearrange("p (j d) -> p j d", j=2),
                                      sm[:, :, 3:4].to_broadcast([P, 2, 64]), ALU.mult).then_inc(oq_done, 1)
                elif what == "gla_gate":
                    d, t = i % 2, i // 2
                    bias = vec[:, (V_BF, V_BB)[d] + t:(V_BF, V_BB)[d] + t + 1]
                    dve.wait_ge(gate_ps, i + 1)
                    if i >= 1:
                        dve.wait_ge(kint_done, i)
                    dve.tensor_scalar(gx[:, :], ps7[:, :], bias, None, ALU.add).then_inc(gx_done, 1)
                elif what == "gla_decay":
                    d, t = i % 2, i // 2
                    rev = slice(None, None, -1 if d else 1)
                    dve.wait_ge(ln_done, i + 1)
                    chain.link(dve.scalar_tensor_tensor(out=gx[:, :], in0=gx[:, :], scalar=0.0, in1=gl[:, :],
                                                        op0=ALU.min, op1=ALU.subtract))
                    if i == 0:
                        dve.wait_ge(mix1_in, 16 * MIX1_LOADS)
                    else:
                        dve.wait_ge(kT_done, i)
                    dve.tensor_tensor_scan(bb[:, rev], restart[:, :], gx[:, rev], 0.0, ALU.mult, ALU.add)\
                       .then_inc(bb_done, 1)
                    dve.wait_ge(bb_done, i + 1)
                    end = GLA_C - 1 if d == 0 else 0
                    b3 = bb[:, :].rearrange("p (n c) -> p n c", c=GLA_C)
                    dve.tensor_tensor(gl[:, :].rearrange("p (n c) -> p n c", c=GLA_C),
                                      b3[:, :, end:end + 1].to_broadcast([P, NCH, GLA_C]), b3, ALU.subtract)\
                       .then_inc(dk_done, 1)
                elif what == "gla_scaled":
                    d, t = i % 2, i // 2
                    end = GLA_C - 1 if d == 0 else 0
                    dve.wait_ge(eb_done, i + 1)
                    dve.tensor_copy(decay[:, d, t, :], eb[:, :].rearrange("p (n c) -> p n c", c=GLA_C)[:, :, end])\
                       .then_inc(decay_done, 1)
                    if d == 1:
                        dve.wait_ge(qdec_done, i)
                    dve.scalar_tensor_tensor(out=qdec(d, t), in0=qa[:, t, :], scalar=QSCALE, in1=eb[:, :],
                                             op0=ALU.mult, op1=ALU.mult).then_inc(qdec_done, 1)
                elif what == "gla_dS":
                    dve.wait_ge(dS_done, i + 1)
                    dve.wait_ge(decay_done, 4)
                    count = 14 * i
                    for m in range(NCH - 1):
                        for d in range(2):
                            n = m if d == 0 else NCH - 1 - m
                            to = n + 1 if d == 0 else n - 1
                            src = (acc[:, 2:4, :] if d == 0 else psT)[:, n % 2, (n // 2) * P:(n // 2 + 1) * P]
                            if m == 0:
                                ins = dve.tensor_copy(S[:, i, d, to, :], src)
                            else:
                                dve.wait_ge(S_done, count - 1)
                                ins = dve.scalar_tensor_tensor(out=S[:, i, d, to, :], in0=S[:, i, d, n, :],
                                                               scalar=decay[:, d, i, n:n + 1], in1=src,
                                                               op0=ALU.mult, op1=ALU.add)
                            ins.then_inc(S_done, 1)
                            count += 1
                elif what == "gla_A":
                    for d in range(2):
                        dve.wait_ge(A_done, 2 * i + d + 1)
                        if i == 0:
                            dve.wait_ge(Am_set, 1)
                        if i >= 2:
                            dve.wait_ge(og_done, i - 1)
                        mask = masks[:, d:d + 1, :].bitcast(I32).to_broadcast([P, NBLK, P])
                        dve.copy_predicated(Am[:, i % 2, d, :].rearrange("p (m c) -> p m c", c=P), mask,
                                            acc[:, 2 + d, :].rearrange("p (m c) -> p m c", c=P)).then_inc(Am_done, 1)
                elif what == "gla_sum" and i >= 1:
                    gla_normed(i - 1)
                elif what == "attention_halves":
                    lower_halves(o1, (4, 5), 1, 0)
                    split(11)
                    lower_halves(o1, (6, 7), 1, 2)
                elif what == "pooled":
                    dve.wait_ge(wsum_done, i + 1)
                    dve.scalar_tensor_tensor(out=pooled[:, i, :], in0=wsum[:, i % 2, UPAD:], scalar=1.0 / POOLW[i],
                                             in1=uu[:, i, UPAD:], op0=ALU.mult, op1=ALU.subtract)\
                       .then_inc(pooled_done, 1)
                elif what == "attention_gate":
                    for h in range(4):
                        dve.wait_ge(silu2_done, h + 1)
                        if h == 0:
                            dve.wait_ge(o_done, 8)
                        dve.tensor_tensor(o2[:, h, :], o2[:, h, :], ga2[:, h, :], ALU.mult).then_inc(ob_done, 1)
                elif what == "pool_out":
                    lower_halves(o2, (0, 1), 4, 0)
                    split(56)
                    lower_halves(o2, (2, 3), 4, 2)
                    for g in range(4):
                        dve.wait_ge(silu2_done, 5 + g)
                        dve.wait_ge(yb_ps, g + 1)
                        src = (ps6[:, :], ps7[:, :], psT[:, 0, :], psT[:, 1, :])[g]
                        dve.scalar_tensor_tensor(out=o2[:, 4 + g, :], in0=src, scalar=vec[:, V_PSC + g:V_PSC + g + 1],
                                                 in1=gb2[:, g, :], op0=ALU.mult, op1=ALU.mult).then_inc(ob_done, 1)
                        if g >= 1:
                            lower_halves(o2, (3 + g,), 4, 3 + g)
                    lower_halves(o2, (7,), 4, 7)

            def gla_normed(h):
                dve.wait_ge(rr_done, h + 1)
                dve.tensor_tensor(o1[:, h, :], o1[:, h, :], (bb, eb)[h % 2][:, :], ALU.mult).then_inc(on_done, 1)

            def out_tiles(c, n):
                for k in range(KT):
                    if k in (0, 2, 4) and c + 2 + k // 2 < C_END:
                        split(c + 2 + k // 2)
                    dve.wait_ge(tile_done[k % 2], c + k // 2 + 1)
                    if k == KT - 1:
                        dve.wait_ge(sq_done, 8 * (n + 1))
                    dve.tensor_copy(y[:, k, :], acc[:, k % 4, :]).then_inc(evac_done, 1)

            split(0)
            for m in range(2 * NBLK):
                b, g = m // 2, m % 2
                dve.wait_ge(xT_done, m + 1)
                dve.tensor_copy(resid[:, 4 * g:4 * g + 4, b * P:(b + 1) * P],
                                acc[:, m % 4, :].rearrange("p (k n) -> p k n", k=4)).then_inc(resid_done, 1)
            dve.wait_ge(vec_done, 1)
            dve.wait_ge(resid_done, KT)
            for k in range(KT - 1):
                lo_of_scaled(0, k, V_PRE1)
            lo_of_scaled(0, KT - 1, V_PRE1)
            for step in STEPS_OF[0]:
                mixer_step_dve(0, step)
            gla_normed(2)
            gla_normed(3)
            for h in range(4):
                dve.wait_ge(silu_done, h + 1)
                if h == 0:
                    dve.wait_ge(on_done, 4)
                dve.scalar_tensor_tensor(out=o1[:, h, :], in0=o1[:, h, :], scalar=vec[:, V_GN:V_GN + 1],
                                         in1=ga[:, h, :], op0=ALU.mult, op1=ALU.mult).then_inc(og_gated, 1)
                if h >= 1:
                    lower_halves(o1, (h - 1,), 1, 4 + h - 1)
            lower_halves(o1, (3,), 1, 7)
            out_tiles(C_WOUT, 1)
            boundary(1, V_POST1, V_PREM, ty)
            dve.wait_ge(r_done, 3)

            def up_tile(j, bank, c, ring_free):
                dve.wait_ge(tile_done[j], c + 1)
                if ring_free is not None:
                    dve.wait_ge(zq_done, ring_free)
                dve.scalar_tensor_tensor(out=zt[:, j, :], in0=acc[:, bank, :], scalar=0.0, in1=R[:, :],
                                         op0=ALU.max, op1=ALU.mult).then_inc(evac_done, 1)

            for half in range(2):
                cu, cd = (C_UP0, C_DN0) if half == 0 else (C_UP1, C_DN1)
                eu, ed = (E_UP0, E_DN0) if half == 0 else (E_UP1, E_DN1)
                first = 1 if half == 0 else 0
                if half == 0:
                    split(cu + 2)
                    for m in range(4):
                        up_tile(m % 2, m, cu + m // 2, m - 1 if m >= 2 else None)
                        dve.wait_ge(hhi_done, m + 1)
                        dve.tensor_tensor(hid_lo[:, m, :], zq[:, m % 2, :], hid_hi[:, m, :].bitcast(F32), ALU.subtract)\
                           .then_inc(hlo_done, 1)
                with dve.Fori(0, 4 - first) as i:
                    for s in range(2):
                        c_par = cu + s + 1
                        split(i * 2 + (cu + 2 * first + s + 1))
                        for j in range(2):
                            m = i * 4 + (HID * half + 4 * first + 2 * s + j)
                            mh = i * 4 + (4 * first + 2 * s + j)
                            up_tile(j, 2 * s + j, i * 2 + (cu + 2 * first + s), m - 1)
                            dve.wait_ge(hhi_done, m + 1)
                            dve.tensor_tensor(hid_lo[:, bass.ds(mh, 1), :], zq[:, j:j + 1, :],
                                              hid_hi[:, bass.ds(mh, 1), :].bitcast(F32), ALU.subtract)\
                               .then_inc(hlo_done, 1)
                with dve.Fori(0, 2) as i:
                    for pair in range(2):
                        for kg in range(2):
                            c_par = cd + kg + 1
                            split(i * 4 + (cd + 2 * pair + kg + 1))
                        for j in range(2):
                            t = i * 4 + (2 * pair + j)
                            dve.wait_ge(tile_done[j], i * 4 + (cd + 2 * pair + 2))
                            yt = y[:, bass.ds(t, 1), :]
                            bank = acc[:, 2 * pair + j:2 * pair + j + 1, :]
                            if half == 0:
                                dve.tensor_scalar(yt, bank, 1.0, None, ALU.mult).then_inc(evac_done, 1)
                            else:
                                dve.tensor_tensor(yt, bank, yt, ALU.add).then_inc(evac_done, 1)
            boundary(2, V_POSTM, V_PRE2A, ty_e)
            for step in STEPS_OF[1]:
                mixer_step_dve(1, step)
            out_tiles(C_ABOUT, 5)
            boundary(3, V_POST2A, V_PRE2B, ty_c)
            dve.wait_ge(r_done, 7)
            dve.wait_ge(taps_done, 1)
            dve.memset(vacc[:, 0, 0:1], 0.0).then_inc(conv_step, 1)
            dve.memset(vacc[:, 1, 0:1], 0.0).then_inc(prod_done, 1)
            with dve.Fori(0, 2) as i:
                def chunk_out(s):
                    c = C_CAB + s
                    for j in range(2):
                        dve.wait_ge(tile_done[j], i * TURN_CHUNKS + (c + 1))
                        bank = acc[:, (2 * s + j) % 4:(2 * s + j) % 4 + 1, :]
                        R3 = R[:, :].rearrange("p (a n) -> p a n", a=1)
                        if s in TURN_AB:
                            if j == 0:
                                dve.wait_ge(glu_done, i * TURN_TILES + (TURN_AB[s] + 1))
                            dst = ab[:, j:j + 1, :]
                        else:
                            dst = gate[:, bass.ds(i * 4 + (2 * GATE_AT.index(s) + j), 1), :]
                        dve.tensor_tensor(dst, bank, R3, ALU.mult).then_inc(evac_done, 1)

                dve.wait_ge(prod_done, i * (TURN_TILES * ACT_TAPS) + 1)
                dve.tensor_copy(tapw[:, :, 0:TAPS], taps[:, bass.ds(i * TURN_TILES, TURN_TILES), :])\
                   .then_inc(tapw_done, 1)
                dve.tensor_copy(tapw[:, :, TAPS], vec[:, bass.ds(i * TURN_TILES + V_DWB, TURN_TILES)])\
                   .then_inc(tapw_done, 1)
                for t in range(TURN_TILES):
                    vsteps = DVE_TAPS + 1
                    for m in range(DVE_TAPS):
                        for x, s in TURN_WORK[t]:
                            if m == x:
                                chunk_out(s)
                            if m == (x + 5 if x else 0):
                                c_par = C_CAB + s + 2
                                split(i * TURN_CHUNKS + (C_CAB + s + 2))
                        if m == 0:
                            dve.wait_ge(tapw_done, i * 2 + 2)
                            dve.wait_ge(glu_done, i * TURN_TILES + (t + 2))
                            dve.wait_ge(conv_step, i * TURN_TILES + (t + 1))
                        src, sums = glu[:, t % 2, m:m + TOK], vacc[:, m % 2, :]
                        if m >= 2:
                            dve.wait_ge(vacc_step, i * (TURN_TILES * vsteps) + (vsteps * t + m - 1))
                        if m == 0:
                            ins = dve.tensor_scalar(sums, src, tapw[:, t, 0:1], tapw[:, t, TAPS:TAPS + 1],
                                                    ALU.mult, ALU.add)
                        elif m == 1:
                            ins = dve.tensor_scalar(sums, src, tapw[:, t, 1:2], None, ALU.mult)
                        else:
                            ins = dve.scalar_tensor_tensor(out=sums, in0=src, scalar=tapw[:, t, m:m + 1], in1=sums,
                                                           op0=ALU.mult, op1=ALU.add)
                        ins.then_inc(vacc_step, 1)
                    dve.wait_ge(vacc_step, i * (TURN_TILES * vsteps) + (vsteps * t + DVE_TAPS))
                    dve.tensor_tensor(vacc[:, 0, :], vacc[:, 0, :], vacc[:, 1, :], ALU.add).then_inc(vacc_step, 1)
                    dve.wait_ge(vacc_step, i * (TURN_TILES * vsteps) + vsteps * (t + 1))
                    dve.wait_ge(pacc_step, i * (TURN_TILES * ADDS) + ADDS * (t + 2))
                    dve.tensor_tensor(conv[:, bass.ds(i * TURN_TILES + t, 1), :], vacc[:, 0:1, :],
                                      pacc[:, :].rearrange("p (a n) -> p a n", a=1), ALU.add).then_inc(conv_step, 1)
            dve.wait_ge(mu_done, 1)
            dve.wait_ge(conv_step, KT + 1)
            for k in range(KT):
                dve.tensor_tensor(conv[:, k, :], conv[:, k, :], mu[:, :], ALU.subtract).then_inc(cen_done, 1)
            dve.wait_ge(r_done, 8)
            dve.wait_ge(cen_done, KT)
            for k in range(KT + 2):
                if k < KT:
                    dve.tensor_tensor(conv[:, k, :], conv[:, k, :], R[:, :], ALU.mult).then_inc(cn_done, 1)
                if 1 <= k <= KT:
                    m = k - 1
                    dve.wait_ge(csilu_done, m + 1)
                    if m == 0:
                        dve.wait_ge(gsilu_done, 1)
                    if m >= 2:
                        dve.wait_ge(act_lo_done, 8 * 6 + m - 1)
                    dve.tensor_tensor(yc[:, m % 2, :], conv[:, m, :], gate[:, m, :], ALU.mult).then_inc(yc_done, 1)
                if k >= 2:
                    m = k - 2
                    dve.wait_ge(act_hi_done, 8 * 6 + m + 1)
                    dve.tensor_tensor(act_lo[:, m, :], yc[:, m % 2, :], act_hi[:, m, :].bitcast(F32), ALU.subtract)\
                       .then_inc(act_lo_done, 1)
            out_tiles(C_COUT, 8)
            dve.wait_ge(r_done, 9)
            boundary(4, V_POST2B, None, ty_c)
            for f in range(1, 2 * NBLK, 2):
                dve.wait_ge(fT_done, f + 1)
                dve.tensor_copy(o_tok[:, f, :], acc[:, f % 4, :]).then_inc(fo_done[1], 1)


_INS = ["x", "norm_mix_pre", "w_in", "w_gate_up_fwd", "b_gate_fwd", "w_gate_up_bwd", "b_gate_bwd", "gla_norm",
        "swa_sink", "rel_bias", "w_out", "norm_mix_post", "norm_mlp_pre", "w_up", "w_down", "norm_mlp_post",
        "pre_norm_2", "post_norm_2", "a_w_in_2", "a_sinks_2", "b_pool_w_2", "b_pool_scale_2", "ab_w_out_2",
        "c_w_in_2", "c_dw_w_2", "c_dw_b_2", "c_ln_g_2", "c_ln_b_2", "c_w_out_2"]


def kernel(**inputs):
    import numpy as _np
    import concourse.bacc as _bacc
    from concourse import mybir as _mybir
    from concourse.bass_utils import run_bass_kernel_spmd as _run

    nc = _bacc.Bacc("TRN2", target_bir_lowering=False, num_devices=1)
    given = {name: _np.ascontiguousarray(inputs[name]) for name in _INS}
    given.update(shapes=shape_constants(), onehot=t5_bucket_onehot(), alibi=alibi_band(),
                 vectors=vector_rows(given))
    arrays, args = {}, {}
    for name, v in given.items():
        arrays[f"in_{name}_dram"] = v
        args[name] = nc.dram_tensor(f"in_{name}_dram", v.shape, _mybir.dt.from_np(v.dtype), kind="ExternalInput").ap()
    out = nc.dram_tensor("out_0_dram", (1, TOK, D), F32, kind="ExternalOutput").ap()
    block_kernel(nc, args, out)
    r = _run(nc, [arrays], core_ids=[0])
    return r.results[0]["out_0_dram"]
```
